# Optimizing a Trainium2 kernel written in Bass

```python
import math
import jax, jax.numpy as jnp
from jax import lax
import numpy as np

D_MODEL = 1024
BATCH = 1
SEQ = 1024
DEPTH = 1
DEC_BATCH = 1
DEC_SEQ = 32
PAST_LEN = 2048

CHUNK = 64
Q_BLOCK = 128
HEAD_DIM = 64
SSM_HEADS = 8
SSM_WIDTH = SSM_HEADS * HEAD_DIM
SSM_GROUPS = 2
D_STATE = 128
D_CONV = 4
CONV_DIM = SSM_WIDTH + 2 * SSM_GROUPS * D_STATE
SB_HEADS = 8
SB_WIDTH = SB_HEADS * HEAD_DIM
MIX_WIDTH = SSM_WIDTH + SB_WIDTH
SB_SCALE = HEAD_DIM ** -0.5
OFF_XBC = SSM_WIDTH
OFF_DT = OFF_XBC + CONV_DIM
OFF_Q = OFF_DT + SSM_HEADS
OFF_K = OFF_Q + SB_WIDTH
OFF_V = OFF_K + SB_WIDTH
IN_COLS = OFF_V + SB_WIDTH
PEER_HEADS = 8
N_KEYS = 128
N_EXPERTS = N_KEYS * N_KEYS
D_KEY = 256
HALF_KEY = D_KEY // 2
PEER_TOPK = 16
PEER_ROW = 128
EPS = 1e-6

kernel_name = 'hybrid_ssd_stickbreaking_peer'

def rmsnorm(x, w):
    xf = x.astype(jnp.float32)
    y = xf * lax.rsqrt(jnp.mean(xf * xf, axis=-1, keepdims=True) + EPS)
    return (y * w.astype(jnp.float32)).astype(x.dtype)

def causal_conv(xbc, conv_state, conv_w, conv_b):
    L = xbc.shape[1]
    full = jnp.concatenate([conv_state.astype(xbc.dtype), xbc], axis=1)
    out = conv_b
    for j in range(D_CONV):
        out = out + full[:, j:j + L, :] * conv_w[j]
    new_state = full[:, full.shape[1] - (D_CONV - 1):, :]
    return jax.nn.silu(out), new_state

def ssd_scan(x, dt, a, bm, cm, init_state, chunk):
    f32 = jnp.float32
    b, L, h, p = x.shape
    nc = L // chunk
    rep = h // bm.shape[2]
    bh = jnp.repeat(bm.astype(f32), rep, axis=2).reshape(b, nc, chunk, h, D_STATE)
    ch = jnp.repeat(cm.astype(f32), rep, axis=2).reshape(b, nc, chunk, h, D_STATE)
    xdt = (x.astype(f32) * dt[..., None]).reshape(b, nc, chunk, h, p)
    a_cum = jnp.cumsum((dt * a).reshape(b, nc, chunk, h), axis=2)
    causal = jnp.tril(jnp.ones((chunk, chunk), dtype=bool))[None, None, :, :, None]
    seg = a_cum[:, :, :, None, :] - a_cum[:, :, None, :, :]
    decay = jnp.where(causal, jnp.exp(jnp.where(causal, seg, 0.0)), 0.0)
    scores = jnp.einsum('bclhn,bcshn->bclsh', ch, bh) * decay
    y_diag = jnp.einsum('bclsh,bcshp->bclhp', scores, xdt)
    to_end = jnp.exp(a_cum[:, :, -1:, :] - a_cum)
    chunk_states = jnp.einsum('bclhn,bclh,bclhp->bchpn', bh, to_end, xdt)
    chunk_decay = jnp.exp(a_cum[:, :, -1, :])

    def carry_step(state, inp):
        st, dec = inp
        return dec[:, :, None, None] * state + st, state

    final, prev = lax.scan(carry_step, init_state.astype(f32),
                           (jnp.moveaxis(chunk_states, 1, 0), jnp.moveaxis(chunk_decay, 1, 0)))
    prev = jnp.moveaxis(prev, 0, 1)
    y_off = jnp.einsum('bclhn,bchpn,bclh->bclhp', ch, prev, jnp.exp(a_cum))
    return (y_diag + y_off).reshape(b, L, h, p), final

def ssm_group(z, xbc, dt_raw, conv_state, ssm_state, chunk, conv_w, conv_b, dt_bias, a_log, d_skip, ssm_norm_w):
    f32 = jnp.float32
    b, L, _ = z.shape
    xbc_a, new_conv = causal_conv(xbc, conv_state, conv_w, conv_b)
    xs = xbc_a[..., :SSM_WIDTH].reshape(b, L, SSM_HEADS, HEAD_DIM)
    bm = xbc_a[..., SSM_WIDTH:SSM_WIDTH + SSM_GROUPS * D_STATE].reshape(b, L, SSM_GROUPS, D_STATE)
    cm = xbc_a[..., SSM_WIDTH + SSM_GROUPS * D_STATE:].reshape(b, L, SSM_GROUPS, D_STATE)
    dt = jax.nn.softplus(dt_raw.astype(f32) + dt_bias.astype(f32))
    a = -jnp.exp(a_log.astype(f32))
    y, new_ssm = ssd_scan(xs, dt, a, bm, cm, ssm_state, chunk)
    y = y + d_skip.astype(f32)[:, None] * xs.astype(f32)
    y = y.reshape(b, L, SSM_WIDTH) * jax.nn.silu(z.astype(f32))
    yg = y.reshape(b, L, SSM_GROUPS, SSM_WIDTH // SSM_GROUPS)
    yg = yg * lax.rsqrt(jnp.mean(yg * yg, axis=-1, keepdims=True) + EPS)
    y = yg.reshape(b, L, SSM_WIDTH) * ssm_norm_w.astype(f32)
    return y.astype(z.dtype), new_conv, new_ssm.astype(ssm_state.dtype)

def stick_breaking(q, k, v, q_pos, k_pos):
    f32 = jnp.float32
    z = jnp.einsum('bqhd,bkhd->bhqk', q.astype(f32), k.astype(f32)) * SB_SCALE
    mask = k_pos[None, :] < q_pos[:, None]
    log_1m = jnp.where(mask, jax.nn.log_sigmoid(-z), 0.0)
    after = lax.cumsum(log_1m, axis=3, reverse=True) - log_1m
    w = jnp.where(mask, jnp.exp(jax.nn.log_sigmoid(z) + after), 0.0)
    return jnp.einsum('bhqk,bkhd->bqhd', w, v.astype(f32)).astype(v.dtype)

def sb_prompt(q, k, v):
    L = q.shape[1]
    pos = jnp.arange(L)
    outs = []
    for i in range(L // Q_BLOCK):
        lo, hi = i * Q_BLOCK, (i + 1) * Q_BLOCK
        outs.append(stick_breaking(q[:, lo:hi], k[:, :hi], v[:, :hi], pos[lo:hi], pos[:hi]))
    return jnp.concatenate(outs, axis=1)

def sb_cached(q, k, v, k_past, v_past):
    past = k_past.shape[1]
    L = q.shape[1]
    k_all = jnp.concatenate([k_past.astype(k.dtype), k], axis=1)
    v_all = jnp.concatenate([v_past.astype(v.dtype), v], axis=1)
    k_pos = jnp.arange(past + L)
    q_pos = past + jnp.arange(L)
    return stick_breaking(q, k_all, v_all, q_pos, k_pos)

def peer_rows(xr, wq, k1, k2, u_tab, v_tab):
    f32 = jnp.float32
    L = xr.shape[0]
    q = (xr @ wq).astype(f32).reshape(L, PEER_HEADS, D_KEY)
    s1 = jnp.einsum('lhk,hnk->lhn', q[..., :HALF_KEY], k1.astype(f32))
    s2 = jnp.einsum('lhk,hnk->lhn', q[..., HALF_KEY:], k2.astype(f32))
    v1, i1 = lax.top_k(s1, PEER_TOPK)
    v2, i2 = lax.top_k(s2, PEER_TOPK)
    cand = (v1[..., :, None] + v2[..., None, :]).reshape(L, PEER_HEADS, PEER_TOPK * PEER_TOPK)
    best, flat = lax.top_k(cand, PEER_TOPK)
    row = jnp.take_along_axis(i1, flat // PEER_TOPK, axis=-1)
    col = jnp.take_along_axis(i2, flat % PEER_TOPK, axis=-1)
    expert = row * N_KEYS + col
    gate = jax.nn.softmax(best, axis=-1)
    u_sel = jnp.take(u_tab, expert, axis=0)
    act = jax.nn.gelu(jnp.einsum('lhkd,ld->lhk', u_sel, xr).astype(f32), approximate=False)
    coef = (gate * act).astype(xr.dtype)
    return jnp.einsum('lhk,lhkd->ld', coef, jnp.take(v_tab, expert, axis=0))

def peer(x, row_len, wq, k1, k2, u_tab, v_tab):
    rows = x.reshape(-1, row_len, D_MODEL)
    out = lax.map(lambda xr: peer_rows(xr, wq, k1, k2, u_tab, v_tab), rows)
    return out.reshape(x.shape)

def layer(x, conv_state, ssm_state, k_past, v_past, chunk, row_len,
          norm1_w, w_in, conv_w, conv_b, dt_bias, a_log, d_skip, ssm_norm_w, w_out,
          norm2_w, peer_wq, peer_k1, peer_k2, peer_u, peer_v):
    b, L, _ = x.shape
    xn = rmsnorm(x, norm1_w)
    proj = xn @ w_in
    z = proj[..., :OFF_XBC]
    xbc = proj[..., OFF_XBC:OFF_DT]
    dt_raw = proj[..., OFF_DT:OFF_Q]
    q = proj[..., OFF_Q:OFF_K].reshape(b, L, SB_HEADS, HEAD_DIM)
    k = proj[..., OFF_K:OFF_V].reshape(b, L, SB_HEADS, HEAD_DIM)
    v = proj[..., OFF_V:].reshape(b, L, SB_HEADS, HEAD_DIM)
    y_ssm, new_conv, new_ssm = ssm_group(z, xbc, dt_raw, conv_state, ssm_state, chunk,
                                         conv_w, conv_b, dt_bias, a_log, d_skip, ssm_norm_w)
    if k_past is None:
        o_sb = sb_prompt(q, k, v)
    else:
        o_sb = sb_cached(q, k, v, k_past, v_past)
    mixed = jnp.concatenate([y_ssm, o_sb.reshape(b, L, SB_WIDTH).astype(y_ssm.dtype)], axis=-1)
    h = x + mixed @ w_out
    h = h + peer(rmsnorm(h, norm2_w), row_len, peer_wq, peer_k1, peer_k2, peer_u, peer_v)
    return h, k, v, new_ssm, new_conv

def setup_inputs(seed: int = 0) -> dict:
    key = jax.random.key(seed)
    ks = jax.random.split(key, 24)
    f32 = jnp.float32
    nrm = lambda k, shape, s: jax.random.normal(k, shape, f32) * s
    dt = jnp.exp(jax.random.uniform(ks[10], (DEPTH, SSM_HEADS), f32) * (math.log(0.1) - math.log(1e-3)) + math.log(1e-3))
    return {
        'x_prompt': nrm(ks[0], (BATCH, SEQ, D_MODEL), 1.0),
        'x_sample': nrm(ks[1], (DEC_BATCH, DEC_SEQ, D_MODEL), 1.0),
        'cache_sb_k': nrm(ks[2], (DEPTH, DEC_BATCH, PAST_LEN, SB_HEADS, HEAD_DIM), 1.0),
        'cache_sb_v': nrm(ks[3], (DEPTH, DEC_BATCH, PAST_LEN, SB_HEADS, HEAD_DIM), 1.0),
        'state_ssm': nrm(ks[4], (DEPTH, DEC_BATCH, SSM_HEADS, HEAD_DIM, D_STATE), 0.1),
        'state_conv': nrm(ks[5], (DEPTH, DEC_BATCH, D_CONV - 1, CONV_DIM), 1.0),
        'norm1_w': 1.0 + nrm(ks[6], (DEPTH, D_MODEL), 0.01),
        'w_in': nrm(ks[7], (DEPTH, D_MODEL, IN_COLS), D_MODEL ** -0.5),
        'conv_w': nrm(ks[8], (DEPTH, D_CONV, CONV_DIM), D_CONV ** -0.5),
        'conv_b': nrm(ks[9], (DEPTH, CONV_DIM), 0.01),
        'dt_bias': dt + jnp.log(-jnp.expm1(-dt)),
        'a_log': jnp.log(jax.random.uniform(ks[11], (DEPTH, SSM_HEADS), f32, 1.0, 16.0)),
        'd_skip': 1.0 + nrm(ks[12], (DEPTH, SSM_HEADS), 0.1),
        'ssm_norm_w': 1.0 + nrm(ks[13], (DEPTH, SSM_WIDTH), 0.01),
        'w_out': nrm(ks[14], (DEPTH, MIX_WIDTH, D_MODEL), MIX_WIDTH ** -0.5),
        'norm2_w': 1.0 + nrm(ks[15], (DEPTH, D_MODEL), 0.01),
        'peer_wq': nrm(ks[16], (DEPTH, D_MODEL, PEER_HEADS * D_KEY), D_MODEL ** -0.5),
        'peer_k1': nrm(ks[17], (DEPTH, PEER_HEADS, N_KEYS, HALF_KEY), HALF_KEY ** -0.5),
        'peer_k2': nrm(ks[18], (DEPTH, PEER_HEADS, N_KEYS, HALF_KEY), HALF_KEY ** -0.5),
        'peer_u': nrm(ks[19], (DEPTH, N_EXPERTS, D_MODEL), D_MODEL ** -0.5),
        'peer_v': nrm(ks[20], (DEPTH, N_EXPERTS, D_MODEL), PEER_HEADS ** -0.5),
        'final_norm_w': 1.0 + nrm(ks[21], (D_MODEL,), 0.01),
    }

def reference(x_prompt, x_sample, cache_sb_k, cache_sb_v, state_ssm, state_conv,
              norm1_w, w_in, conv_w, conv_b, dt_bias, a_log, d_skip, ssm_norm_w, w_out,
              norm2_w, peer_wq, peer_k1, peer_k2, peer_u, peer_v, final_norm_w):
    hp, hs = x_prompt, x_sample
    bp, bs, ls = x_prompt.shape[0], x_sample.shape[0], x_sample.shape[1]
    kp_l, vp_l, sp_l, cp_l, ks_l, vs_l, ss_l, cs_l = [], [], [], [], [], [], [], []
    for l in range(DEPTH):
        w = (norm1_w[l], w_in[l], conv_w[l], conv_b[l], dt_bias[l], a_log[l], d_skip[l],
             ssm_norm_w[l], w_out[l], norm2_w[l], peer_wq[l], peer_k1[l], peer_k2[l], peer_u[l], peer_v[l])
        conv0 = jnp.zeros((bp, D_CONV - 1, CONV_DIM), hp.dtype)
        ssm0 = jnp.zeros((bp, SSM_HEADS, HEAD_DIM, D_STATE), jnp.float32)
        hp, kp, vp, sp, cp = layer(hp, conv0, ssm0, None, None, CHUNK, PEER_ROW, *w)
        hs, ks_, vs_, ss, cs = layer(hs, state_conv[l], state_ssm[l], cache_sb_k[l], cache_sb_v[l], ls, ls, *w)
        kp_l.append(kp); vp_l.append(vp); sp_l.append(sp); cp_l.append(cp)
        ks_l.append(ks_); vs_l.append(vs_); ss_l.append(ss); cs_l.append(cs)
    y_prompt = rmsnorm(hp, final_norm_w)
    y_sample = rmsnorm(hs, final_norm_w)
    return (y_prompt, y_sample,
            jnp.stack(kp_l), jnp.stack(vp_l), jnp.stack(sp_l), jnp.stack(cp_l),
            jnp.stack(ks_l), jnp.stack(vs_l), jnp.stack(ss_l), jnp.stack(cs_l))


_drawn_inputs = setup_inputs


def setup_inputs(seed=0):
    import zlib

    import numpy as np

    out = dict(_drawn_inputs(seed))
    spreads = {}
    factors = {'norm1_w': 3.279,
     'conv_b': 11.713,
     'ssm_norm_w': 22.139,
     'norm2_w': 17.788,
     'final_norm_w': 30.095,
     'd_skip': 8.0}
    for name, (base, spread) in spreads.items():
        noise = np.random.default_rng([zlib.crc32(name.encode()), seed]).standard_normal(out[name].shape)
        drawn = base * np.exp(spread * noise) if base else spread * noise
        out[name] = __import__('jax').numpy.asarray(drawn.astype(out[name].dtype))
    for name, factor in factors.items():
        out[name] = (out[name] * factor).astype(out[name].dtype)
    return out
```

```python
from contextlib import ExitStack, contextmanager

import numpy as np

import concourse.bass as bass
from concourse import mybir

F32 = mybir.dt.float32
F32R = mybir.dt.float32r
BF16 = mybir.dt.bfloat16
U32 = mybir.dt.uint32
ACT = mybir.ActivationFunctionType
ALU = mybir.AluOpType
AX = mybir.AxisListType

P = 128
D = 1024
DC = D // P
PROMPT = 1024
SAMPLE = 32
TOK = PROMPT + SAMPLE
NB = 352
NBN = TOK // NB
EPS = 1e-6

SSM_HEADS = 8
HD = 64
STATE = 128
TAPS = 4
CONV_TILES = 8
Z_TILE, Q_TILE, K_TILE, V_TILE, IN_TILES = 8, 12, 16, 20, 24
CHUNKS = PROMPT // P
S_OFF = PROMPT + TAPS - 1
CONV_W = TOK + 2 * (TAPS - 1)
CONV_OUT = CONV_W - (TAPS - 1)

PAIRS = 4
PAST = 2048
PB = PAST // P
QW = 512

PEER_HEADS = 8
HALVES = 2 * PEER_HEADS
KEYS = 128
TOPK = 16
TILES = 9
LOWEST = -3.0e38
MASKED = -1.0e30
GT = 96
GTILES = TOK // GT
GG = 4

KE = 2
BLOCKS = KEYS // KE


def credit(engine, sem, n):
    engine.sem_inc(sem, n)


def tokens_of(tile):
    return P if tile < TILES - 1 else SAMPLE


class Sems:

    def __init__(self, nc, ctx, phase):
        self.nc, self.ctx, self.phase = nc, ctx, phase

    def __call__(self, name):
        return self.ctx.enter_context(self.nc.semaphore(f"{self.phase}_{name}"))


@contextmanager
def phase(nc, name):
    with ExitStack() as ctx:
        def sb(n, shape, dt=F32):
            return ctx.enter_context(nc.sbuf_tensor(f"{name}_{n}", shape, dt))

        def ps(n, shape, dt=F32):
            return ctx.enter_context(nc.psum_tensor(f"{name}_{n}", shape, dt))

        block = nc.Block()
        yield sb, ps, Sems(nc, ctx, name), block


def project(nc, out, w_hi, w_lo, x_hi, x_lo, n):
    tok = slice(n * NB, (n + 1) * NB)
    for k in range(DC):
        nc.tensor.matmul(out, w_hi[:, k, :], x_hi[:, k, tok], start=(k == 0), stop=False)
        nc.tensor.matmul(out, w_hi[:, k, :], x_lo[:, k, tok], start=False, stop=False)
        last = nc.tensor.matmul(out, w_lo[:, k, :], x_hi[:, k, tok], start=False, stop=(k == DC - 1))
    return last


def norm_phase(nc, name, src, weight, consts, hi=None, lo=None, src_dram=None, out=None, out_dram=None):
    with phase(nc, name) as (sb, ps, sem, blk):
        squares = sb("squares", [P, 2, TOK])
        rstd = sb("rstd", [P, TOK])
        scaled = sb("scaled", [P, 2, TOK])
        total = ps("total", [P, NBN, 512])
        landed, squared, summed = sem("landed"), sem("squared"), sem("summed")
        mean_ready, root_ready, rstd_ready = sem("mean"), sem("root"), sem("rstd")
        scaled_ready, hi_ready, lo_ready, stored = sem("scaled"), sem("hi"), sem("lo"), sem("stored")
        split = hi is not None
        with blk as block:
            @block.sync
            def _(sp):
                if src_dram is not None:
                    sp.dma_start(src[:], src_dram).then_inc(landed, 16)
                if not split:
                    sp.wait_ge(scaled_ready, DC)
                    sp.dma_start(out_dram, out[:]).then_inc(stored, 16)
                    sp.wait_ge(stored, 16)

            @block.scalar
            def _(act):
                if src_dram is not None:
                    act.wait_ge(landed, 16)
                for k in range(DC):
                    if k >= 2:
                        act.wait_ge(summed, k - 1)
                    nc.scalar.activation(squares[:, k % 2, :], src[:, k, :], ACT.Square).then_inc(squared, 1)
                act.wait_ge(mean_ready, 1)
                nc.scalar.activation(rstd[:], rstd[:], ACT.Sqrt).then_inc(root_ready, 1)
                if split:
                    for k in range(DC):
                        act.wait_ge(scaled_ready, k + 1)
                        nc.scalar.activation(hi[:, k, :], scaled[:, k % 2, :], ACT.Copy).then_inc(hi_ready, 1)

            @block.tensor
            def _(pe):
                for k in range(DC):
                    pe.wait_ge(squared, k + 1)
                    for n in range(NBN):
                        last = nc.tensor.matmul(total[:, n, :NB], consts["ones"][:], squares[:, k % 2, n * NB:(n + 1) * NB],
                                                start=(k == 0), stop=(k == DC - 1))
                    last.then_inc(summed, 1)

            @block.vector
            def _(dve):
                dve.wait_ge(summed, DC)
                nc.vector.tensor_scalar(rstd[:].rearrange("p (n t) -> p n t", n=NBN), total[:, :, :NB],
                                        1.0 / D, EPS, ALU.mult, ALU.add).then_inc(mean_ready, 1)
                dve.wait_ge(root_ready, 1)
                nc.vector.reciprocal(rstd[:], rstd[:]).then_inc(rstd_ready, 1)
                dve.wait_ge(rstd_ready, 1)

                def split_low(k):
                    dve.wait_ge(hi_ready, k + 1)
                    nc.vector.tensor_tensor(lo[:, k, :], scaled[:, k % 2, :], hi[:, k, :].bitcast(F32),
                                            ALU.subtract).then_inc(lo_ready, 1)

                for k in range(DC):
                    if split and k >= 2:
                        split_low(k - 2)
                        dve.wait_ge(lo_ready, k - 1)
                    to = scaled[:, k % 2, :] if split else out[:, k, :]
                    nc.vector.scalar_tensor_tensor(to, src[:, k, :], weight[:, k:k + 1], rstd[:],
                                                   ALU.mult, ALU.mult).then_inc(scaled_ready, 1)
                if split:
                    split_low(DC - 2)
                    split_low(DC - 1)


def input_projection(nc, consts, x_hi, x_lo, dt_raw, w_in, w_dt, proj):
    with phase(nc, "inproj") as (sb, ps, sem, blk):
        w_raw = sb("w_raw", [P, 2, DC, P])
        w_hi = sb("w_hi", [P, 2, DC, P], F32R)
        w_lo = sb("w_lo", [P, 2, DC, P], F32R)
        wdt_raw = sb("wdt_raw", [P, DC, SSM_HEADS])
        wdt_hi = sb("wdt_hi", [P, DC, SSM_HEADS], F32R)
        wdt_lo = sb("wdt_lo", [P, DC, SSM_HEADS], F32R)
        result = sb("result", [P, 2, TOK])
        acc = ps("acc", [P, 2, 3, 512])
        dt_acc = ps("dt_acc", [P, TILES, SSM_HEADS])
        w_landed = [sem("w_landed0"), sem("w_landed1")]
        hi_ready, lo_ready = sem("hi_ready"), sem("lo_ready")
        projected, acc_free = sem("projected"), sem("acc_free")
        stored = [sem("stored0"), sem("stored1")]
        dt_landed, dt_split, dt_done = sem("dt_landed"), sem("dt_split"), sem("dt_done")
        pairs = IN_TILES // 2
        with blk as block:
            @block.sync
            def _(sp):
                sp.dma_start(wdt_raw[:], w_dt).then_inc(dt_landed, 16)
                credit(sp, lo_ready, 2)
                with sp.Fori(0, pairs) as i:
                    for u in range(2):
                        sp.wait_ge(lo_ready, 2 * i + u + 1)
                        sp.dma_start(w_raw[:, u], w_in[bass.ds(2 * i + u, 1)]
                                     .rearrange("a p k m -> p (a k) m")).then_inc(w_landed[u], 16)

            @block.scalar
            def _(act):
                act.wait_ge(dt_landed, 16)
                nc.scalar.activation(wdt_hi[:], wdt_raw[:], ACT.Copy).then_inc(dt_split, 1)
                credit(act, stored[0], 16)
                credit(act, stored[1], 16)

                def split_high(i, u):
                    act.wait_ge(w_landed[u], 16 * i + 16)
                    act.wait_ge(projected, 6 * i + 3 * u + 3)
                    nc.scalar.activation(w_hi[:, u], w_raw[:, u], ACT.Copy).then_inc(hi_ready, 1)

                def evacuate(i, u):
                    act.wait_ge(stored[u], 16 * i + 16)
                    for n in range(NBN):
                        act.wait_ge(projected, 6 * i + 3 * u + n + 7)
                        nc.scalar.activation(result[:, u, n * NB:(n + 1) * NB], acc[:, u, n, :NB],
                                             ACT.Copy).then_inc(acc_free, 1)
                    act.wait_ge(acc_free, 6 * i + 3 * u + 9)
                    act.dma_start(proj[bass.ds(2 * i + u, 1)].rearrange("a p t -> (a p) t"),
                                  result[:, u]).then_inc(stored[u], 16)

                split_high(0, 0)
                with act.Fori(0, pairs - 1) as i:
                    split_high(i, 1)
                    evacuate(i, 0)
                    split_high(i + 1, 0)
                    evacuate(i, 1)
                split_high(pairs - 1, 1)
                evacuate(pairs - 1, 0)
                evacuate(pairs - 1, 1)
                for u in range(2):
                    act.wait_ge(stored[u], 16 * pairs + 16)

            @block.vector
            def _(dve):
                dve.wait_ge(dt_split, 1)
                nc.vector.tensor_tensor(wdt_lo[:], wdt_raw[:], wdt_hi[:].bitcast(F32), ALU.subtract).then_inc(dt_split, 1)
                nc.vector.memset(dt_raw[:], 0.0).then_inc(dt_split, 1)
                with dve.Fori(0, pairs) as i:
                    for u in range(2):
                        dve.wait_ge(hi_ready, 2 * i + u + 1)
                        nc.vector.tensor_tensor(w_lo[:, u], w_raw[:, u], w_hi[:, u].bitcast(F32),
                                                ALU.subtract).then_inc(lo_ready, 1)
                dve.wait_ge(dt_done, 1)
                dve.wait_ge(dt_split, 3)
                nc.vector.tensor_copy(dt_raw[:, :TILES - 1], dt_acc[:, :TILES - 1])
                nc.vector.tensor_copy(dt_raw[:SAMPLE, TILES - 1], dt_acc[:SAMPLE, TILES - 1])

            @block.tensor
            def _(pe):
                credit(pe, acc_free, 6)
                credit(pe, projected, 6)
                with pe.Fori(0, pairs) as i:
                    for u in range(2):
                        pe.wait_ge(lo_ready, 2 * i + u + 3)
                        for n in range(NBN):
                            pe.wait_ge(acc_free, 6 * i + 3 * u + n + 1)
                            last = project(nc, acc[:, u, n, :NB], w_hi[:, u], w_lo[:, u], x_hi, x_lo, n)
                            last.then_inc(projected, 1)
                pe.wait_ge(dt_split, 3)
                for t in range(TILES):
                    tok = slice(t * P, t * P + tokens_of(t))
                    out = dt_acc[:tokens_of(t), t, :]
                    for k in range(DC):
                        nc.tensor.matmul(out, x_hi[:, k, tok], wdt_hi[:, k, :], start=(k == 0), stop=False)
                        nc.tensor.matmul(out, x_hi[:, k, tok], wdt_lo[:, k, :], start=False, stop=False)
                        last = nc.tensor.matmul(out, x_lo[:, k, tok], wdt_hi[:, k, :], start=False, stop=(k == DC - 1))
                last.then_inc(dt_done, 1)


def ssd_phase(nc, consts, vecs, head_vec, dt_raw, t, mixed):
    ssm_norm_w, d_skip, conv_wb = vecs
    XT, BT, CT = 4, 2, 2
    CW = SSM_HEADS * TILES
    with phase(nc, "ssd") as (sb, ps, sem, blk):
        window = sb("window", [P, CONV_TILES, CONV_W])
        conv = sb("conv", [P, CONV_TILES, CONV_OUT])
        gate = sb("gate", [P, XT, TOK])
        state = sb("state", [P, 2, SSM_HEADS, HD])
        stage = sb("stage", [P, XT + BT, P])
        dta_stage = sb("dta_stage", [P, SSM_HEADS])
        dt, dta, tmp, acum, to_end, decay, dt_end = (sb(n, [P, CW]) for n in (
            "dt", "dta", "tmp", "acum", "to_end", "decay", "dt_end"))
        exp_row = sb("exp_row", [P, SSM_HEADS, P])
        seg = sb("seg", [P, SSM_HEADS, P])
        c_scaled = sb("c_scaled", [P, SSM_HEADS, P])
        xdt = sb("xdt", [P, SSM_HEADS, HD])
        x_end = sb("x_end", [P, SSM_HEADS, HD])
        b_rows = sb("b_rows", [P, BT, P])
        rows_ps = ps("rows_ps", [P, XT + BT, P])
        acum_ps = ps("acum_ps", [P, SSM_HEADS, P])
        score_ps = ps("score_ps", [P, BT, 256])
        y_ps = ps("y_ps", [P, XT, P])
        state_ps = ps("state_ps", [P, SSM_HEADS, HD])
        small_ps = ps("small_ps", [P, 2, 256])
        landed, z_landed, cleared = sem("landed"), sem("z_landed"), sem("cleared")
        convolved, silu_done = sem("convolved"), sem("silu_done")
        dt_step, dt_act, dt_pe = sem("dt_step"), sem("dt_act"), sem("dt_pe")
        staged, transposed, acum_ready, scored = sem("staged"), sem("transposed"), sem("acum_ready"), sem("scored")
        exp_row_done, seg_ready, seg_exp, weighted = sem("exp_row_done"), sem("seg_ready"), sem("seg_exp"), sem("weighted")
        x_ready, c_ready, b_ready = sem("x_ready"), sem("c_ready"), sem("b_ready")
        y_done, state_done, y_out, decayed, state_new = (
            sem("y_done"), sem("state_done"), sem("y_out"), sem("decayed"), sem("state_new"))
        gated, squared, grouped, mean_ready, root_ready, rstd_ready = (
            sem("gated"), sem("squared"), sem("grouped"), sem("mean"), sem("root"), sem("rstd"))
        stored = sem("stored")

        def group_out(g, n):
            flat = [acum_ps[:, 0:4], acum_ps[:, 4:8], rows_ps[:, 0:4], y_ps[:], state_ps[:], score_ps[:]][3 * g + n]
            return flat.rearrange("p a b -> p (a b)")[:, :NB]

        def columns(c):
            return (bass.ds(c * P, P), P) if c is not None else (slice(S_OFF, S_OFF + SAMPLE), SAMPLE)

        with blk as block:
            @block.sync
            def _(sp):
                src = t["proj"][:CONV_TILES].rearrange("c p t -> p c t")
                sp.dma_start(window[:, :, TAPS - 1:TAPS - 1 + PROMPT], src[:, :, :PROMPT]).then_inc(landed, 16)
                sp.dma_start(window[:, :, S_OFF:S_OFF + TAPS - 1], t["conv_in"]).then_inc(landed, 16)
                sp.dma_start(window[:, :, S_OFF + TAPS - 1:], src[:, :, PROMPT:]).then_inc(landed, 16)
                sp.dma_start(state[:, 1].rearrange("p h d -> p (h d)"), t["state_in"]).then_inc(landed, 16)
                sp.dma_start(gate[:], t["proj"][Z_TILE:Z_TILE + XT].rearrange("c p t -> p c t")).then_inc(z_landed, 16)
                sp.wait_ge(state_new, CHUNKS + 1)
                sp.dma_start(t["state_prompt"], state[:, 0].rearrange("p h d -> p (h d)")).then_inc(stored, 16)
                sp.wait_ge(state_new, CHUNKS + 2)
                sp.dma_start(t["state_sample"], state[:, 1].rearrange("p h d -> p (h d)")).then_inc(stored, 16)
                sp.wait_ge(stored, 32)

            @block.gpsimd
            def _(pool):
                nc.gpsimd.memset(window[:, :, :TAPS - 1], 0.0).then_inc(cleared, 1)
                nc.gpsimd.memset(state[:, 0], 0.0).then_inc(cleared, 1)
                pool.wait_ge(silu_done, CONV_TILES)
                pool.wait_ge(dt_step, 5)
                credit(pool, acum_ready, 1)
                credit(pool, transposed, 1)
                credit(pool, scored, 1)

                def stage_chunk(c, i):
                    cols, n = columns(c)
                    pool.wait_ge(transposed, i + 1)
                    pool.wait_ge(scored, i + 1)
                    pool.wait_ge(acum_ready, i + 1)
                    nc.gpsimd.tensor_copy(stage[:, :, :n], conv[:, :XT + BT, cols]).then_inc(staged, 1)
                    h = bass.ds(i * SSM_HEADS, SSM_HEADS)
                    nc.gpsimd.tensor_copy(dta_stage[:], dta[:, h]).then_inc(staged, 1)

                with pool.Fori(0, CHUNKS) as c:
                    stage_chunk(c, c)
                stage_chunk(None, CHUNKS)

            @block.scalar
            def _(act):
                act.preload_act_table_set("natural_log_exp_and_others")
                act.wait_ge(dt_step, 2)
                nc.scalar.activation(tmp[:], tmp[:], ACT.Exp).then_inc(dt_act, 1)
                act.wait_ge(dt_act, 1)
                nc.scalar.activation(tmp[:], tmp[:], ACT.Ln, bias=1.0).then_inc(dt_act, 1)
                nc.scalar.activation(head_vec[:, 1], head_vec[:, 1], ACT.Exp).then_inc(dt_act, 1)
                act.wait_ge(dt_step, 7)
                nc.scalar.activation(to_end[:], to_end[:], ACT.Exp).then_inc(dt_act, 1)
                nc.scalar.activation(decay[:], small_ps[:, 1, :CW], ACT.Exp).then_inc(dt_act, 1)
                for c in range(CONV_TILES):
                    act.wait_ge(convolved, TAPS * CONV_TILES - CONV_TILES + c + 1)
                    nc.scalar.activation(conv[:, c, :], conv[:, c, :], ACT.Silu).then_inc(silu_done, 1)
                act.wait_ge(z_landed, 16)
                nc.scalar.activation(gate[:], gate[:], ACT.Silu).then_inc(silu_done, 1)
                act.preload_act_table_set("exp_and_others")
                credit(act, c_ready, 1)
                credit(act, y_done, 1)
                credit(act, state_done, 1)

                def chunk(c, i):
                    _, n = columns(c)
                    act.wait_ge(c_ready, i + 1)
                    act.wait_ge(acum_ready, i + 2)
                    nc.scalar.activation(exp_row[:, :, :n], acum_ps[:, :, :n], ACT.Exp).then_inc(exp_row_done, 1)
                    act.wait_ge(seg_ready, i * SSM_HEADS + SSM_HEADS)
                    nc.scalar.activation(seg[:n, :, :n], seg[:n, :, :n], ACT.Exp).then_inc(seg_exp, 1)
                    act.wait_ge(transposed, i + 2)
                    act.wait_ge(state_done, i + 1)
                    nc.scalar.activation(b_rows[:n], rows_ps[:n, XT:], ACT.Copy).then_inc(b_ready, 1)

                with act.Fori(0, CHUNKS) as c:
                    chunk(c, c)
                chunk(None, CHUNKS)
                for j in range(XT):
                    act.wait_ge(gated, j + 1)
                    nc.scalar.activation(conv[:, j, :TOK], mixed[:, j, :], ACT.Square).then_inc(squared, 1)
                act.wait_ge(mean_ready, 2)
                nc.scalar.activation(gate[:, :2], gate[:, :2], ACT.Sqrt).then_inc(root_ready, 1)

            @block.tensor
            def _(pe):
                pe.wait_ge(dt_step, 5)
                for a, lhs in enumerate(("causal", "ones")):
                    last = nc.tensor.matmul(small_ps[:, a, :CW], consts[lhs][:], dta[:], start=True, stop=True)
                last.then_inc(dt_pe, 1)
                pe.wait_ge(cleared, 2)
                pe.wait_ge(landed, 64)
                credit(pe, exp_row_done, 1)
                credit(pe, seg_exp, 1)
                credit(pe, b_ready, 1)
                credit(pe, x_ready, 2)
                credit(pe, weighted, 2)
                credit(pe, y_out, XT)
                credit(pe, state_new, 1)

                def chunk(c, i):
                    cols, n = columns(c)
                    s = 0 if c is not None else 1
                    pe.wait_ge(staged, 2 * i + 2)
                    pe.wait_ge(exp_row_done, i + 1)
                    pe.wait_ge(seg_exp, i + 1)
                    for h in range(SSM_HEADS):
                        last = nc.tensor.matmul(acum_ps[:, h, :n], dta_stage[:n, h:h + 1].to_broadcast([n, P]),
                                                consts["causal"][:n, :n], start=True, stop=True)
                    last.then_inc(acum_ready, 1)
                    pe.wait_ge(weighted, 2 * i + 2)
                    for g in range(BT):
                        last = nc.tensor.matmul(score_ps[:n, g, :n], stage[:, XT + g, :n], conv[:, XT + BT + g, cols],
                                                start=True, stop=True)
                    last.then_inc(scored, 1)
                    pe.wait_ge(b_ready, i + 1)
                    pe.wait_ge(x_ready, 2 * i + 2)
                    for j in range(XT + BT):
                        last = nc.tensor.transpose(rows_ps[:n, j, :], stage[:, j, :n], consts["ident"][:])
                    last.then_inc(transposed, 1)
                    pe.wait_ge(x_ready, 2 * i + 4)
                    pe.wait_ge(b_ready, i + 2)
                    pe.wait_ge(state_new, i + 1)
                    for g in range(BT):
                        last = nc.tensor.matmul(state_ps[:, 4 * g:4 * g + 4], b_rows[:n, g], x_end[:n, 4 * g:4 * g + 4],
                                                start=True, stop=True)
                    last.then_inc(state_done, 1)
                    pe.wait_ge(weighted, 2 * i + 4)
                    pe.wait_ge(c_ready, i + 2)
                    pe.wait_ge(y_out, XT * i + XT)
                    for h in range(SSM_HEADS):
                        out = y_ps[HD * (h % 2):HD * (h % 2) + HD, h // 2, :n]
                        nc.tensor.matmul(out, xdt[:n, h], seg[:n, h, :n], start=True, stop=False)
                        last = nc.tensor.matmul(out, state[:, s, h], c_scaled[:, h, :n], start=False, stop=True)
                    last.then_inc(y_done, 1)

                with pe.Fori(0, CHUNKS) as c:
                    chunk(c, c)
                chunk(None, CHUNKS)
                for g in range(2):
                    for n in range(NBN):
                        out = group_out(g, n)
                        for j in (2 * g, 2 * g + 1):
                            pe.wait_ge(squared, j + 1)
                            last = nc.tensor.matmul(out, consts["ones"][:], conv[:, j, n * NB:(n + 1) * NB],
                                                    start=(j == 2 * g), stop=(j == 2 * g + 1))
                    last.then_inc(grouped, 1)

            @block.vector
            def _(dve):
                dt_bias = head_vec[:, 0:1].to_broadcast([P, TILES, SSM_HEADS])
                neg_a = head_vec[:, 1:2].to_broadcast([P, TILES, SSM_HEADS])
                flat = dt[:].rearrange("p (c h) -> p c h", h=SSM_HEADS)
                nc.vector.tensor_tensor(flat, dt_raw[:], dt_bias, ALU.add).then_inc(dt_step, 1)
                dve.wait_ge(dt_step, 1)
                nc.vector.scalar_tensor_tensor(tmp[:], dt[:], -1.0, dt[:], ALU.mult, ALU.min).then_inc(dt_step, 1)
                dve.wait_ge(dt_act, 3)
                nc.vector.scalar_tensor_tensor(dt[:], dt[:], 0.0, tmp[:], ALU.max, ALU.add).then_inc(dt_step, 1)
                dve.wait_ge(dt_step, 3)
                nc.vector.scalar_tensor_tensor(dta[:].rearrange("p (c h) -> p c h", h=SSM_HEADS), flat, -1.0, neg_a,
                                               ALU.mult, ALU.mult).then_inc(dt_step, 1)
                dve.wait_ge(dt_step, 4)
                nc.vector.memset(dta[SAMPLE:SAMPLE * 2, CW - SSM_HEADS:], 0.0)
                nc.vector.memset(dta[HD:, CW - SSM_HEADS:], 0.0).then_inc(dt_step, 1)
                dve.wait_ge(dt_pe, 1)
                nc.vector.tensor_copy(acum[:], small_ps[:, 0, :CW]).then_inc(dt_step, 1)
                dve.wait_ge(dt_step, 6)
                nc.vector.scalar_tensor_tensor(to_end[:], small_ps[:, 1, :CW], 1.0, acum[:],
                                               ALU.mult, ALU.subtract).then_inc(dt_step, 1)
                dve.wait_ge(dt_act, 5)
                nc.vector.tensor_tensor(dt_end[:], dt[:], to_end[:], ALU.mult).then_inc(dt_step, 1)
                dve.wait_ge(landed, 64)
                dve.wait_ge(cleared, 2)
                for j in range(TAPS):
                    for c in range(CONV_TILES):
                        if j:
                            dve.wait_ge(convolved, CONV_TILES * (j - 1) + c + 1)
                            nc.vector.scalar_tensor_tensor(conv[:, c, :], window[:, c, j:j + CONV_OUT], conv_wb[:, c, j:j + 1],
                                                           conv[:, c, :], ALU.mult, ALU.add).then_inc(convolved, 1)
                        else:
                            nc.vector.tensor_scalar(conv[:, c, :], window[:, c, :CONV_OUT], conv_wb[:, c, 0:1],
                                                    conv_wb[:, c, TAPS:], ALU.mult, ALU.add).then_inc(convolved, 1)
                dve.wait_ge(silu_done, CONV_TILES)
                dve.wait_ge(dt_step, 8)

                def chunk(c, i):
                    cols, n = columns(c)
                    s = 0 if c is not None else 1
                    per_head = bass.ds(i * SSM_HEADS, SSM_HEADS)
                    dve.wait_ge(exp_row_done, i + 2)
                    dve.wait_ge(y_done, i + 1)
                    for h in range(SSM_HEADS):
                        nc.vector.scalar_tensor_tensor(seg[:n, h, :n], acum_ps[:n, h, :n],
                                                       acum[:n, bass.ds(i * SSM_HEADS + h, 1)],
                                                       consts["masked"][:n, :n], ALU.subtract, ALU.add).then_inc(seg_ready, 1)
                    for g in range(BT):
                        heads = slice(4 * g, 4 * g + 4)
                        c_rows = conv[:, XT + BT + g:XT + BT + g + 1, cols].to_broadcast([P, 4, n])
                        last = nc.vector.tensor_tensor(c_scaled[:, heads, :n], exp_row[:, heads, :n], c_rows, ALU.mult)
                    last.then_inc(c_ready, 1)
                    dve.wait_ge(transposed, i + 2)
                    dve.wait_ge(state_done, i + 1)
                    x_rows = rows_ps[:n, :XT].rearrange("p j (a d) -> p (j a) d", a=2)
                    for to, by in ((xdt, dt), (x_end, dt_end)):
                        scale = by[:n, per_head].unsqueeze(2).to_broadcast([n, SSM_HEADS, HD])
                        nc.vector.tensor_tensor(to[:n], x_rows, scale, ALU.mult).then_inc(x_ready, 1)
                    dve.wait_ge(seg_exp, i + 2)
                    dve.wait_ge(scored, i + 2)
                    for g in range(BT):
                        heads = slice(4 * g, 4 * g + 4)
                        nc.vector.tensor_tensor(seg[:n, heads, :n], seg[:n, heads, :n],
                                                score_ps[:n, g:g + 1, :n].to_broadcast([n, 4, n]),
                                                ALU.mult).then_inc(weighted, 1)
                    dve.wait_ge(y_done, i + 2)
                    for j in range(XT):
                        nc.vector.scalar_tensor_tensor(mixed[:, j, bass.ds(i * P, n)], conv[:, j, cols], d_skip[:, j:j + 1],
                                                       y_ps[:, j, :n], ALU.mult, ALU.add).then_inc(y_out, 1)
                    scale = decay[:, per_head].unsqueeze(2).to_broadcast([P, SSM_HEADS, HD])
                    nc.vector.tensor_tensor(state[:, s], state[:, s], scale, ALU.mult).then_inc(decayed, 1)
                    dve.wait_ge(decayed, i + 1)
                    nc.vector.tensor_tensor(state[:, s], state[:, s], state_ps[:], ALU.add).then_inc(state_new, 1)
                    dve.wait_ge(state_new, i + 2)

                with dve.Fori(0, CHUNKS) as c:
                    chunk(c, c)
                chunk(None, CHUNKS)
                dve.wait_ge(silu_done, CONV_TILES + 1)
                dve.wait_ge(y_out, XT * (TILES + 1))
                for j in range(XT):
                    nc.vector.tensor_tensor(mixed[:, j, :], mixed[:, j, :], gate[:, j, :], ALU.mult).then_inc(gated, 1)
                dve.wait_ge(gated, XT)
                for g in range(2):
                    dve.wait_ge(grouped, g + 1)
                    for n in range(NBN):
                        last = nc.vector.tensor_scalar(gate[:, g, n * NB:(n + 1) * NB], group_out(g, n),
                                                       2.0 / (SSM_HEADS * HD), EPS, ALU.mult, ALU.add)
                    last.then_inc(mean_ready, 1)
                dve.wait_ge(root_ready, 1)
                nc.vector.reciprocal(gate[:, :2], gate[:, :2]).then_inc(rstd_ready, 1)
                dve.wait_ge(rstd_ready, 1)
                for j in range(XT):
                    nc.vector.scalar_tensor_tensor(mixed[:, j, :], mixed[:, j, :], ssm_norm_w[:, j:j + 1], gate[:, j // 2, :],
                                                   ALU.mult, ALU.mult)


class Job:

    def __init__(self, kind, n, h=0, qb=0, j=0, b0=0):
        self.kind, self.n, self.h, self.qb, self.j, self.b0 = kind, n, h, qb, j, b0
        self.slot = n % 4
        if kind == "prompt":
            self.step = 4 * qb + 3 - j
            self.diag = self.step < 4
            self.lo = max(0, j - 4 * qb) * P
            self.hi, self.keys = QW, P
            self.t_lo = self.lo + P if self.diag else self.lo
        else:
            self.lo, self.hi = 0, 2 * SAMPLE if kind == "new" else QW
            self.keys = SAMPLE if kind == "new" else P

    @property
    def cols(self):
        return slice(self.lo, self.hi)


def attention_jobs():
    jobs = []
    for qb in range(PROMPT // QW):
        for j in range(4 * qb + 3, -1, -1):
            for h in range(2):
                jobs.append(Job("prompt", len(jobs), h, qb, j))
    jobs.append(Job("new", len(jobs)))
    jobs.append(Job("past", len(jobs), b0=8))
    jobs.append(Job("past", len(jobs), b0=0))
    return jobs


def attention_phase(nc, consts, t, mixed):
    jobs = attention_jobs()
    JN = len(jobs)
    SL = slice(PROMPT, TOK)
    with phase(nc, "sb") as (sb, ps, sem, blk):
        q, k, v = (sb(n, [P, 2, TOK]) for n in "qkv")
        past_k = sb("past_k", [P, 2, PAST])
        past_v = sb("past_v", [P, 2, PB, P])
        q_diag = sb("q_diag", [P, 2, 2 * SAMPLE])
        v_rows = sb("v_rows", [P, TILES, P])
        e, softplus, weight = sb("e", [P, 4, QW]), sb("softplus", [P, 4, QW]), sb("weight", [P, 4, QW])
        later = sb("later", [P, 2, 2, QW])
        s_later = sb("s_later", [P, PB, 2 * SAMPLE])
        strict, strict_masked, neg_ones = sb("strict", [P, P]), sb("strict_masked", [P, P]), sb("neg_ones", [P, P])
        z = ps("z", [P, 4, QW])
        o = ps("o", [P, 2, QW])
        spare = ps("spare", [P, 2, 4, P])
        const_landed = sem("const_landed")
        landed = [sem("landed0"), sem("landed1")]
        cleared = sem("cleared")
        scaled, v_turned, v_copied = sem("scaled"), sem("v_turned"), sem("v_copied")
        z_ready, clipped, exp_done, log_done, sp_ready = (
            sem("z_ready"), sem("clipped"), sem("exp_done"), sem("log_done"), sem("sp_ready"))
        sums_ready, w_ready, pv_done, o_copied, dve_step = (
            sem("sums_ready"), sem("w_ready"), sem("pv_done"), sem("o_copied"), sem("dve_step"))

        def keys_of(job):
            return slice(0, job.keys)

        with blk as block:
            @block.sync
            def _(sp):
                for tile, src in ((strict, "strict"), (strict_masked, "strict_masked"), (neg_ones, "neg_ones")):
                    sp.dma_start(tile[:], t[src]).then_inc(const_landed, 16)

                def load(p, u):
                    for to, base in ((q, Q_TILE), (k, K_TILE), (v, V_TILE)):
                        sp.dma_start(to[:, u], t["proj"][bass.ds(p + base, 1)].rearrange("a p t -> (a p) t")).then_inc(landed[u], 16)
                    sp.dma_start(past_k[:, u], t["past_k"][bass.ds(p, 1)].rearrange("a p t -> (a p) t")).then_inc(landed[u], 16)
                    sp.dma_start(past_v[:, u].rearrange("p b d -> p (b d)"),
                                 t["past_v"][bass.ds(p, 1)].rearrange("a p b d -> (a p) (b d)")).then_inc(landed[u], 16)

                for p in range(PAIRS):
                    if p >= 2:
                        sp.wait_ge(pv_done, 4 + JN * (p - 1))
                    load(p, p % 2)

            @block.gpsimd
            def _(pool):
                nc.gpsimd.memset(q_diag[:], 0.0).then_inc(cleared, 1)

            @block.scalar
            def _(act):
                credit(act, pv_done, 4)
                act.wait_ge(cleared, 1)
                act.preload_act_table_set("natural_log_exp_and_others")

                def weights(p, job):
                    act.wait_ge(sums_ready, JN * p + job.n + 5)
                    act.wait_ge(pv_done, JN * p + job.n + 1)
                    nc.scalar.activation(weight[keys_of(job), job.slot, job.cols], z[keys_of(job), job.slot, job.cols],
                                         ACT.Exp).then_inc(w_ready, 1)

                def copy_out(p, job):
                    act.wait_ge(pv_done, JN * p + job.n + 5)
                    if job.kind == "prompt":
                        to, src = slice(job.qb * QW, job.qb * QW + QW), o[:, job.qb, :]
                    else:
                        to, src = SL, spare[:, 1, 0, :SAMPLE]
                    nc.scalar.activation(mixed[:, bass.ds(p + 4, 1), to], src.unsqueeze(1), ACT.Copy).then_inc(o_copied, 1)

                def pair(p, u):
                    act.wait_ge(landed[u], (p - u) * 40 + 80)
                    for h in range(2):
                        hp = slice(HD * h, HD * h + HD)
                        nc.scalar.activation(q_diag[hp, u, h * SAMPLE:h * SAMPLE + SAMPLE], q[hp, u, SL], ACT.Copy,
                                             scale=HD ** -0.5).then_inc(scaled, 1)
                    nc.scalar.activation(q[:, u, :PROMPT], q[:, u, :PROMPT], ACT.Copy, scale=HD ** -0.5).then_inc(scaled, 1)
                    for part, (lo, hi) in enumerate(((0, 4), (4, 8), (8, 9))):
                        act.wait_ge(v_turned, 3 * p + part + 1)
                        n = P if part < 2 else SAMPLE
                        nc.scalar.activation(v_rows[:n, lo:hi, :], spare[:n, part % 2, :hi - lo, :], ACT.Copy).then_inc(v_copied, 1)
                    for step in range(JN + 3):
                        if step < JN:
                            job = jobs[step]
                            tile = e[keys_of(job), job.slot, job.cols]
                            act.wait_ge(clipped, JN * p + job.n + 1)
                            nc.scalar.activation(tile, tile, ACT.Exp).then_inc(exp_done, 1)
                            act.wait_ge(exp_done, JN * p + job.n + 1)
                            nc.scalar.activation(tile, tile, ACT.Ln, bias=1.0).then_inc(log_done, 1)
                        if 2 <= step < JN + 2:
                            weights(p, jobs[step - 2])
                        done = jobs[step - 3] if step >= 3 else None
                        if done and (done.kind == "past" and done.b0 == 0 or done.kind == "prompt" and done.j == 0 and done.h):
                            copy_out(p, done)

                for p in range(PAIRS):
                    pair(p, p % 2)

            @block.tensor
            def _(pe):
                pe.wait_ge(const_landed, 48)
                credit(pe, w_ready, 4)
                credit(pe, o_copied, 3)
                credit(pe, v_copied, 3)

                def turn_v(p, u):
                    pe.wait_ge(landed[u], (p - u) * 40 + 80)
                    pe.wait_ge(pv_done, JN * p + 4)
                    pe.wait_ge(o_copied, 3 * p + 3)
                    for part, (lo, hi) in enumerate(((0, 4), (4, 8), (8, 9))):
                        if part == 2:
                            pe.wait_ge(v_copied, 3 * p + 4)
                        for b in range(lo, hi):
                            n = tokens_of(b)
                            last = nc.tensor.transpose(spare[:n, part % 2, b - lo, :], v[:, u, b * P:b * P + n], consts["ident"][:])
                        last.then_inc(v_turned, 1)

                def scores(p, u, job):
                    pe.wait_ge(w_ready, JN * p + job.n + 1)
                    if job.kind == "prompt":
                        hp = slice(HD * job.h, HD * job.h + HD)
                        last = nc.tensor.matmul(z[:, job.slot, job.cols], k[hp, u, job.j * P:job.j * P + P],
                                                q[hp, u, job.qb * QW + job.lo:job.qb * QW + QW],
                                                start=True, stop=True, skip_group_check=True)
                    else:
                        for b in range(1 if job.kind == "new" else 8):
                            rows = k[:, u, SL] if job.kind == "new" else past_k[:, u, (job.b0 + b) * P:(job.b0 + b + 1) * P]
                            last = nc.tensor.matmul(z[keys_of(job), job.slot, b * 64:b * 64 + 64], rows, q_diag[:, u],
                                                    start=True, stop=True, skip_group_check=True)
                    last.then_inc(z_ready, 1)

                def suffix_sums(p, job):
                    pe.wait_ge(sp_ready, JN * p + job.n + 1)
                    bank, sp_tile, kk = z[keys_of(job), job.slot, :], softplus[keys_of(job), job.slot, :], job.keys

                    def add(cols, lhs, rhs):
                        return nc.tensor.matmul(bank[:, cols], lhs, rhs, start=False, stop=True, skip_group_check=True)

                    if job.kind == "prompt" and job.diag:
                        add(slice(job.lo, job.lo + P), consts["ident"][:], strict_masked[:])
                    if job.kind == "new":
                        for h in range(2):
                            add(slice(h * SAMPLE, h * SAMPLE + SAMPLE), consts["ident"][:kk, :kk], strict_masked[:kk, :SAMPLE])
                    last = add(job.cols, consts["suffix"][:kk, :kk], sp_tile[:, job.cols])
                    if job.kind == "prompt" and job.step:
                        cols = slice(job.t_lo, QW)
                        last = add(cols, neg_ones[:], later[:, job.h, job.step % 2, cols])
                    if job.kind == "past":
                        new = softplus[:SAMPLE, jobs[JN - 3].slot, :2 * SAMPLE]
                        for b in range(8):
                            last = add(slice(b * 64, b * 64 + 64), neg_ones[:SAMPLE], new)
                        nb = min(job.b0 + 8, PB - 1) - job.b0
                        last = add(slice(0, nb * 64), neg_ones[:], s_later[:, job.b0:job.b0 + nb].rearrange("p b c -> p (b c)"))
                    last.then_inc(sums_ready, 1)

                def outputs(p, u, job):
                    pe.wait_ge(w_ready, JN * p + job.n + 5)
                    if job.kind == "prompt":
                        if job.step == 0:
                            pe.wait_ge(o_copied, 3 * p + job.qb + 1)
                        hp = slice(HD * job.h, HD * job.h + HD)
                        last = nc.tensor.matmul(o[hp, job.qb, job.cols], v_rows[:, job.j, hp], weight[:, job.slot, job.cols],
                                                start=(job.step == 0), stop=(job.j == 0), skip_group_check=True)
                    else:
                        for b in range(1 if job.kind == "new" else 8):
                            for h in range(2):
                                hp = slice(HD * h, HD * h + HD)
                                rows = v_rows[:SAMPLE, TILES - 1, hp] if job.kind == "new" else past_v[:, u, job.b0 + b, hp]
                                at = (2 * b + h) * SAMPLE
                                last = nc.tensor.matmul(spare[hp, 1, 0, :SAMPLE], rows, weight[keys_of(job), job.slot, at:at + SAMPLE],
                                                        start=(job.kind == "new"), stop=(job.kind == "past" and job.b0 == 0 and b == 7),
                                                        skip_group_check=True)
                    last.then_inc(pv_done, 1)

                def pair(p, u):
                    turn_v(p, u)
                    pe.wait_ge(scaled, 3 * p + 3)
                    for step in range(JN + 3):
                        if step < JN:
                            scores(p, u, jobs[step])
                        if 2 <= step < JN + 2:
                            suffix_sums(p, jobs[step - 2])
                        if step == 3:
                            pe.wait_ge(v_copied, 3 * p + 6)
                        if step >= 3:
                            outputs(p, u, jobs[step - 3])

                for p in range(PAIRS):
                    pair(p, p % 2)

            @block.vector
            def _(dve):
                dve.wait_ge(const_landed, 48)
                credit(dve, sums_ready, 4)
                links = [0]

                def link(instruction):
                    links[0] += 1
                    instruction.then_inc(dve_step, 1)
                    dve.wait_ge(dve_step, links[0])

                def clip(p, job):
                    dve.wait_ge(z_ready, JN * p + job.n + 1)
                    nc.vector.tensor_scalar(e[keys_of(job), job.slot, job.cols], z[keys_of(job), job.slot, job.cols],
                                            40.0, None, ALU.min).then_inc(clipped, 1)

                def soft(p, job):
                    tile = softplus[keys_of(job), job.slot, :]
                    dve.wait_ge(log_done, JN * p + job.n + 1)
                    dve.wait_ge(sums_ready, JN * p + job.n + 1)
                    soft_max = nc.vector.tensor_tensor(tile[:, job.cols], z[keys_of(job), job.slot, job.cols],
                                                       e[keys_of(job), job.slot, job.cols], ALU.max)
                    if job.kind == "prompt":
                        first = slice(job.lo, job.lo + P)
                        if job.diag:
                            link(soft_max)
                            masking = nc.vector.tensor_tensor(tile[:, first], tile[:, first], strict[:], ALU.mult)
                        last = masking if job.diag else soft_max
                        if job.j:
                            link(last)
                            dve.wait_ge(sums_ready, JN * p + job.n + 3)
                            to = later[:, job.h, (job.step + 1) % 2, :]
                            if job.diag:
                                last = nc.vector.tensor_copy(to[:, first], tile[:, first])
                            if job.step:
                                cols = slice(job.t_lo, QW)
                                last = nc.vector.tensor_tensor(to[:, cols], later[:, job.h, job.step % 2, cols], tile[:, cols], ALU.add)
                    elif job.kind == "new":
                        link(soft_max)
                        halves = tile[:, :64].rearrange("p (h q) -> p h q", h=2)
                        last = nc.vector.tensor_tensor(halves, halves, strict[:SAMPLE, :SAMPLE].unsqueeze(1).to_broadcast([SAMPLE, 2, SAMPLE]), ALU.mult)
                    else:
                        link(soft_max)
                        if job.b0:
                            dve.wait_ge(sums_ready, JN * p + 4)
                            link(nc.vector.tensor_copy(s_later[:, PB - 2], tile[:, 7 * 64:8 * 64]))
                        for b in range(PB - 3 if job.b0 else 7, job.b0 - 1 if job.b0 else -1, -1):
                            nxt = jobs[JN - 2 if b + 1 >= 8 else JN - 1]
                            last = nc.vector.tensor_tensor(s_later[:, b], s_later[:, b + 1],
                                                           softplus[:, nxt.slot, (b + 1) % 8 * 64:(b + 1) % 8 * 64 + 64], ALU.add)
                            if b > job.b0:
                                link(last)
                    last.then_inc(sp_ready, 1)
                    dve.wait_ge(sp_ready, JN * p + job.n + 1)

                for p in range(PAIRS):
                    clip(p, jobs[0])
                    for n in range(JN):
                        if n + 1 < JN:
                            clip(p, jobs[n + 1])
                        soft(p, jobs[n])


def output_projection(nc, mixed, h, w_out, x, h_dram):
    with phase(nc, "outproj") as (sb, ps, sem, blk):
        m_hi, m_lo = sb("m_hi", [P, DC, TOK], F32R), sb("m_lo", [P, DC, TOK], F32R)
        w_raw = sb("w_raw", [P, DC, P])
        w_hi, w_lo = sb("w_hi", [P, 2, DC, P], F32R), sb("w_lo", [P, 2, DC, P], F32R)
        residual = sb("residual", [P, 2, TOK])
        acc = ps("acc", [P, 2, 3, 512])
        w_landed, x_landed = sem("w_landed"), [sem("x_landed0"), sem("x_landed1")]
        m_hi_ready, m_lo_ready = sem("m_hi_ready"), sem("m_lo_ready")
        hi_ready, lo_ready, projected, added, stored = (
            sem("hi_ready"), sem("lo_ready"), sem("projected"), sem("added"), sem("stored"))
        pairs = DC // 2
        with blk as block:
            @block.sync
            def _(sp):
                credit(sp, lo_ready, 1)
                with sp.Fori(0, pairs) as i:
                    for u in range(2):
                        sp.wait_ge(lo_ready, 2 * i + u + 1)
                        sp.dma_start(w_raw[:], w_out[bass.ds(2 * i + u, 1)].rearrange("a p k m -> p (a k) m")).then_inc(w_landed, 16)
                        sp.wait_ge(added, 6 * i + 3 * u + 3)
                        sp.dma_start(residual[:, u], x[:, bass.ds(2 * i + u, 1), :].rearrange("p a t -> p (a t)")).then_inc(x_landed[u], 16)
                sp.wait_ge(added, 3 * DC + 6)
                sp.dma_start(h_dram, h[:]).then_inc(stored, 16)
                sp.wait_ge(stored, 16)

            @block.scalar
            def _(act):
                for k in range(DC):
                    nc.scalar.activation(m_hi[:, k], mixed[:, k], ACT.Copy).then_inc(m_hi_ready, 1)
                with act.Fori(0, pairs) as i:
                    for u in range(2):
                        act.wait_ge(w_landed, 32 * i + 16 * u + 16)
                        act.wait_ge(projected, 6 * i + 3 * u + 3)
                        nc.scalar.activation(w_hi[:, u], w_raw[:], ACT.Copy).then_inc(hi_ready, 1)

            @block.vector
            def _(dve):
                credit(dve, added, 6)
                for k in range(DC):
                    dve.wait_ge(m_hi_ready, k + 1)
                    nc.vector.tensor_tensor(m_lo[:, k], mixed[:, k], m_hi[:, k].bitcast(F32), ALU.subtract).then_inc(m_lo_ready, 1)

                def split_low(i, u):
                    dve.wait_ge(hi_ready, 2 * i + u + 1)
                    nc.vector.tensor_tensor(w_lo[:, u], w_raw[:], w_hi[:, u].bitcast(F32), ALU.subtract).then_inc(lo_ready, 1)

                def add_residual(i, u):
                    dve.wait_ge(x_landed[u], 16 * i + 16)
                    for n in range(NBN):
                        tok = slice(n * NB, n * NB + NB)
                        dve.wait_ge(projected, 6 * i + 3 * u + n + 7)
                        nc.vector.tensor_tensor(h[:, bass.ds(2 * i + u, 1), tok], acc[:, u:u + 1, n, :NB], residual[:, u:u + 1, tok],
                                                ALU.add).then_inc(added, 1)

                split_low(0, 0)
                with dve.Fori(0, pairs - 1) as i:
                    split_low(i, 1)
                    add_residual(i, 0)
                    split_low(i + 1, 0)
                    add_residual(i, 1)
                split_low(pairs - 1, 1)
                add_residual(pairs - 1, 0)
                add_residual(pairs - 1, 1)

            @block.tensor
            def _(pe):
                credit(pe, projected, 6)
                pe.wait_ge(m_lo_ready, DC)
                with pe.Fori(0, pairs) as i:
                    for u in range(2):
                        pe.wait_ge(lo_ready, 2 * i + u + 2)
                        for n in range(NBN):
                            pe.wait_ge(added, 6 * i + 3 * u + n + 1)
                            project(nc, acc[:, u, n, :NB], w_hi[:, u], w_lo[:, u], m_hi, m_lo, n).then_inc(projected, 1)


def held(dve, sem, value, passed):
    dve.wait_ge(sem, value)
    dve.sem_inc(passed, 1)


def retrieval_phase(nc, x_hi, x_lo, w_q, keys, top_v, top_i):
    with phase(nc, "retrieve") as (sb, ps, sem, blk):
        w_raw = sb("w_raw", [P, DC, P])
        w_hi, w_lo = sb("w_hi", [P, 2, DC, P], F32R), sb("w_lo", [P, 2, DC, P], F32R)
        key_tile = sb("key_tile", [P, 2, KEYS])
        query = sb("query", [P, 2, TOK])
        scores = sb("scores", [P, 2, TILES, KEYS])
        rest = sb("rest", [P, TILES, KEYS])
        best_v, best_i = sb("best_v", [P, TILES, TOPK]), sb("best_i", [P, TILES, TOPK], U32)
        acc = ps("acc", [P, 3, 512])
        score_ps = ps("score_ps", [P, 3, 4, KEYS])
        w_landed, k_landed = sem("w_landed"), [sem("k_landed0"), sem("k_landed1")]
        hi_ready, lo_ready, projected, query_ready = sem("hi_ready"), sem("lo_ready"), sem("projected"), sem("query_ready")
        scored, copied = sem("scored"), sem("copied")
        max1, place1, replaced, max2, place2, kept = (sem(n) for n in ("max1", "place1", "replaced", "max2", "place2", "kept"))
        passed, cleared = sem("passed"), sem("cleared")
        pairs = HALVES // 2
        with blk as block:
            @block.sync
            def _(sp):
                credit(sp, lo_ready, 1)
                with sp.Fori(0, pairs) as i:
                    for u in range(2):
                        sp.wait_ge(lo_ready, 2 * i + u + 1)
                        sp.dma_start(w_raw[:], w_q[bass.ds(2 * i + u, 1)].rearrange("a p k m -> p (a k) m")).then_inc(w_landed, 16)
                        sp.wait_ge(scored, 6 * i + 3 * u + 3)
                        sp.dma_start(key_tile[:, u], keys[bass.ds(2 * i + u, 1)].rearrange("a p n -> (a p) n")).then_inc(k_landed[u], 16)

            @block.gpsimd
            def _(pool):
                nc.gpsimd.memset(best_v[:, TILES - 1], 0.0).then_inc(cleared, 1)
                nc.gpsimd.memset(best_i[:, TILES - 1], 0).then_inc(cleared, 1)

            @block.scalar
            def _(act):
                credit(act, scored, 6)
                credit(act, kept, 2)

                def split_high(i, u):
                    act.wait_ge(w_landed, 32 * i + 16 * u + 16)
                    act.wait_ge(projected, 6 * i + 3 * u + 3)
                    nc.scalar.activation(w_hi[:, u], w_raw[:], ACT.Copy).then_inc(hi_ready, 1)

                def copy_query(i, u):
                    act.wait_ge(scored, 6 * i + 3 * u + 3)
                    for n in range(NBN):
                        act.wait_ge(projected, 6 * i + 3 * u + n + 7)
                        nc.scalar.activation(query[:, u, n * NB:n * NB + NB], acc[:, n, :NB], ACT.Copy).then_inc(query_ready, 1)

                def copy_scores(i, u):
                    act.wait_ge(kept, 2 * i + u + 1)
                    for b in range(3):
                        act.wait_ge(scored, 6 * i + 3 * u + b + 7)
                        rows, last = (P, 4) if b < 2 else (SAMPLE, 1)
                        nc.scalar.activation(scores[:rows, u, 4 * b:4 * b + last], score_ps[:rows, b, :last], ACT.Copy).then_inc(copied, 1)

                split_high(0, 0)
                split_high(0, 1)
                copy_query(0, 0)
                with act.Fori(0, pairs - 1) as i:
                    split_high(i + 1, 0)
                    copy_query(i, 1)
                    copy_scores(i, 0)
                    split_high(i + 1, 1)
                    copy_query(i + 1, 0)
                    copy_scores(i, 1)
                copy_query(pairs - 1, 1)
                copy_scores(pairs - 1, 0)
                copy_scores(pairs - 1, 1)

            @block.tensor
            def _(pe):
                credit(pe, projected, 6)
                credit(pe, query_ready, 3)
                credit(pe, copied, 3)

                def queries(i, u):
                    pe.wait_ge(lo_ready, 2 * i + u + 2)
                    for n in range(NBN):
                        pe.wait_ge(query_ready, 6 * i + 3 * u + n + 1)
                        project(nc, acc[:, n, :NB], w_hi[:, u], w_lo[:, u], x_hi, x_lo, n).then_inc(projected, 1)

                def score(i, u):
                    pe.wait_ge(query_ready, 6 * i + 3 * u + 6)
                    pe.wait_ge(k_landed[u], 16 * i + 16)
                    for b in range(3):
                        pe.wait_ge(copied, 6 * i + 3 * u + b + 1)
                        for tile in range(4 * b, min(4 * b + 4, TILES)):
                            n = tokens_of(tile)
                            last = nc.tensor.matmul(score_ps[:n, b, tile - 4 * b], query[:, u, tile * P:tile * P + n],
                                                    key_tile[:, u], start=True, stop=True)
                        last.then_inc(scored, 1)

                queries(0, 0)
                with pe.Fori(0, pairs - 1) as i:
                    queries(i, 1)
                    score(i, 0)
                    queries(i + 1, 0)
                    score(i, 1)
                queries(pairs - 1, 1)
                score(pairs - 1, 0)
                score(pairs - 1, 1)

            @block.vector
            def _(dve):
                dve.wait_ge(cleared, 2)

                def split_low(i, u):
                    dve.wait_ge(hi_ready, 2 * i + u + 1)
                    nc.vector.tensor_tensor(w_lo[:, u], w_raw[:], w_hi[:, u].bitcast(F32), ALU.subtract).then_inc(lo_ready, 1)

                def best(i, u):
                    at = 2 * i + u
                    rows = [(tile, tokens_of(tile)) for tile in range(TILES)]
                    first, second = slice(0, 8), slice(8, 16)
                    held(dve, copied, 6 * i + 3 * u + 6, passed)
                    held(dve, kept, at + 2, passed)
                    for tile, n in rows:
                        nc.vector.max(best_v[:n, tile, first], scores[:n, u, tile]).then_inc(max1, 1)
                    held(dve, max1, TILES * at + TILES, passed)
                    for tile, n in rows:
                        nc.vector.max_index(best_i[:n, tile, first], best_v[:n, tile, first], scores[:n, u, tile]).then_inc(place1, 1)
                    for tile, n in rows:
                        nc.vector.match_replace(rest[:n, tile], best_v[:n, tile, first], scores[:n, u, tile], LOWEST).then_inc(replaced, 1)
                    held(dve, replaced, TILES * at + TILES, passed)
                    for tile, n in rows:
                        nc.vector.max(best_v[:n, tile, second], rest[:n, tile]).then_inc(max2, 1)
                    held(dve, max2, TILES * at + TILES, passed)
                    for tile, n in rows:
                        nc.vector.max_index(best_i[:n, tile, second], best_v[:n, tile, second], rest[:n, tile]).then_inc(place2, 1)
                    dve.wait_ge(place2, TILES * at + TILES)
                    nc.vector.tensor_copy(top_v[:, :, bass.ds(at, 1), :], best_v[:].unsqueeze(2))
                    nc.vector.tensor_copy(top_i[:, :, bass.ds(at, 1), :], best_i[:].unsqueeze(2)).then_inc(kept, 1)

                split_low(0, 0)
                split_low(0, 1)
                with dve.Fori(0, pairs - 1) as i:
                    split_low(i + 1, 0)
                    best(i, 0)
                    split_low(i + 1, 1)
                    best(i, 1)
                best(pairs - 1, 0)
                best(pairs - 1, 1)


def routing_phase(nc, consts, t, top_v, top_i, routes):
    HK = PEER_HEADS * TOPK
    with phase(nc, "route") as (sb, ps, sem, blk):
        cand, rest = sb("cand", [P, PEER_HEADS, TOPK, TOPK]), sb("rest", [P, PEER_HEADS, TOPK * TOPK])
        best_v, best_i = sb("best_v", [P, PEER_HEADS, TOPK]), sb("best_i", [P, PEER_HEADS, TOPK], U32)
        half_i, half = sb("half_i", [P, 2, PEER_HEADS, TOPK], U32), sb("half", [P, 2, HK])
        found = sb("found", [P, 2, PEER_HEADS * TOPK, TOPK])
        rows = sb("rows", [P, 3, HK])
        shifted = sb("shifted", [P, PEER_HEADS, TOPK])
        total = sb("total", [P, PEER_HEADS])
        iota = sb("iota", [P, P])
        turned = ps("turned", [P, 2, 4, P])
        landed, passed = sem("landed"), sem("passed")
        step, maxed, exp_done, rows_ready, transposed, copied = (
            sem("step"), sem("maxed"), sem("exp_done"), sem("rows_ready"), sem("transposed"), sem("copied"))
        with blk as block:
            @block.sync
            def _(sp):
                sp.dma_start(iota[:], t["iota"]).then_inc(landed, 16)

            @block.scalar
            def _(act):
                act.preload_act_table_set("exp_and_others")

                def tile(i, n, at):
                    act.wait_ge(maxed, i + 1)
                    nc.scalar.activation(shifted[:n], shifted[:n], ACT.Exp).then_inc(exp_done, 1)
                    act.wait_ge(transposed, i + 2)
                    nc.scalar.activation(routes[:, :, bass.ds(at, n)], turned[:, 0, :3, :n], ACT.Copy).then_inc(copied, 1)

                with act.Fori(0, TILES - 1) as i:
                    tile(i, P, i * P)
                tile(TILES - 1, SAMPLE, PROMPT)

            @block.tensor
            def _(pe):
                credit(pe, copied, 1)
                credit(pe, transposed, 1)

                def tile(i, n):
                    pe.wait_ge(rows_ready, i + 1)
                    pe.wait_ge(copied, i + 1)
                    for a in range(3):
                        last = nc.tensor.transpose(turned[:, 0, a, :n], rows[:n, a], consts["ident"][:n, :n])
                    last.then_inc(transposed, 1)

                with pe.Fori(0, TILES - 1) as i:
                    tile(i, P)
                tile(TILES - 1, SAMPLE)

            @block.vector
            def _(dve):
                dve.wait_ge(landed, 16)
                STEPS = 12

                def tile(i, n):
                    done = [0]

                    def link(instruction):
                        instruction.then_inc(step, 1)
                        done[0] += 1
                        held(dve, step, i * STEPS + done[0], passed)

                    halves = top_v[:n, bass.ds(i, 1)].rearrange("p a (h s) k -> p (a h) s k", s=2)
                    places = top_i[:n, bass.ds(i, 1)].rearrange("p a (h s) k -> p (a h) s k", s=2)
                    shape = [n, PEER_HEADS, TOPK, TOPK]
                    link(nc.vector.tensor_tensor(cand[:n], halves[:, :, 0].unsqueeze(3).to_broadcast(shape),
                                                 halves[:, :, 1].unsqueeze(2).to_broadcast(shape), ALU.add))
                    sums = cand[:n].rearrange("p h i j -> p h (i j)")
                    for h in range(PEER_HEADS):
                        last = nc.vector.max(best_v[:n, h, :8], sums[:, h])
                    link(last)
                    for h in range(PEER_HEADS):
                        nc.vector.max_index(best_i[:n, h, :8], best_v[:n, h, :8], sums[:, h])
                    for h in range(PEER_HEADS):
                        last = nc.vector.match_replace(rest[:n, h], best_v[:n, h, :8], sums[:, h], LOWEST)
                    link(last)
                    for h in range(PEER_HEADS):
                        last = nc.vector.max(best_v[:n, h, 8:], rest[:n, h])
                    link(last)
                    nc.vector.tensor_tensor(shifted[:n], best_v[:n], best_v[:n, :, :1].to_broadcast([n, PEER_HEADS, TOPK]),
                                            ALU.subtract).then_inc(maxed, 1)
                    for h in range(PEER_HEADS):
                        last = nc.vector.max_index(best_i[:n, h, 8:], best_v[:n, h, 8:], rest[:n, h])
                    link(last)
                    nc.vector.tensor_scalar(half_i[:n, 0], best_i[:n], 4, None, ALU.logical_shift_right)
                    link(nc.vector.tensor_scalar(half_i[:n, 1], best_i[:n], TOPK - 1, None, ALU.bitwise_and))
                    link(nc.vector.tensor_copy(half[:n], half_i[:n].rearrange("p a h k -> p a (h k)")))
                    wide = [n, HK, TOPK]
                    for s in range(2):
                        last = nc.vector.tensor_tensor(found[:n, s], half[:n, s].unsqueeze(2).to_broadcast(wide),
                                                       iota[:n, :TOPK].unsqueeze(1).to_broadcast(wide), ALU.is_equal)
                    link(last)
                    for s in range(2):
                        by_head = found[:n, s].rearrange("p (h k) i -> p h k i", h=PEER_HEADS)
                        last = nc.vector.tensor_tensor(by_head, by_head, places[:, :, s].unsqueeze(2).to_broadcast(shape), ALU.mult)
                    link(last)
                    dve.wait_ge(transposed, i + 1)
                    nc.vector.tensor_reduce(rows[:n, 0:2], found[:n], AX.X, ALU.add)
                    dve.wait_ge(exp_done, i + 1)
                    link(nc.vector.tensor_reduce(total[:n], shifted[:n], AX.X, ALU.add))
                    link(nc.vector.reciprocal(total[:n], total[:n]))
                    gate = rows[:n, 2].rearrange("p (h k) -> p h k", h=PEER_HEADS)
                    link(nc.vector.tensor_tensor(gate, shifted[:n], total[:n].unsqueeze(2).to_broadcast([n, PEER_HEADS, TOPK]), ALU.mult))
                    dve.sem_inc(rows_ready, 1)
                    assert done[0] == STEPS

                with dve.Fori(0, TILES - 1) as i:
                    tile(i, P)
                tile(TILES - 1, SAMPLE)


def gate_phase(nc, t, routes):
    with phase(nc, "gates") as (sb, ps, sem, blk):
        iota = sb("iota", [P, P])
        picked = sb("picked", [P, 2, 3, GG])
        row_hot, col_hot = sb("row_hot", [P, 2, GG, P]), sb("col_hot", [P, 2, GG, P])
        tile_buf = sb("tile_buf", [P, 2, KEYS, GT])
        product = ps("product", [P, 2, GG, P])
        iota_landed, stored = sem("iota_landed"), [sem("stored0"), sem("stored1")]
        picked_ready, hot_ready, multiplied, copied = sem("picked_ready"), sem("hot_ready"), sem("multiplied"), sem("copied")
        groups = GT // GG
        with blk as block:
            @block.sync
            def _(sp):
                sp.dma_start(iota[:], t["iota"]).then_inc(iota_landed, 16)
                credit(sp, stored[0], 16)
                credit(sp, stored[1], 16)

                def store(tile, u):
                    sp.wait_ge(copied, groups * (tile + 1) + 2)
                    sp.dma_start(t["gates"][:, bass.ds(tile, 1)].rearrange("p a c l -> p (a c l)"),
                                 tile_buf[:, u].rearrange("p c l -> p (c l)")).then_inc(stored[u], 16)

                with sp.Fori(0, GTILES // 2) as i:
                    store(2 * i, 0)
                    store(2 * i + 1, 1)
                store(GTILES - 1, 0)
                sp.wait_ge(stored[0], 16 * (GTILES // 2 + 1) + 16)
                sp.wait_ge(stored[1], 16 * (GTILES // 2) + 16)

            @block.vector
            def _(dve):
                dve.wait_ge(iota_landed, 16)
                credit(dve, multiplied, 2)
                credit(dve, hot_ready, 2)
                with dve.Fori(0, TOK // GG // 2) as g:
                    for u in range(2):
                        dve.wait_ge(hot_ready, 2 * g + u + 1)
                        nc.vector.tensor_copy(picked[:, u], routes[:, :, bass.ds(2 * GG * g + GG * u, GG)]).then_inc(picked_ready, 1)
                    for u in range(2):
                        dve.wait_ge(picked_ready, 2 * g + u + 1)
                        dve.wait_ge(multiplied, 2 * g + u + 1)
                        for a in range(GG):
                            nc.vector.tensor_scalar(row_hot[:, u, a], iota[:], picked[:, u, 0, a:a + 1], None, ALU.is_equal)
                            last = nc.vector.tensor_scalar(col_hot[:, u, a], iota[:], picked[:, u, 1, a:a + 1],
                                                           picked[:, u, 2, a:a + 1], ALU.is_equal, ALU.mult)
                        last.then_inc(hot_ready, 1)

            @block.tensor
            def _(pe):
                credit(pe, copied, 2)
                with pe.Fori(0, TOK // GG // 2) as g:
                    for u in range(2):
                        pe.wait_ge(hot_ready, 2 * g + u + 3)
                        pe.wait_ge(copied, 2 * g + u + 1)
                        for a in range(GG):
                            last = nc.tensor.matmul(product[:, u, a], row_hot[:, u, a], col_hot[:, u, a], start=True, stop=True)
                        last.then_inc(multiplied, 1)

            @block.scalar
            def _(act):
                def tile(i, u, after):
                    act.wait_ge(stored[u], 16 * i + 16)
                    with act.Fori(0, groups // 2) as g:
                        for s in range(2):
                            act.wait_ge(multiplied, after + 2 * g + s + 3)
                            to = tile_buf[:, u, :, bass.ds((2 * g + s) * GG, GG)].rearrange("p c l -> p l c")
                            nc.scalar.activation(to, product[:, s], ACT.Copy).then_inc(copied, 1)

                with act.Fori(0, GTILES // 2) as i:
                    tile(i, 0, i * 2 * groups)
                    tile(i, 1, i * 2 * groups + groups)
                tile(GTILES // 2, 0, (GTILES - 1) * groups)


def experts_phase(nc, t, x_hi, x_lo, acc):
    DT, CH = D // P, 4
    with phase(nc, "experts") as (sb, ps, sem, blk):
        u_raw, v_raw = sb("u_raw", [P, DC, P]), sb("v_raw", [P, D])
        u_hi, u_lo = sb("u_hi", [P, KE, DC, P], F32R), sb("u_lo", [P, KE, DC, P], F32R)
        v_hi, v_lo = sb("v_hi", [P, 2, KE, D], F32R), sb("v_lo", [P, 2, KE, D], F32R)
        gate = sb("gate", [P, KE, TOK])
        coef = sb("coef", [P, KE, TOK])
        c_hi, c_lo = sb("c_hi", [P, 2, KE, TOK], F32R), sb("c_lo", [P, 2, KE, TOK], F32R)
        hidden = ps("hidden", [P, 3, 512])
        mixed = ps("mixed", [P, CH, 512])
        h_landed = sem("h_landed")
        u_landed, v_landed, g_landed = sem("u_landed"), sem("v_landed"), [sem("g_landed0"), sem("g_landed1")]
        u_split, u_ready, v_split, v_ready = sem("u_split"), sem("u_ready"), sem("v_split"), sem("v_ready")
        hidden_ready, activated, gated, c_split, c_ready = (
            sem("hidden_ready"), sem("activated"), sem("gated"), sem("c_split"), sem("c_ready"))
        mixed_ready, added = sem("mixed_ready"), sem("added")

        def over_blocks(engine, step):
            step(0, 0, True, False, True)
            with engine.Fori(0, BLOCKS // 2 - 1) as i:
                step(2 * i + 1, 1, True, True, True)
                step(2 * i + 2, 0, True, True, True)
            step(BLOCKS - 1, 1, True, True, False)
            step(BLOCKS, 0, False, True, False)

        with blk as block:
            @block.sync
            def _(sp):
                sp.dma_start(acc[:], t["h"]).then_inc(h_landed, 16)
                credit(sp, u_ready, 1)
                credit(sp, v_ready, 1)
                credit(sp, gated, 2)

                def load_u(tile):
                    sp.wait_ge(u_ready, tile + 1)
                    sp.dma_start(u_raw[:], t["peer_u"][bass.ds(tile, 1)].rearrange("a p k m -> p (a k) m")).then_inc(u_landed, 16)

                def step(b, par, has_u, has_v, more):
                    if not has_u:
                        return
                    for a in range(KE):
                        tile = KE * b + a
                        sp.wait_ge(gated, tile + 1)
                        sp.dma_start(gate[:, a].rearrange("p (n l) -> p n l", n=GTILES),
                                     t["gates"][:, :, bass.ds(tile, 1), :].rearrange("p n a l -> p n (a l)")).then_inc(g_landed[a], 16)
                        if more:
                            load_u(tile + KE)
                        sp.wait_ge(v_ready, tile + 1)
                        sp.dma_start(v_raw[:], t["peer_v"][bass.ds(tile, 1)].rearrange("a p d -> (a p) d")).then_inc(v_landed, 16)

                load_u(0)
                load_u(1)
                over_blocks(sp, step)

            @block.scalar
            def _(act):
                def split_u(tile, a):
                    act.wait_ge(u_landed, 16 * tile + 16)
                    act.wait_ge(hidden_ready, 3 * tile + 3)
                    nc.scalar.activation(u_hi[:, a], u_raw[:], ACT.Copy).then_inc(u_split, 1)

                def step(b, par, has_u, has_v, more):
                    if not has_u:
                        return
                    for a in range(KE):
                        tile = KE * b + a
                        act.wait_ge(c_ready, tile + 1)
                        for n in range(NBN):
                            act.wait_ge(hidden_ready, 3 * tile + n + 7)
                            nc.scalar.activation(coef[:, a, n * NB:n * NB + NB], hidden[:, n, :NB], ACT.Gelu).then_inc(activated, 1)
                        if more:
                            split_u(tile + KE, a)
                        act.wait_ge(v_landed, 16 * tile + 16)
                        act.wait_ge(mixed_ready, 24 * b + 24)
                        nc.scalar.activation(v_hi[:, par, a], v_raw[:], ACT.Copy).then_inc(v_split, 1)
                        act.wait_ge(gated, tile + 3)
                        nc.scalar.activation(c_hi[:, par, a], coef[:, a], ACT.Copy).then_inc(c_split, 1)

                act.preload_act_table_set("gelu_and_others")
                credit(act, mixed_ready, 48)
                split_u(0, 0)
                split_u(1, 1)
                over_blocks(act, step)

            @block.tensor
            def _(pe):
                def step(b, par, has_u, has_v, more):
                    for a in range(KE if has_u else 0):
                        tile = KE * b + a
                        pe.wait_ge(u_ready, tile + 2)
                        for n in range(NBN):
                            pe.wait_ge(activated, 3 * tile + n + 1)
                            project(nc, hidden[:, n, :NB], u_hi[:, a], u_lo[:, a], x_hi, x_lo, n).then_inc(hidden_ready, 1)
                    if not has_v:
                        return
                    old = 1 - par
                    pe.wait_ge(v_ready, KE * b + 1)
                    pe.wait_ge(c_ready, KE * b + 2)
                    for d in range(DT):
                        cols = slice(d * P, d * P + P)
                        for n in range(NBN):
                            at = NBN * d + n
                            tok = slice(n * NB, n * NB + NB)
                            pe.wait_ge(added, 24 * b + at - 23)
                            out = mixed[:, at % CH, :NB]
                            for a in range(KE):
                                nc.tensor.matmul(out, v_hi[:, old, a, cols], c_hi[:, old, a, tok], start=(a == 0), stop=False)
                                nc.tensor.matmul(out, v_lo[:, old, a, cols], c_hi[:, old, a, tok], start=False, stop=False)
                                last = nc.tensor.matmul(out, v_hi[:, old, a, cols], c_lo[:, old, a, tok], start=False, stop=(a == KE - 1))
                            last.then_inc(mixed_ready, 1)

                credit(pe, hidden_ready, 6)
                credit(pe, activated, 3)
                credit(pe, added, CH)
                over_blocks(pe, step)

            @block.vector
            def _(dve):
                def split_u(tile, a):
                    dve.wait_ge(u_split, tile + 1)
                    nc.vector.tensor_tensor(u_lo[:, a], u_raw[:], u_hi[:, a].bitcast(F32), ALU.subtract).then_inc(u_ready, 1)

                def split_v(tile, par, a):
                    dve.wait_ge(v_split, tile + 1)
                    nc.vector.tensor_tensor(v_lo[:, par, a], v_raw[:], v_hi[:, par, a].bitcast(F32), ALU.subtract).then_inc(v_ready, 1)

                def coefficients(tile, par, a):
                    dve.wait_ge(g_landed[a], (tile - a) * (16 // KE) + 16)
                    dve.wait_ge(activated, 3 * tile + 6)
                    nc.vector.tensor_tensor(coef[:, a], coef[:, a], gate[:, a], ALU.mult).then_inc(gated, 1)

                def split_c(tile, par, a):
                    dve.wait_ge(c_split, tile + 1)
                    nc.vector.tensor_tensor(c_lo[:, par, a], coef[:, a], c_hi[:, par, a].bitcast(F32), ALU.subtract).then_inc(c_ready, 1)

                def add(b, lo, hi):
                    for at in range(lo, hi):
                        d, tok = at // NBN, slice(at % NBN * NB, at % NBN * NB + NB)
                        dve.wait_ge(mixed_ready, 24 * b + at + 25)
                        nc.vector.tensor_tensor(acc[:, d, tok], acc[:, d, tok], mixed[:, at % CH, :NB], ALU.add).then_inc(added, 1)

                def step(b, par, has_u, has_v, more):
                    t0, t1 = KE * b, KE * b + 1
                    if has_u:
                        coefficients(t0, par, 0)
                        if more:
                            split_u(t0 + KE, 0)
                        split_v(t0, par, 0)
                        split_c(t0, par, 0)
                        coefficients(t1, par, 1)
                        if more:
                            split_u(t1 + KE, 1)
                    if has_v:
                        add(b, 0, 4)
                    if has_u:
                        split_v(t1, par, 1)
                        split_c(t1, par, 1)
                    if has_v:
                        add(b, 4, 24)

                credit(dve, c_ready, 2)
                dve.wait_ge(h_landed, 16)
                split_u(0, 0)
                split_u(1, 1)
                over_blocks(dve, step)


def build(nc, t, upto=99):
    with ExitStack() as ctx:
        def sb(n, shape, dt=F32):
            return ctx.enter_context(nc.sbuf_tensor(n, shape, dt))

        ones, ident, causal, masked = sb("ones", [P, P]), sb("ident", [P, P]), sb("causal", [P, P]), sb("masked", [P, P])
        suffix = sb("suffix", [P, P])
        consts = {"ones": ones, "ident": ident, "causal": causal, "masked": masked, "suffix": suffix}
        vectors = sb("vectors", [P, 4 * DC + CONV_TILES * (TAPS + 1)])
        norm1_w, norm2_w, final_w = (vectors[:, DC * a:DC * (a + 1)] for a in range(3))
        ssm_norm_w, d_skip = vectors[:, 3 * DC:3 * DC + 4], vectors[:, 3 * DC + 4:4 * DC]
        conv_wb = vectors[:, 4 * DC:].rearrange("p (c a) -> p c a", a=TAPS + 1)
        head_vec = sb("head_vec", [P, 2, SSM_HEADS])
        dt_raw = sb("dt_raw", [P, TILES, SSM_HEADS])
        const_landed = ctx.enter_context(nc.semaphore("const_landed"))
        with nc.Block() as block:
            @block.sync
            def _(sp):
                for tile, src in ((ones, "ones"), (ident, "ident"), (causal, "causal"), (masked, "masked"),
                                  (suffix, "suffix"), (vectors, "vectors"), (head_vec, "head_vec")):
                    sp.dma_start(tile[:], t[src]).then_inc(const_landed, 16)
                sp.wait_ge(const_landed, 16 * 7)

        with ExitStack() as early:
            x_hi = early.enter_context(nc.sbuf_tensor("x1_hi", [P, DC, TOK], F32R))
            x_lo = early.enter_context(nc.sbuf_tensor("x1_lo", [P, DC, TOK], F32R))
            with nc.sbuf_tensor("x", [P, DC, TOK], F32) as x:
                norm_phase(nc, "norm1", x, norm1_w, consts, hi=x_hi, lo=x_lo, src_dram=t["x"])
            input_projection(nc, consts, x_hi, x_lo, dt_raw, t["w_in"], t["w_dt"], t["proj"])
        if upto <= 1:
            return
        with ExitStack() as middle:
            mixed = middle.enter_context(nc.sbuf_tensor("mixed", [P, DC, TOK], F32))
            ssd_phase(nc, consts, (ssm_norm_w, d_skip, conv_wb), head_vec, dt_raw, t, mixed)
            if upto == 2:
                return dump(nc, mixed[:, :4], t["mixed"][:, :4])
            attention_phase(nc, consts, t, mixed)
            if upto == 3:
                return dump(nc, mixed[:], t["mixed"])
            h = middle.enter_context(nc.sbuf_tensor("h_tile", [P, DC, TOK], F32))
            output_projection(nc, mixed, h, t["w_out"], t["x"], t["h"])
        if upto == 4:
            return
        with ExitStack() as late:
            n_hi = late.enter_context(nc.sbuf_tensor("n_hi", [P, DC, TOK], F32R))
            n_lo = late.enter_context(nc.sbuf_tensor("n_lo", [P, DC, TOK], F32R))
            with nc.sbuf_tensor("h_again", [P, DC, TOK], F32) as h:
                norm_phase(nc, "norm2", h, norm2_w, consts, hi=n_hi, lo=n_lo, src_dram=t["h"])
            with ExitStack() as routing:
                routes = routing.enter_context(nc.sbuf_tensor("routes", [P, 3, TOK], F32))
                with ExitStack() as tops:
                    top_v = tops.enter_context(nc.sbuf_tensor("top_v", [P, TILES, HALVES, TOPK], F32))
                    top_i = tops.enter_context(nc.sbuf_tensor("top_i", [P, TILES, HALVES, TOPK], F32))
                    retrieval_phase(nc, n_hi, n_lo, t["w_q"], t["keys"], top_v, top_i)
                    routing_phase(nc, consts, t, top_v, top_i, routes)
                gate_phase(nc, t, routes)
            if upto == 5:
                return
            acc = late.enter_context(nc.sbuf_tensor("acc", [P, DC, TOK], F32))
            experts_phase(nc, t, n_hi, n_lo, acc)
            with nc.sbuf_tensor("y", [P, DC, TOK], F32) as y:
                norm_phase(nc, "norm3", acc, final_w, consts, out=y, out_dram=t["y"])


_OUT = {
    "proj": [IN_TILES, P, TOK], "y": [P, DC, TOK], "state_prompt": [P, SSM_HEADS * HD],
    "state_sample": [P, SSM_HEADS * HD],
}
_SCRATCH = {"mixed": [P, DC, TOK], "h": [P, DC, TOK], "gates": [P, GTILES, KEYS, GT]}


def dump(nc, tile, dram):
    with nc.semaphore("dumped") as sem, nc.Block() as block:
        @block.sync
        def _(sp):
            sp.dma_start(dram, tile[:]).then_inc(sem, 16)
            sp.wait_ge(sem, 16)


def chunked(w, cols):
    n = w.shape[1] // cols
    return np.ascontiguousarray(w.reshape(DC, P, n, cols).transpose(2, 1, 0, 3))


def per_partition(v):
    return v.reshape(-1, P).T


def lay_out(x_prompt, x_sample, cache_sb_k, cache_sb_v, state_ssm, state_conv,
            norm1_w, w_in, conv_w, conv_b, dt_bias, a_log, d_skip, ssm_norm_w, w_out,
            norm2_w, peer_wq, peer_k1, peer_k2, peer_u, peer_v, final_norm_w):
    x = np.concatenate([x_prompt[0], x_sample[0]], 0)
    w = w_in[0]
    conv = np.concatenate([conv_w[0], conv_b[0][None]], 0)
    k_idx, q_idx = np.arange(P)[:, None], np.arange(P)[None]
    vectors = np.concatenate([
        per_partition(norm1_w[0]), per_partition(norm2_w[0]), per_partition(final_norm_w),
        per_partition(ssm_norm_w[0]), per_partition(np.repeat(d_skip[0], HD)),
        conv.reshape(TAPS + 1, CONV_TILES, P).transpose(2, 1, 0).reshape(P, -1)], 1)
    a = {
        "x": x.T.reshape(DC, P, TOK).transpose(1, 0, 2),
        "w_in": chunked(np.concatenate([w[:, 512:1536], w[:, :512], w[:, 1544:]], 1), P),
        "w_dt": w[:, 1536:1544].reshape(DC, P, SSM_HEADS).transpose(1, 0, 2),
        "vectors": vectors,
        "head_vec": np.broadcast_to(np.stack([dt_bias[0], a_log[0]])[None], (P, 2, SSM_HEADS)),
        "conv_in": state_conv[0, 0].T.reshape(CONV_TILES, P, TAPS - 1).transpose(1, 0, 2),
        "state_in": state_ssm[0, 0].transpose(2, 0, 1).reshape(P, SSM_HEADS * HD),
        "past_k": cache_sb_k[0, 0].reshape(PAST, PAIRS, 2 * HD).transpose(1, 2, 0),
        "past_v": cache_sb_v[0, 0].reshape(PB, P, PAIRS, 2 * HD).transpose(2, 1, 0, 3),
        "w_out": chunked(w_out[0], P),
        "w_q": chunked(peer_wq[0], P),
        "keys": np.stack([peer_k1[0], peer_k2[0]], 1).reshape(HALVES, KEYS, P).transpose(0, 2, 1),
        "peer_u": peer_u[0].reshape(KEYS, KEYS, DC, P).transpose(1, 3, 2, 0),
        "peer_v": peer_v[0].reshape(KEYS, KEYS, D).transpose(1, 0, 2),
        "ones": np.ones((P, P), np.float32),
        "ident": np.eye(P, dtype=np.float32),
        "causal": (k_idx <= q_idx).astype(np.float32),
        "masked": np.where(k_idx <= q_idx, 0.0, MASKED).astype(np.float32),
        "strict": (k_idx < q_idx).astype(np.float32),
        "strict_masked": np.where(k_idx < q_idx, 0.0, MASKED).astype(np.float32),
        "neg_ones": -np.ones((P, P), np.float32),
        "suffix": -(k_idx >= q_idx).astype(np.float32),
        "iota": np.broadcast_to(np.arange(P, dtype=np.float32)[None], (P, P)),
    }
    return {n: np.ascontiguousarray(v) for n, v in a.items()}


def give_back(r):
    proj = r["proj"]

    def rows(tile, lo, hi):
        return proj[tile:tile + 4, :, lo:hi].transpose(2, 0, 1).reshape(1, 1, hi - lo, 8, HD)

    def conv_state(end):
        return proj[:CONV_TILES, :, end - (TAPS - 1):end].transpose(2, 0, 1).reshape(1, 1, TAPS - 1, D)

    def state(s):
        return s.reshape(P, SSM_HEADS, HD).transpose(1, 2, 0)[None, None]

    y = r["y"].transpose(2, 1, 0).reshape(TOK, D)
    out = (y[None, :PROMPT], y[None, PROMPT:], rows(K_TILE, 0, PROMPT), rows(V_TILE, 0, PROMPT),
           state(r["state_prompt"]), conv_state(PROMPT), rows(K_TILE, PROMPT, TOK), rows(V_TILE, PROMPT, TOK),
           state(r["state_sample"]), conv_state(TOK))
    return tuple(np.ascontiguousarray(o) for o in out)


def kernel(**inputs):
    import concourse.bacc as bacc
    from concourse.bass_utils import run_bass_kernel_spmd

    nc = bacc.Bacc("TRN2", target_bir_lowering=False, num_devices=1)
    arrays = lay_out(**{n: np.asarray(v) for n, v in inputs.items()})
    t = {n: nc.dram_tensor(f"in_{n}", a.shape, F32, kind="ExternalInput").ap() for n, a in arrays.items()}
    for n, shape in _OUT.items():
        t[n] = nc.dram_tensor(f"out_{n}", shape, F32, kind="ExternalOutput").ap()
    for n, shape in _SCRATCH.items():
        t[n] = nc.dram_tensor(f"scratch_{n}", shape, F32, kind="Internal").ap()
    build(nc, t)
    r = run_bass_kernel_spmd(nc, [{f"in_{n}": a for n, a in arrays.items()}], core_ids=[0])
    return give_back({n: r.results[0][f"out_{n}"] for n in _OUT})
```

```python
from contextlib import ExitStack, contextmanager

import numpy as np

import concourse.bass as bass
from concourse import mybir

F32 = mybir.dt.float32
F32R = mybir.dt.float32r
BF16 = mybir.dt.bfloat16
U32 = mybir.dt.uint32
ACT = mybir.ActivationFunctionType
ALU = mybir.AluOpType
AX = mybir.AxisListType

P = 128
D = 1024
DC = D // P
PROMPT = 1024
SAMPLE = 32
TOK = PROMPT + SAMPLE
NB = 352
NBN = TOK // NB
EPS = 1e-6

SSM_HEADS = 8
HD = 64
STATE = 128
TAPS = 4
CONV_TILES = 8
Z_TILE, Q_TILE, K_TILE, V_TILE, IN_TILES = 8, 12, 16, 20, 24
CHUNKS = PROMPT // P
S_OFF = PROMPT + TAPS - 1
CONV_W = TOK + 2 * (TAPS - 1)
CONV_OUT = CONV_W - (TAPS - 1)

PAIRS = 4
PAST = 2048
PB = PAST // P
QW = 512

PEER_HEADS = 8
HALVES = 2 * PEER_HEADS
KEYS = 128
TOPK = 16
TILES = 9
LOWEST = -3.0e38
MASKED = -1.0e30
GT = 66
GTILES = TOK // GT
GG = 3
RING = 4

KE = 2
BLOCKS = KEYS // KE
ROUTE_U = 3
GATE_U = 3
EARLY_ROUTE = ROUTE_U * TILES + 1
EARLY = EARLY_ROUTE + GATE_U * GTILES


def credit(engine, sem, n):
    engine.sem_inc(sem, n)


def tokens_of(tile):
    return P if tile < TILES - 1 else SAMPLE


class Sems:

    def __init__(self, nc, ctx, phase):
        self.nc, self.ctx, self.phase = nc, ctx, phase

    def __call__(self, name):
        return self.ctx.enter_context(self.nc.semaphore(f"{self.phase}_{name}"))


@contextmanager
def phase(nc, name):
    with ExitStack() as ctx:
        def sb(n, shape, dt=F32):
            return ctx.enter_context(nc.sbuf_tensor(f"{name}_{n}", shape, dt))

        def ps(n, shape, dt=F32):
            return ctx.enter_context(nc.psum_tensor(f"{name}_{n}", shape, dt))

        block = nc.Block()
        yield sb, ps, Sems(nc, ctx, name), block


def project(nc, out, w_hi, w_lo, x_hi, x_lo, n):
    tok = slice(n * NB, (n + 1) * NB)
    for k in range(DC):
        nc.tensor.matmul(out, w_hi[:, k, :], x_hi[:, k, tok], start=(k == 0), stop=False)
        nc.tensor.matmul(out, w_hi[:, k, :], x_lo[:, k, tok], start=False, stop=False)
        last = nc.tensor.matmul(out, w_lo[:, k, :], x_hi[:, k, tok], start=False, stop=(k == DC - 1))
    return last


def norm_phase(nc, name, src, weight, consts, hi=None, lo=None, src_dram=None, out=None, out_dram=None):
    with phase(nc, name) as (sb, ps, sem, blk):
        squares = sb("squares", [P, 2, TOK])
        rstd = sb("rstd", [P, TOK])
        scaled = sb("scaled", [P, 2, TOK])
        total = ps("total", [P, NBN, 512])
        split = hi is not None
        squared, summed, scaled_ready = sem("squared"), sem("summed"), sem("scaled")
        rstd_step = sem("rstd_step")
        if src_dram is not None:
            landed = sem("landed")
        if split:
            hi_ready, lo_ready = sem("hi"), sem("lo")
        else:
            stored = sem("stored")
        with blk as block:
            @block.sync
            def _(sp):
                if src_dram is not None:
                    sp.dma_start(src[:], src_dram).then_inc(landed, 16)
                if not split:
                    sp.wait_ge(scaled_ready, DC)
                    sp.dma_start(out_dram, out[:]).then_inc(stored, 16)
                    sp.wait_ge(stored, 16)

            @block.scalar
            def _(act):
                if src_dram is not None:
                    act.wait_ge(landed, 16)
                for k in range(DC):
                    if k >= 2:
                        act.wait_ge(summed, k - 1)
                    nc.scalar.activation(squares[:, k % 2, :], src[:, k, :], ACT.Square).then_inc(squared, 1)
                act.wait_ge(rstd_step, 1)
                nc.scalar.activation(rstd[:], rstd[:], ACT.Sqrt).then_inc(rstd_step, 1)
                if split:
                    for k in range(DC):
                        act.wait_ge(scaled_ready, k + 1)
                        nc.scalar.activation(hi[:, k, :], scaled[:, k % 2, :], ACT.Copy).then_inc(hi_ready, 1)

            @block.tensor
            def _(pe):
                for k in range(DC):
                    pe.wait_ge(squared, k + 1)
                    for n in range(NBN):
                        last = nc.tensor.matmul(total[:, n, :NB], consts["ones"][:], squares[:, k % 2, n * NB:(n + 1) * NB],
                                                start=(k == 0), stop=(k == DC - 1))
                    last.then_inc(summed, 1)

            @block.vector
            def _(dve):
                dve.wait_ge(summed, DC)
                nc.vector.tensor_scalar(rstd[:].rearrange("p (n t) -> p n t", n=NBN), total[:, :, :NB],
                                        1.0 / D, EPS, ALU.mult, ALU.add).then_inc(rstd_step, 1)
                dve.wait_ge(rstd_step, 2)
                nc.vector.reciprocal(rstd[:], rstd[:]).then_inc(rstd_step, 1)
                dve.wait_ge(rstd_step, 3)

                def split_low(k):
                    dve.wait_ge(hi_ready, k + 1)
                    nc.vector.tensor_tensor(lo[:, k, :], scaled[:, k % 2, :], hi[:, k, :].bitcast(F32),
                                            ALU.subtract).then_inc(lo_ready, 1)

                for k in range(DC):
                    if split and k >= 2:
                        split_low(k - 2)
                        dve.wait_ge(lo_ready, k - 1)
                    to = scaled[:, k % 2, :] if split else out[:, k, :]
                    nc.vector.scalar_tensor_tensor(to, src[:, k, :], weight[:, k:k + 1], rstd[:],
                                                   ALU.mult, ALU.mult).then_inc(scaled_ready, 1)
                if split:
                    split_low(DC - 2)
                    split_low(DC - 1)


def input_projection(nc, consts, x_hi, x_lo, dt_raw, w_in, w_dt, proj):
    with phase(nc, "inproj") as (sb, ps, sem, blk):
        w_raw = sb("w_raw", [P, 2, DC, P])
        w_hi = sb("w_hi", [P, 2, DC, P], F32R)
        w_lo = sb("w_lo", [P, 2, DC, P], F32R)
        wdt_raw = sb("wdt_raw", [P, DC, SSM_HEADS])
        wdt_hi = sb("wdt_hi", [P, DC, SSM_HEADS], F32R)
        wdt_lo = sb("wdt_lo", [P, DC, SSM_HEADS], F32R)
        result = sb("result", [P, 2, TOK])
        acc = ps("acc", [P, 2, 3, 512])
        dt_acc = ps("dt_acc", [P, TILES, SSM_HEADS])
        w_landed = [sem("w_landed0"), sem("w_landed1")]
        hi_ready, lo_ready = sem("hi_ready"), sem("lo_ready")
        projected, acc_free = sem("projected"), sem("acc_free")
        stored = [sem("stored0"), sem("stored1")]
        dt_landed, dt_split, dt_done = sem("dt_landed"), sem("dt_split"), sem("dt_done")
        pairs = IN_TILES // 2
        with blk as block:
            @block.sync
            def _(sp):
                sp.dma_start(wdt_raw[:], w_dt).then_inc(dt_landed, 16)
                credit(sp, lo_ready, 2)
                with sp.Fori(0, pairs) as i:
                    for u in range(2):
                        sp.wait_ge(lo_ready, 2 * i + u + 1)
                        sp.dma_start(w_raw[:, u], w_in[bass.ds(2 * i + u, 1)]
                                     .rearrange("a p k m -> p (a k) m")).then_inc(w_landed[u], 16)

            @block.scalar
            def _(act):
                act.wait_ge(dt_landed, 16)
                nc.scalar.activation(wdt_hi[:], wdt_raw[:], ACT.Copy).then_inc(dt_split, 1)
                credit(act, stored[0], 16)
                credit(act, stored[1], 16)

                def split_high(i, u):
                    act.wait_ge(w_landed[u], 16 * i + 16)
                    act.wait_ge(projected, 6 * i + 3 * u + 3)
                    nc.scalar.activation(w_hi[:, u], w_raw[:, u], ACT.Copy).then_inc(hi_ready, 1)

                def evacuate(i, u):
                    act.wait_ge(stored[u], 16 * i + 16)
                    for n in range(NBN):
                        act.wait_ge(projected, 6 * i + 3 * u + n + 7)
                        nc.scalar.activation(result[:, u, n * NB:(n + 1) * NB], acc[:, u, n, :NB],
                                             ACT.Copy).then_inc(acc_free, 1)
                    act.wait_ge(acc_free, 6 * i + 3 * u + 9)
                    act.dma_start(proj[bass.ds(2 * i + u, 1)].rearrange("a p t -> (a p) t"),
                                  result[:, u]).then_inc(stored[u], 16)

                split_high(0, 0)
                with act.Fori(0, pairs - 1) as i:
                    split_high(i, 1)
                    evacuate(i, 0)
                    split_high(i + 1, 0)
                    evacuate(i, 1)
                split_high(pairs - 1, 1)
                evacuate(pairs - 1, 0)
                evacuate(pairs - 1, 1)
                for u in range(2):
                    act.wait_ge(stored[u], 16 * pairs + 16)

            @block.vector
            def _(dve):
                dve.wait_ge(dt_split, 1)
                nc.vector.tensor_tensor(wdt_lo[:], wdt_raw[:], wdt_hi[:].bitcast(F32), ALU.subtract).then_inc(dt_split, 1)
                nc.vector.memset(dt_raw[:], 0.0).then_inc(dt_split, 1)
                with dve.Fori(0, pairs) as i:
                    for u in range(2):
                        dve.wait_ge(hi_ready, 2 * i + u + 1)
                        nc.vector.tensor_tensor(w_lo[:, u], w_raw[:, u], w_hi[:, u].bitcast(F32),
                                                ALU.subtract).then_inc(lo_ready, 1)
                dve.wait_ge(dt_done, 1)
                dve.wait_ge(dt_split, 3)
                nc.vector.tensor_copy(dt_raw[:, :TILES - 1], dt_acc[:, :TILES - 1])
                nc.vector.tensor_copy(dt_raw[:SAMPLE, TILES - 1], dt_acc[:SAMPLE, TILES - 1])

            @block.tensor
            def _(pe):
                credit(pe, acc_free, 6)
                credit(pe, projected, 6)
                with pe.Fori(0, pairs) as i:
                    for u in range(2):
                        pe.wait_ge(lo_ready, 2 * i + u + 3)
                        for n in range(NBN):
                            pe.wait_ge(acc_free, 6 * i + 3 * u + n + 1)
                            last = project(nc, acc[:, u, n, :NB], w_hi[:, u], w_lo[:, u], x_hi, x_lo, n)
                            last.then_inc(projected, 1)
                pe.wait_ge(dt_split, 3)
                for t in range(TILES):
                    tok = slice(t * P, t * P + tokens_of(t))
                    out = dt_acc[:tokens_of(t), t, :]
                    for k in range(DC):
                        nc.tensor.matmul(out, x_hi[:, k, tok], wdt_hi[:, k, :], start=(k == 0), stop=False)
                        nc.tensor.matmul(out, x_hi[:, k, tok], wdt_lo[:, k, :], start=False, stop=False)
                        last = nc.tensor.matmul(out, x_lo[:, k, tok], wdt_hi[:, k, :], start=False, stop=(k == DC - 1))
                last.then_inc(dt_done, 1)


def ssd_phase(nc, consts, vecs, head_vec, dt_raw, t, mixed):
    ssm_norm_w, d_skip, conv_wb = vecs
    XT, BT, CT = 4, 2, 2
    CW = SSM_HEADS * TILES
    with phase(nc, "ssd") as (sb, ps, sem, blk):
        window = sb("window", [P, CONV_TILES, CONV_W])
        conv = sb("conv", [P, CONV_TILES, CONV_OUT])
        gate = sb("gate", [P, XT, TOK])
        state = sb("state", [P, 2, SSM_HEADS, HD])
        stage = sb("stage", [P, XT + BT, P])
        dta_stage = sb("dta_stage", [P, SSM_HEADS])
        dt, dta, tmp, acum, to_end, decay, dt_end = (sb(n, [P, CW]) for n in (
            "dt", "dta", "tmp", "acum", "to_end", "decay", "dt_end"))
        exp_row = sb("exp_row", [P, SSM_HEADS, P])
        seg = sb("seg", [P, SSM_HEADS, P])
        c_scaled = sb("c_scaled", [P, SSM_HEADS, P])
        xdt = sb("xdt", [P, SSM_HEADS, HD])
        x_end = sb("x_end", [P, SSM_HEADS, HD])
        b_rows = sb("b_rows", [P, BT, P])
        rows_ps = ps("rows_ps", [P, XT + BT, P])
        acum_ps = ps("acum_ps", [P, SSM_HEADS, P])
        score_ps = ps("score_ps", [P, BT, 256])
        y_ps = ps("y_ps", [P, XT, P])
        state_ps = ps("state_ps", [P, SSM_HEADS, HD])
        small_ps = ps("small_ps", [P, 2, 256])
        landed, z_landed, cleared = sem("landed"), sem("z_landed"), sem("cleared")
        convolved, silu_done = sem("convolved"), sem("silu_done")
        dt_step, dt_act, dt_pe = sem("dt_step"), sem("dt_act"), sem("dt_pe")
        staged, transposed, acum_ready, scored = sem("staged"), sem("transposed"), sem("acum_ready"), sem("scored")
        exp_row_done, seg_ready, seg_exp, weighted = sem("exp_row_done"), sem("seg_ready"), sem("seg_exp"), sem("weighted")
        x_ready, c_ready, b_ready = sem("x_ready"), sem("c_ready"), sem("b_ready")
        y_done, state_done, y_out, decayed, state_new = (
            sem("y_done"), sem("state_done"), sem("y_out"), sem("decayed"), sem("state_new"))
        gated, squared, grouped, mean_ready, root_ready, rstd_ready = (
            sem("gated"), sem("squared"), sem("grouped"), sem("mean"), sem("root"), sem("rstd"))
        stored = sem("stored")

        def group_out(g, n):
            flat = [acum_ps[:, 0:4], acum_ps[:, 4:8], rows_ps[:, 0:4], y_ps[:], state_ps[:], score_ps[:]][3 * g + n]
            return flat.rearrange("p a b -> p (a b)")[:, :NB]

        def columns(c):
            return (bass.ds(c * P, P), P) if c is not None else (slice(S_OFF, S_OFF + SAMPLE), SAMPLE)

        with blk as block:
            @block.sync
            def _(sp):
                src = t["proj"][:CONV_TILES].rearrange("c p t -> p c t")
                sp.dma_start(window[:, :, TAPS - 1:TAPS - 1 + PROMPT], src[:, :, :PROMPT]).then_inc(landed, 16)
                sp.dma_start(window[:, :, S_OFF:S_OFF + TAPS - 1], t["conv_in"]).then_inc(landed, 16)
                sp.dma_start(window[:, :, S_OFF + TAPS - 1:], src[:, :, PROMPT:]).then_inc(landed, 16)
                sp.dma_start(state[:, 1].rearrange("p h d -> p (h d)"), t["state_in"]).then_inc(landed, 16)
                sp.dma_start(gate[:], t["proj"][Z_TILE:Z_TILE + XT].rearrange("c p t -> p c t")).then_inc(z_landed, 16)
                sp.wait_ge(state_new, CHUNKS + 1)
                sp.dma_start(t["state_prompt"], state[:, 0].rearrange("p h d -> p (h d)")).then_inc(stored, 16)
                sp.wait_ge(state_new, CHUNKS + 2)
                sp.dma_start(t["state_sample"], state[:, 1].rearrange("p h d -> p (h d)")).then_inc(stored, 16)
                sp.wait_ge(stored, 32)

            @block.gpsimd
            def _(pool):
                nc.gpsimd.memset(window[:, :, :TAPS - 1], 0.0).then_inc(cleared, 1)
                nc.gpsimd.memset(state[:, 0], 0.0).then_inc(cleared, 1)
                pool.wait_ge(silu_done, CONV_TILES)
                pool.wait_ge(dt_step, 5)
                credit(pool, acum_ready, 1)
                credit(pool, transposed, 1)
                credit(pool, scored, 1)

                def stage_chunk(c, i):
                    cols, n = columns(c)
                    pool.wait_ge(transposed, i + 1)
                    pool.wait_ge(scored, i + 1)
                    pool.wait_ge(acum_ready, i + 1)
                    nc.gpsimd.tensor_copy(stage[:, :, :n], conv[:, :XT + BT, cols]).then_inc(staged, 1)
                    h = bass.ds(i * SSM_HEADS, SSM_HEADS)
                    nc.gpsimd.tensor_copy(dta_stage[:], dta[:, h]).then_inc(staged, 1)

                with pool.Fori(0, CHUNKS) as c:
                    stage_chunk(c, c)
                stage_chunk(None, CHUNKS)

            @block.scalar
            def _(act):
                act.preload_act_table_set("natural_log_exp_and_others")
                act.wait_ge(dt_step, 2)
                nc.scalar.activation(tmp[:], tmp[:], ACT.Exp).then_inc(dt_act, 1)
                act.wait_ge(dt_act, 1)
                nc.scalar.activation(tmp[:], tmp[:], ACT.Ln, bias=1.0).then_inc(dt_act, 1)
                nc.scalar.activation(head_vec[:, 1], head_vec[:, 1], ACT.Exp).then_inc(dt_act, 1)
                act.wait_ge(dt_step, 7)
                nc.scalar.activation(to_end[:], to_end[:], ACT.Exp).then_inc(dt_act, 1)
                nc.scalar.activation(decay[:], small_ps[:, 1, :CW], ACT.Exp).then_inc(dt_act, 1)
                for c in range(CONV_TILES):
                    act.wait_ge(convolved, TAPS * CONV_TILES - CONV_TILES + c + 1)
                    nc.scalar.activation(conv[:, c, :], conv[:, c, :], ACT.Silu).then_inc(silu_done, 1)
                act.wait_ge(z_landed, 16)
                nc.scalar.activation(gate[:], gate[:], ACT.Silu).then_inc(silu_done, 1)
                act.preload_act_table_set("exp_and_others")
                credit(act, c_ready, 1)
                credit(act, y_done, 1)
                credit(act, state_done, 1)

                def chunk(c, i):
                    _, n = columns(c)
                    act.wait_ge(c_ready, i + 1)
                    act.wait_ge(acum_ready, i + 2)
                    nc.scalar.activation(exp_row[:, :, :n], acum_ps[:, :, :n], ACT.Exp).then_inc(exp_row_done, 1)
                    act.wait_ge(seg_ready, i * SSM_HEADS + SSM_HEADS)
                    nc.scalar.activation(seg[:n, :, :n], seg[:n, :, :n], ACT.Exp).then_inc(seg_exp, 1)
                    act.wait_ge(transposed, i + 2)
                    act.wait_ge(state_done, i + 1)
                    nc.scalar.activation(b_rows[:n], rows_ps[:n, XT:], ACT.Copy).then_inc(b_ready, 1)

                with act.Fori(0, CHUNKS) as c:
                    chunk(c, c)
                chunk(None, CHUNKS)
                for j in range(XT):
                    act.wait_ge(gated, j + 1)
                    nc.scalar.activation(conv[:, j, :TOK], mixed[:, j, :], ACT.Square).then_inc(squared, 1)
                act.wait_ge(mean_ready, 2)
                nc.scalar.activation(gate[:, :2], gate[:, :2], ACT.Sqrt).then_inc(root_ready, 1)

            @block.tensor
            def _(pe):
                pe.wait_ge(dt_step, 5)
                for a, lhs in enumerate(("causal", "ones")):
                    last = nc.tensor.matmul(small_ps[:, a, :CW], consts[lhs][:], dta[:], start=True, stop=True)
                last.then_inc(dt_pe, 1)
                pe.wait_ge(cleared, 2)
                pe.wait_ge(landed, 64)
                credit(pe, exp_row_done, 1)
                credit(pe, seg_exp, 1)
                credit(pe, b_ready, 1)
                credit(pe, x_ready, 2)
                credit(pe, weighted, 2)
                credit(pe, y_out, XT)
                credit(pe, state_new, 1)

                def chunk(c, i):
                    cols, n = columns(c)
                    s = 0 if c is not None else 1
                    pe.wait_ge(staged, 2 * i + 2)
                    pe.wait_ge(exp_row_done, i + 1)
                    pe.wait_ge(seg_exp, i + 1)
                    for h in range(SSM_HEADS):
                        last = nc.tensor.matmul(acum_ps[:, h, :n], dta_stage[:n, h:h + 1].to_broadcast([n, P]),
                                                consts["causal"][:n, :n], start=True, stop=True)
                    last.then_inc(acum_ready, 1)
                    pe.wait_ge(weighted, 2 * i + 2)
                    for g in range(BT):
                        last = nc.tensor.matmul(score_ps[:n, g, :n], stage[:, XT + g, :n], conv[:, XT + BT + g, cols],
                                                start=True, stop=True)
                    last.then_inc(scored, 1)
                    pe.wait_ge(b_ready, i + 1)
                    pe.wait_ge(x_ready, 2 * i + 2)
                    for j in range(XT + BT):
                        last = nc.tensor.transpose(rows_ps[:n, j, :], stage[:, j, :n], consts["ident"][:])
                    last.then_inc(transposed, 1)
                    pe.wait_ge(x_ready, 2 * i + 4)
                    pe.wait_ge(b_ready, i + 2)
                    pe.wait_ge(state_new, i + 1)
                    for g in range(BT):
                        last = nc.tensor.matmul(state_ps[:, 4 * g:4 * g + 4], b_rows[:n, g], x_end[:n, 4 * g:4 * g + 4],
                                                start=True, stop=True)
                    last.then_inc(state_done, 1)
                    pe.wait_ge(weighted, 2 * i + 4)
                    pe.wait_ge(c_ready, i + 2)
                    pe.wait_ge(y_out, XT * i + XT)
                    for h in range(SSM_HEADS):
                        out = y_ps[HD * (h % 2):HD * (h % 2) + HD, h // 2, :n]
                        nc.tensor.matmul(out, xdt[:n, h], seg[:n, h, :n], start=True, stop=False)
                        last = nc.tensor.matmul(out, state[:, s, h], c_scaled[:, h, :n], start=False, stop=True)
                    last.then_inc(y_done, 1)

                with pe.Fori(0, CHUNKS) as c:
                    chunk(c, c)
                chunk(None, CHUNKS)
                for g in range(2):
                    for n in range(NBN):
                        out = group_out(g, n)
                        for j in (2 * g, 2 * g + 1):
                            pe.wait_ge(squared, j + 1)
                            last = nc.tensor.matmul(out, consts["ones"][:], conv[:, j, n * NB:(n + 1) * NB],
                                                    start=(j == 2 * g), stop=(j == 2 * g + 1))
                    last.then_inc(grouped, 1)

            @block.vector
            def _(dve):
                dt_bias = head_vec[:, 0:1].to_broadcast([P, TILES, SSM_HEADS])
                neg_a = head_vec[:, 1:2].to_broadcast([P, TILES, SSM_HEADS])
                flat = dt[:].rearrange("p (c h) -> p c h", h=SSM_HEADS)
                nc.vector.tensor_tensor(flat, dt_raw[:], dt_bias, ALU.add).then_inc(dt_step, 1)
                dve.wait_ge(dt_step, 1)
                nc.vector.scalar_tensor_tensor(tmp[:], dt[:], -1.0, dt[:], ALU.mult, ALU.min).then_inc(dt_step, 1)
                dve.wait_ge(dt_act, 3)
                nc.vector.scalar_tensor_tensor(dt[:], dt[:], 0.0, tmp[:], ALU.max, ALU.add).then_inc(dt_step, 1)
                dve.wait_ge(dt_step, 3)
                nc.vector.scalar_tensor_tensor(dta[:].rearrange("p (c h) -> p c h", h=SSM_HEADS), flat, -1.0, neg_a,
                                               ALU.mult, ALU.mult).then_inc(dt_step, 1)
                dve.wait_ge(dt_step, 4)
                nc.vector.memset(dta[SAMPLE:SAMPLE * 2, CW - SSM_HEADS:], 0.0)
                nc.vector.memset(dta[HD:, CW - SSM_HEADS:], 0.0).then_inc(dt_step, 1)
                dve.wait_ge(dt_pe, 1)
                nc.vector.tensor_copy(acum[:], small_ps[:, 0, :CW]).then_inc(dt_step, 1)
                dve.wait_ge(dt_step, 6)
                nc.vector.scalar_tensor_tensor(to_end[:], small_ps[:, 1, :CW], 1.0, acum[:],
                                               ALU.mult, ALU.subtract).then_inc(dt_step, 1)
                dve.wait_ge(dt_act, 5)
                nc.vector.tensor_tensor(dt_end[:], dt[:], to_end[:], ALU.mult).then_inc(dt_step, 1)
                dve.wait_ge(landed, 64)
                dve.wait_ge(cleared, 2)
                for j in range(TAPS):
                    for c in range(CONV_TILES):
                        if j:
                            dve.wait_ge(convolved, CONV_TILES * (j - 1) + c + 1)
                            nc.vector.scalar_tensor_tensor(conv[:, c, :], window[:, c, j:j + CONV_OUT], conv_wb[:, c, j:j + 1],
                                                           conv[:, c, :], ALU.mult, ALU.add).then_inc(convolved, 1)
                        else:
                            nc.vector.tensor_scalar(conv[:, c, :], window[:, c, :CONV_OUT], conv_wb[:, c, 0:1],
                                                    conv_wb[:, c, TAPS:], ALU.mult, ALU.add).then_inc(convolved, 1)
                dve.wait_ge(silu_done, CONV_TILES)
                dve.wait_ge(dt_step, 8)

                def chunk(c, i):
                    cols, n = columns(c)
                    s = 0 if c is not None else 1
                    per_head = bass.ds(i * SSM_HEADS, SSM_HEADS)
                    dve.wait_ge(exp_row_done, i + 2)
                    dve.wait_ge(y_done, i + 1)
                    for h in range(SSM_HEADS):
                        nc.vector.scalar_tensor_tensor(seg[:n, h, :n], acum_ps[:n, h, :n],
                                                       acum[:n, bass.ds(i * SSM_HEADS + h, 1)],
                                                       consts["masked"][:n, :n], ALU.subtract, ALU.add).then_inc(seg_ready, 1)
                    for g in range(BT):
                        heads = slice(4 * g, 4 * g + 4)
                        c_rows = conv[:, XT + BT + g:XT + BT + g + 1, cols].to_broadcast([P, 4, n])
                        last = nc.vector.tensor_tensor(c_scaled[:, heads, :n], exp_row[:, heads, :n], c_rows, ALU.mult)
                    last.then_inc(c_ready, 1)
                    dve.wait_ge(transposed, i + 2)
                    dve.wait_ge(state_done, i + 1)
                    x_rows = rows_ps[:n, :XT].rearrange("p j (a d) -> p (j a) d", a=2)
                    for to, by in ((xdt, dt), (x_end, dt_end)):
                        scale = by[:n, per_head].unsqueeze(2).to_broadcast([n, SSM_HEADS, HD])
                        nc.vector.tensor_tensor(to[:n], x_rows, scale, ALU.mult).then_inc(x_ready, 1)
                    dve.wait_ge(seg_exp, i + 2)
                    dve.wait_ge(scored, i + 2)
                    for g in range(BT):
                        heads = slice(4 * g, 4 * g + 4)
                        nc.vector.tensor_tensor(seg[:n, heads, :n], seg[:n, heads, :n],
                                                score_ps[:n, g:g + 1, :n].to_broadcast([n, 4, n]),
                                                ALU.mult).then_inc(weighted, 1)
                    dve.wait_ge(y_done, i + 2)
                    for j in range(XT):
                        nc.vector.scalar_tensor_tensor(mixed[:, j, bass.ds(i * P, n)], conv[:, j, cols], d_skip[:, j:j + 1],
                                                       y_ps[:, j, :n], ALU.mult, ALU.add).then_inc(y_out, 1)
                    scale = decay[:, per_head].unsqueeze(2).to_broadcast([P, SSM_HEADS, HD])
                    nc.vector.tensor_tensor(state[:, s], state[:, s], scale, ALU.mult).then_inc(decayed, 1)
                    dve.wait_ge(decayed, i + 1)
                    nc.vector.tensor_tensor(state[:, s], state[:, s], state_ps[:], ALU.add).then_inc(state_new, 1)
                    dve.wait_ge(state_new, i + 2)

                with dve.Fori(0, CHUNKS) as c:
                    chunk(c, c)
                chunk(None, CHUNKS)
                dve.wait_ge(silu_done, CONV_TILES + 1)
                dve.wait_ge(y_out, XT * (TILES + 1))
                for j in range(XT):
                    nc.vector.tensor_tensor(mixed[:, j, :], mixed[:, j, :], gate[:, j, :], ALU.mult).then_inc(gated, 1)
                dve.wait_ge(gated, XT)
                for g in range(2):
                    dve.wait_ge(grouped, g + 1)
                    for n in range(NBN):
                        last = nc.vector.tensor_scalar(gate[:, g, n * NB:(n + 1) * NB], group_out(g, n),
                                                       2.0 / (SSM_HEADS * HD), EPS, ALU.mult, ALU.add)
                    last.then_inc(mean_ready, 1)
                dve.wait_ge(root_ready, 1)
                nc.vector.reciprocal(gate[:, :2], gate[:, :2]).then_inc(rstd_ready, 1)
                dve.wait_ge(rstd_ready, 1)
                for j in range(XT):
                    nc.vector.scalar_tensor_tensor(mixed[:, j, :], mixed[:, j, :], ssm_norm_w[:, j:j + 1], gate[:, j // 2, :],
                                                   ALU.mult, ALU.mult)


class Job:

    def __init__(self, kind, n, h=0, qb=0, j=0, b0=0):
        self.kind, self.n, self.h, self.qb, self.j, self.b0 = kind, n, h, qb, j, b0
        self.slot = n % 4
        if kind == "prompt":
            self.step = 4 * qb + 3 - j
            self.diag = self.step < 4
            self.lo = max(0, j - 4 * qb) * P
            self.hi, self.keys = QW, P
            self.t_lo = self.lo + P if self.diag else self.lo
        else:
            self.lo, self.hi = 0, 2 * SAMPLE if kind == "new" else QW
            self.keys = SAMPLE if kind == "new" else P

    @property
    def cols(self):
        return slice(self.lo, self.hi)


def attention_jobs():
    jobs = []
    for qb in range(PROMPT // QW):
        for j in range(4 * qb + 3, -1, -1):
            for h in range(2):
                jobs.append(Job("prompt", len(jobs), h, qb, j))
    jobs.append(Job("new", len(jobs)))
    jobs.append(Job("past", len(jobs), b0=8))
    jobs.append(Job("past", len(jobs), b0=0))
    return jobs


def attention_phase(nc, consts, t, mixed):
    jobs = attention_jobs()
    JN = len(jobs)
    SL = slice(PROMPT, TOK)
    with phase(nc, "sb") as (sb, ps, sem, blk):
        q, k, v = (sb(n, [P, 2, TOK]) for n in "qkv")
        past_k = sb("past_k", [P, 2, PAST])
        past_v = sb("past_v", [P, 2, PB, P])
        q_diag = sb("q_diag", [P, 2, 2 * SAMPLE])
        v_rows = sb("v_rows", [P, TILES, P])
        e, softplus, weight = sb("e", [P, 4, QW]), sb("softplus", [P, 4, QW]), sb("weight", [P, 4, QW])
        later = sb("later", [P, 2, 2, QW])
        s_later = sb("s_later", [P, PB, 2 * SAMPLE])
        strict, strict_masked, neg_ones = sb("strict", [P, P]), sb("strict_masked", [P, P]), sb("neg_ones", [P, P])
        z = ps("z", [P, 4, QW])
        o = ps("o", [P, 2, QW])
        spare = ps("spare", [P, 2, 4, P])
        const_landed = sem("const_landed")
        landed = [sem("landed0"), sem("landed1")]
        cleared = sem("cleared")
        scaled, v_turned, v_copied = sem("scaled"), sem("v_turned"), sem("v_copied")
        z_ready, clipped, exp_done, log_done, sp_ready = (
            sem("z_ready"), sem("clipped"), sem("exp_done"), sem("log_done"), sem("sp_ready"))
        sums_ready, w_ready, pv_done, o_copied, dve_step = (
            sem("sums_ready"), sem("w_ready"), sem("pv_done"), sem("o_copied"), sem("dve_step"))

        def keys_of(job):
            return slice(0, job.keys)

        with blk as block:
            @block.sync
            def _(sp):
                for tile, src in ((strict, "strict"), (strict_masked, "strict_masked"), (neg_ones, "neg_ones")):
                    sp.dma_start(tile[:], t[src]).then_inc(const_landed, 16)

                def load(p, u):
                    for to, base in ((q, Q_TILE), (k, K_TILE), (v, V_TILE)):
                        sp.dma_start(to[:, u], t["proj"][bass.ds(p + base, 1)].rearrange("a p t -> (a p) t")).then_inc(landed[u], 16)
                    sp.dma_start(past_k[:, u], t["past_k"][bass.ds(p, 1)].rearrange("a p t -> (a p) t")).then_inc(landed[u], 16)
                    sp.dma_start(past_v[:, u].rearrange("p b d -> p (b d)"),
                                 t["past_v"][bass.ds(p, 1)].rearrange("a p b d -> (a p) (b d)")).then_inc(landed[u], 16)

                for p in range(PAIRS):
                    if p >= 2:
                        sp.wait_ge(pv_done, 4 + JN * (p - 1))
                    load(p, p % 2)

            @block.gpsimd
            def _(pool):
                nc.gpsimd.memset(q_diag[:], 0.0).then_inc(cleared, 1)

            @block.scalar
            def _(act):
                credit(act, pv_done, 4)
                act.wait_ge(cleared, 1)
                act.preload_act_table_set("natural_log_exp_and_others")

                def weights(p, job):
                    act.wait_ge(sums_ready, JN * p + job.n + 5)
                    act.wait_ge(pv_done, JN * p + job.n + 1)
                    nc.scalar.activation(weight[keys_of(job), job.slot, job.cols], z[keys_of(job), job.slot, job.cols],
                                         ACT.Exp).then_inc(w_ready, 1)

                def copy_out(p, job):
                    act.wait_ge(pv_done, JN * p + job.n + 5)
                    if job.kind == "prompt":
                        to, src = slice(job.qb * QW, job.qb * QW + QW), o[:, job.qb, :]
                    else:
                        to, src = SL, spare[:, 1, 0, :SAMPLE]
                    nc.scalar.activation(mixed[:, bass.ds(p + 4, 1), to], src.unsqueeze(1), ACT.Copy).then_inc(o_copied, 1)

                def pair(p, u):
                    act.wait_ge(landed[u], (p - u) * 40 + 80)
                    for h in range(2):
                        hp = slice(HD * h, HD * h + HD)
                        nc.scalar.activation(q_diag[hp, u, h * SAMPLE:h * SAMPLE + SAMPLE], q[hp, u, SL], ACT.Copy,
                                             scale=HD ** -0.5).then_inc(scaled, 1)
                    nc.scalar.activation(q[:, u, :PROMPT], q[:, u, :PROMPT], ACT.Copy, scale=HD ** -0.5).then_inc(scaled, 1)
                    for part, (lo, hi) in enumerate(((0, 4), (4, 8), (8, 9))):
                        act.wait_ge(v_turned, 3 * p + part + 1)
                        n = P if part < 2 else SAMPLE
                        nc.scalar.activation(v_rows[:n, lo:hi, :], spare[:n, part % 2, :hi - lo, :], ACT.Copy).then_inc(v_copied, 1)
                    for step in range(JN + 3):
                        if step < JN:
                            job = jobs[step]
                            tile = e[keys_of(job), job.slot, job.cols]
                            act.wait_ge(clipped, JN * p + job.n + 1)
                            nc.scalar.activation(tile, tile, ACT.Exp).then_inc(exp_done, 1)
                            act.wait_ge(exp_done, JN * p + job.n + 1)
                            nc.scalar.activation(tile, tile, ACT.Ln, bias=1.0).then_inc(log_done, 1)
                        if 2 <= step < JN + 2:
                            weights(p, jobs[step - 2])
                        done = jobs[step - 3] if step >= 3 else None
                        if done and (done.kind == "past" and done.b0 == 0 or done.kind == "prompt" and done.j == 0 and done.h):
                            copy_out(p, done)

                for p in range(PAIRS):
                    pair(p, p % 2)

            @block.tensor
            def _(pe):
                pe.wait_ge(const_landed, 48)
                credit(pe, w_ready, 4)
                credit(pe, o_copied, 3)
                credit(pe, v_copied, 3)

                def turn_v(p, u):
                    pe.wait_ge(landed[u], (p - u) * 40 + 80)
                    pe.wait_ge(pv_done, JN * p + 4)
                    pe.wait_ge(o_copied, 3 * p + 3)
                    for part, (lo, hi) in enumerate(((0, 4), (4, 8), (8, 9))):
                        if part == 2:
                            pe.wait_ge(v_copied, 3 * p + 4)
                        for b in range(lo, hi):
                            n = tokens_of(b)
                            last = nc.tensor.transpose(spare[:n, part % 2, b - lo, :], v[:, u, b * P:b * P + n], consts["ident"][:])
                        last.then_inc(v_turned, 1)

                def scores(p, u, job):
                    pe.wait_ge(w_ready, JN * p + job.n + 1)
                    if job.kind == "prompt":
                        hp = slice(HD * job.h, HD * job.h + HD)
                        last = nc.tensor.matmul(z[:, job.slot, job.cols], k[hp, u, job.j * P:job.j * P + P],
                                                q[hp, u, job.qb * QW + job.lo:job.qb * QW + QW],
                                                start=True, stop=True, skip_group_check=True)
                    else:
                        for b in range(1 if job.kind == "new" else 8):
                            rows = k[:, u, SL] if job.kind == "new" else past_k[:, u, (job.b0 + b) * P:(job.b0 + b + 1) * P]
                            last = nc.tensor.matmul(z[keys_of(job), job.slot, b * 64:b * 64 + 64], rows, q_diag[:, u],
                                                    start=True, stop=True, skip_group_check=True)
                    last.then_inc(z_ready, 1)

                def suffix_sums(p, job):
                    pe.wait_ge(sp_ready, JN * p + job.n + 1)
                    bank, sp_tile, kk = z[keys_of(job), job.slot, :], softplus[keys_of(job), job.slot, :], job.keys

                    def add(cols, lhs, rhs):
                        return nc.tensor.matmul(bank[:, cols], lhs, rhs, start=False, stop=True, skip_group_check=True)

                    if job.kind == "prompt" and job.diag:
                        add(slice(job.lo, job.lo + P), consts["ident"][:], strict_masked[:])
                    if job.kind == "new":
                        for h in range(2):
                            add(slice(h * SAMPLE, h * SAMPLE + SAMPLE), consts["ident"][:kk, :kk], strict_masked[:kk, :SAMPLE])
                    last = add(job.cols, consts["suffix"][:kk, :kk], sp_tile[:, job.cols])
                    if job.kind == "prompt" and job.step:
                        cols = slice(job.t_lo, QW)
                        last = add(cols, neg_ones[:], later[:, job.h, job.step % 2, cols])
                    if job.kind == "past":
                        new = softplus[:SAMPLE, jobs[JN - 3].slot, :2 * SAMPLE]
                        for b in range(8):
                            last = add(slice(b * 64, b * 64 + 64), neg_ones[:SAMPLE], new)
                        nb = min(job.b0 + 8, PB - 1) - job.b0
                        last = add(slice(0, nb * 64), neg_ones[:], s_later[:, job.b0:job.b0 + nb].rearrange("p b c -> p (b c)"))
                    last.then_inc(sums_ready, 1)

                def outputs(p, u, job):
                    pe.wait_ge(w_ready, JN * p + job.n + 5)
                    if job.kind == "prompt":
                        if job.step == 0:
                            pe.wait_ge(o_copied, 3 * p + job.qb + 1)
                        hp = slice(HD * job.h, HD * job.h + HD)
                        last = nc.tensor.matmul(o[hp, job.qb, job.cols], v_rows[:, job.j, hp], weight[:, job.slot, job.cols],
                                                start=(job.step == 0), stop=(job.j == 0), skip_group_check=True)
                    else:
                        for b in range(1 if job.kind == "new" else 8):
                            for h in range(2):
                                hp = slice(HD * h, HD * h + HD)
                                rows = v_rows[:SAMPLE, TILES - 1, hp] if job.kind == "new" else past_v[:, u, job.b0 + b, hp]
                                at = (2 * b + h) * SAMPLE
                                last = nc.tensor.matmul(spare[hp, 1, 0, :SAMPLE], rows, weight[keys_of(job), job.slot, at:at + SAMPLE],
                                                        start=(job.kind == "new"), stop=(job.kind == "past" and job.b0 == 0 and b == 7),
                                                        skip_group_check=True)
                    last.then_inc(pv_done, 1)

                def pair(p, u):
                    turn_v(p, u)
                    pe.wait_ge(scaled, 3 * p + 3)
                    for step in range(JN + 3):
                        if step < JN:
                            scores(p, u, jobs[step])
                        if 2 <= step < JN + 2:
                            suffix_sums(p, jobs[step - 2])
                        if step == 3:
                            pe.wait_ge(v_copied, 3 * p + 6)
                        if step >= 3:
                            outputs(p, u, jobs[step - 3])

                for p in range(PAIRS):
                    pair(p, p % 2)

            @block.vector
            def _(dve):
                dve.wait_ge(const_landed, 48)
                credit(dve, sums_ready, 4)
                links = [0]

                def link(instruction):
                    links[0] += 1
                    instruction.then_inc(dve_step, 1)
                    dve.wait_ge(dve_step, links[0])

                def clip(p, job):
                    dve.wait_ge(z_ready, JN * p + job.n + 1)
                    nc.vector.tensor_scalar(e[keys_of(job), job.slot, job.cols], z[keys_of(job), job.slot, job.cols],
                                            40.0, None, ALU.min).then_inc(clipped, 1)

                def soft(p, job):
                    tile = softplus[keys_of(job), job.slot, :]
                    dve.wait_ge(log_done, JN * p + job.n + 1)
                    dve.wait_ge(sums_ready, JN * p + job.n + 1)
                    soft_max = nc.vector.tensor_tensor(tile[:, job.cols], z[keys_of(job), job.slot, job.cols],
                                                       e[keys_of(job), job.slot, job.cols], ALU.max)
                    if job.kind == "prompt":
                        first = slice(job.lo, job.lo + P)
                        if job.diag:
                            link(soft_max)
                            masking = nc.vector.tensor_tensor(tile[:, first], tile[:, first], strict[:], ALU.mult)
                        last = masking if job.diag else soft_max
                        if job.j:
                            link(last)
                            dve.wait_ge(sums_ready, JN * p + job.n + 3)
                            to = later[:, job.h, (job.step + 1) % 2, :]
                            if job.diag:
                                last = nc.vector.tensor_copy(to[:, first], tile[:, first])
                            if job.step:
                                cols = slice(job.t_lo, QW)
                                last = nc.vector.tensor_tensor(to[:, cols], later[:, job.h, job.step % 2, cols], tile[:, cols], ALU.add)
                    elif job.kind == "new":
                        link(soft_max)
                        halves = tile[:, :64].rearrange("p (h q) -> p h q", h=2)
                        last = nc.vector.tensor_tensor(halves, halves, strict[:SAMPLE, :SAMPLE].unsqueeze(1).to_broadcast([SAMPLE, 2, SAMPLE]), ALU.mult)
                    else:
                        link(soft_max)
                        if job.b0:
                            dve.wait_ge(sums_ready, JN * p + 4)
                            link(nc.vector.tensor_copy(s_later[:, PB - 2], tile[:, 7 * 64:8 * 64]))
                        for b in range(PB - 3 if job.b0 else 7, job.b0 - 1 if job.b0 else -1, -1):
                            nxt = jobs[JN - 2 if b + 1 >= 8 else JN - 1]
                            last = nc.vector.tensor_tensor(s_later[:, b], s_later[:, b + 1],
                                                           softplus[:, nxt.slot, (b + 1) % 8 * 64:(b + 1) % 8 * 64 + 64], ALU.add)
                            if b > job.b0:
                                link(last)
                    last.then_inc(sp_ready, 1)
                    dve.wait_ge(sp_ready, JN * p + job.n + 1)

                for p in range(PAIRS):
                    clip(p, jobs[0])
                    for n in range(JN):
                        if n + 1 < JN:
                            clip(p, jobs[n + 1])
                        soft(p, jobs[n])


def output_projection(nc, mixed, h, w_out, x, h_dram):
    with phase(nc, "outproj") as (sb, ps, sem, blk):
        m_hi, m_lo = sb("m_hi", [P, DC, TOK], F32R), sb("m_lo", [P, DC, TOK], F32R)
        w_raw = sb("w_raw", [P, DC, P])
        w_hi, w_lo = sb("w_hi", [P, 2, DC, P], F32R), sb("w_lo", [P, 2, DC, P], F32R)
        residual = sb("residual", [P, 2, TOK])
        acc = ps("acc", [P, 2, 3, 512])
        w_landed, x_landed = sem("w_landed"), [sem("x_landed0"), sem("x_landed1")]
        m_hi_ready, m_lo_ready = sem("m_hi_ready"), sem("m_lo_ready")
        hi_ready, lo_ready, projected, added, stored = (
            sem("hi_ready"), sem("lo_ready"), sem("projected"), sem("added"), sem("stored"))
        pairs = DC // 2
        with blk as block:
            @block.sync
            def _(sp):
                credit(sp, lo_ready, 1)
                with sp.Fori(0, pairs) as i:
                    for u in range(2):
                        sp.wait_ge(lo_ready, 2 * i + u + 1)
                        sp.dma_start(w_raw[:], w_out[bass.ds(2 * i + u, 1)].rearrange("a p k m -> p (a k) m")).then_inc(w_landed, 16)
                        sp.wait_ge(added, 6 * i + 3 * u + 3)
                        sp.dma_start(residual[:, u], x[:, bass.ds(2 * i + u, 1), :].rearrange("p a t -> p (a t)")).then_inc(x_landed[u], 16)
                sp.wait_ge(added, 3 * DC + 6)
                sp.dma_start(h_dram, h[:]).then_inc(stored, 16)
                sp.wait_ge(stored, 16)

            @block.scalar
            def _(act):
                for k in range(DC):
                    nc.scalar.activation(m_hi[:, k], mixed[:, k], ACT.Copy).then_inc(m_hi_ready, 1)
                with act.Fori(0, pairs) as i:
                    for u in range(2):
                        act.wait_ge(w_landed, 32 * i + 16 * u + 16)
                        act.wait_ge(projected, 6 * i + 3 * u + 3)
                        nc.scalar.activation(w_hi[:, u], w_raw[:], ACT.Copy).then_inc(hi_ready, 1)

            @block.vector
            def _(dve):
                credit(dve, added, 6)
                for k in range(DC):
                    dve.wait_ge(m_hi_ready, k + 1)
                    nc.vector.tensor_tensor(m_lo[:, k], mixed[:, k], m_hi[:, k].bitcast(F32), ALU.subtract).then_inc(m_lo_ready, 1)

                def split_low(i, u):
                    dve.wait_ge(hi_ready, 2 * i + u + 1)
                    nc.vector.tensor_tensor(w_lo[:, u], w_raw[:], w_hi[:, u].bitcast(F32), ALU.subtract).then_inc(lo_ready, 1)

                def add_residual(i, u):
                    dve.wait_ge(x_landed[u], 16 * i + 16)
                    for n in range(NBN):
                        tok = slice(n * NB, n * NB + NB)
                        dve.wait_ge(projected, 6 * i + 3 * u + n + 7)
                        nc.vector.tensor_tensor(h[:, bass.ds(2 * i + u, 1), tok], acc[:, u:u + 1, n, :NB], residual[:, u:u + 1, tok],
                                                ALU.add).then_inc(added, 1)

                split_low(0, 0)
                with dve.Fori(0, pairs - 1) as i:
                    split_low(i, 1)
                    add_residual(i, 0)
                    split_low(i + 1, 0)
                    add_residual(i, 1)
                split_low(pairs - 1, 1)
                add_residual(pairs - 1, 0)
                add_residual(pairs - 1, 1)

            @block.tensor
            def _(pe):
                credit(pe, projected, 6)
                pe.wait_ge(m_lo_ready, DC)
                with pe.Fori(0, pairs) as i:
                    for u in range(2):
                        pe.wait_ge(lo_ready, 2 * i + u + 2)
                        for n in range(NBN):
                            pe.wait_ge(added, 6 * i + 3 * u + n + 1)
                            project(nc, acc[:, u, n, :NB], w_hi[:, u], w_lo[:, u], m_hi, m_lo, n).then_inc(projected, 1)


def held(dve, sem, value, passed):
    dve.wait_ge(sem, value)
    dve.sem_inc(passed, 1)


def retrieval_phase(nc, x_hi, x_lo, w_q, keys, top_v, top_i):
    with phase(nc, "retrieve") as (sb, ps, sem, blk):
        w_raw = sb("w_raw", [P, DC, P])
        w_hi, w_lo = sb("w_hi", [P, 2, DC, P], F32R), sb("w_lo", [P, 2, DC, P], F32R)
        key_tile = sb("key_tile", [P, 2, KEYS])
        query = sb("query", [P, 2, TOK])
        scores = sb("scores", [P, 2, TILES, KEYS])
        rest = sb("rest", [P, TILES, KEYS])
        best_v, best_i = sb("best_v", [P, TILES, TOPK]), sb("best_i", [P, TILES, TOPK], U32)
        acc = ps("acc", [P, 3, 512])
        score_ps = ps("score_ps", [P, 3, 4, KEYS])
        w_landed, k_landed = sem("w_landed"), [sem("k_landed0"), sem("k_landed1")]
        hi_ready, lo_ready, projected, query_ready = sem("hi_ready"), sem("lo_ready"), sem("projected"), sem("query_ready")
        scored, copied = sem("scored"), sem("copied")
        max1, place1, replaced, max2, place2, kept = (sem(n) for n in ("max1", "place1", "replaced", "max2", "place2", "kept"))
        passed, cleared = sem("passed"), sem("cleared")
        pairs = HALVES // 2
        with blk as block:
            @block.sync
            def _(sp):
                credit(sp, lo_ready, 1)
                with sp.Fori(0, pairs) as i:
                    for u in range(2):
                        sp.wait_ge(lo_ready, 2 * i + u + 1)
                        sp.dma_start(w_raw[:], w_q[bass.ds(2 * i + u, 1)].rearrange("a p k m -> p (a k) m")).then_inc(w_landed, 16)
                        sp.wait_ge(scored, 6 * i + 3 * u + 3)
                        sp.dma_start(key_tile[:, u], keys[bass.ds(2 * i + u, 1)].rearrange("a p n -> (a p) n")).then_inc(k_landed[u], 16)

            @block.gpsimd
            def _(pool):
                nc.gpsimd.memset(best_v[:, TILES - 1], 0.0).then_inc(cleared, 1)
                nc.gpsimd.memset(best_i[:, TILES - 1], 0).then_inc(cleared, 1)

            @block.scalar
            def _(act):
                credit(act, scored, 6)
                credit(act, kept, 2)

                def split_high(i, u):
                    act.wait_ge(w_landed, 32 * i + 16 * u + 16)
                    act.wait_ge(projected, 6 * i + 3 * u + 3)
                    nc.scalar.activation(w_hi[:, u], w_raw[:], ACT.Copy).then_inc(hi_ready, 1)

                def copy_query(i, u):
                    act.wait_ge(scored, 6 * i + 3 * u + 3)
                    for n in range(NBN):
                        act.wait_ge(projected, 6 * i + 3 * u + n + 7)
                        nc.scalar.activation(query[:, u, n * NB:n * NB + NB], acc[:, n, :NB], ACT.Copy).then_inc(query_ready, 1)

                def copy_scores(i, u):
                    act.wait_ge(kept, 2 * i + u + 1)
                    for b in range(3):
                        act.wait_ge(scored, 6 * i + 3 * u + b + 7)
                        rows, last = (P, 4) if b < 2 else (SAMPLE, 1)
                        nc.scalar.activation(scores[:rows, u, 4 * b:4 * b + last], score_ps[:rows, b, :last], ACT.Copy).then_inc(copied, 1)

                split_high(0, 0)
                split_high(0, 1)
                copy_query(0, 0)
                with act.Fori(0, pairs - 1) as i:
                    split_high(i + 1, 0)
                    copy_query(i, 1)
                    copy_scores(i, 0)
                    split_high(i + 1, 1)
                    copy_query(i + 1, 0)
                    copy_scores(i, 1)
                copy_query(pairs - 1, 1)
                copy_scores(pairs - 1, 0)
                copy_scores(pairs - 1, 1)

            @block.tensor
            def _(pe):
                credit(pe, projected, 6)
                credit(pe, query_ready, 3)
                credit(pe, copied, 3)

                def queries(i, u):
                    pe.wait_ge(lo_ready, 2 * i + u + 2)
                    for n in range(NBN):
                        pe.wait_ge(query_ready, 6 * i + 3 * u + n + 1)
                        project(nc, acc[:, n, :NB], w_hi[:, u], w_lo[:, u], x_hi, x_lo, n).then_inc(projected, 1)

                def score(i, u):
                    pe.wait_ge(query_ready, 6 * i + 3 * u + 6)
                    pe.wait_ge(k_landed[u], 16 * i + 16)
                    for b in range(3):
                        pe.wait_ge(copied, 6 * i + 3 * u + b + 1)
                        for tile in range(4 * b, min(4 * b + 4, TILES)):
                            n = tokens_of(tile)
                            last = nc.tensor.matmul(score_ps[:n, b, tile - 4 * b], query[:, u, tile * P:tile * P + n],
                                                    key_tile[:, u], start=True, stop=True)
                        last.then_inc(scored, 1)

                queries(0, 0)
                with pe.Fori(0, pairs - 1) as i:
                    queries(i, 1)
                    score(i, 0)
                    queries(i + 1, 0)
                    score(i, 1)
                queries(pairs - 1, 1)
                score(pairs - 1, 0)
                score(pairs - 1, 1)

            @block.vector
            def _(dve):
                dve.wait_ge(cleared, 2)

                def split_low(i, u):
                    dve.wait_ge(hi_ready, 2 * i + u + 1)
                    nc.vector.tensor_tensor(w_lo[:, u], w_raw[:], w_hi[:, u].bitcast(F32), ALU.subtract).then_inc(lo_ready, 1)

                def best(i, u):
                    at = 2 * i + u
                    rows = [(tile, tokens_of(tile)) for tile in range(TILES)]
                    first, second = slice(0, 8), slice(8, 16)
                    held(dve, copied, 6 * i + 3 * u + 6, passed)
                    held(dve, kept, at + 2, passed)
                    for tile, n in rows:
                        nc.vector.max(best_v[:n, tile, first], scores[:n, u, tile]).then_inc(max1, 1)
                    held(dve, max1, TILES * at + TILES, passed)
                    for tile, n in rows:
                        nc.vector.max_index(best_i[:n, tile, first], best_v[:n, tile, first], scores[:n, u, tile]).then_inc(place1, 1)
                    for tile, n in rows:
                        nc.vector.match_replace(rest[:n, tile], best_v[:n, tile, first], scores[:n, u, tile], LOWEST).then_inc(replaced, 1)
                    held(dve, replaced, TILES * at + TILES, passed)
                    for tile, n in rows:
                        nc.vector.max(best_v[:n, tile, second], rest[:n, tile]).then_inc(max2, 1)
                    held(dve, max2, TILES * at + TILES, passed)
                    for tile, n in rows:
                        nc.vector.max_index(best_i[:n, tile, second], best_v[:n, tile, second], rest[:n, tile]).then_inc(place2, 1)
                    dve.wait_ge(place2, TILES * at + TILES)
                    nc.vector.tensor_copy(top_v[:, :, bass.ds(at, 1), :], best_v[:].unsqueeze(2))
                    nc.vector.tensor_copy(top_i[:, :, bass.ds(at, 1), :], best_i[:].unsqueeze(2)).then_inc(kept, 1)

                split_low(0, 0)
                split_low(0, 1)
                with dve.Fori(0, pairs - 1) as i:
                    split_low(i + 1, 0)
                    best(i, 0)
                    split_low(i + 1, 1)
                    best(i, 1)
                best(pairs - 1, 0)
                best(pairs - 1, 1)


class EarlyHidden:

    def __init__(self, nc, t, sb, ps, sem, x_hi, x_lo, base, slots):
        self.nc, self.t, self.x_hi, self.x_lo, self.base, self.slots = nc, t, x_hi, x_lo, base, slots
        self.raw = sb("u_raw", [P, DC, P])
        self.hi, self.lo = sb("u_hi", [P, slots, DC, P], F32R), sb("u_lo", [P, slots, DC, P], F32R)
        self.out = sb("hidden_out", [P, NBN, NB])
        self.acc = ps("hidden", [P, NBN, 512])
        self.landed, self.split, self.ready = sem("u_landed"), sem("u_split"), sem("u_ready")
        self.products, self.activated = sem("u_products"), sem("u_activated")
        self.stored = [sem(f"u_stored{n}") for n in range(NBN)]

    def sync_start(self, sp):
        credit(sp, self.ready, 1)
        for n in range(NBN):
            credit(sp, self.stored[n], 16)

    def load(self, sp, j):
        sp.wait_ge(self.ready, j + 1)
        sp.dma_start(self.raw[:], self.t["peer_u"][bass.ds(j + self.base, 1)]
                     .rearrange("a p k m -> p (a k) m")).then_inc(self.landed, 16)

    def store_bank(self, sp, j, n):
        sp.wait_ge(self.activated, 3 * j + n + 4)
        sp.dma_start(self.t["hidden"][bass.ds(j + self.base, 1), :, n * NB:n * NB + NB].rearrange("a p t -> (a p) t"),
                     self.out[:, n]).then_inc(self.stored[n], 16)

    def store(self, sp, j):
        for n in range(NBN):
            self.store_bank(sp, j, n)

    def sync_end(self, sp, tiles):
        for n in range(NBN):
            sp.wait_ge(self.stored[n], 16 * tiles + 16)

    def split_high(self, act, j, slot):
        act.wait_ge(self.landed, 16 * j + 16)
        act.wait_ge(self.products, 3 * j + 3)
        self.nc.scalar.activation(self.hi[:, slot], self.raw[:], ACT.Copy).then_inc(self.split, 1)

    def activate(self, act, j, n):
        act.wait_ge(self.stored[n], 16 * j + 16)
        act.wait_ge(self.products, 3 * j + n + 3 * self.slots + 1)
        self.nc.scalar.activation(self.out[:, n], self.acc[:, n, :NB], ACT.Gelu).then_inc(self.activated, 1)

    def split_low(self, dve, j, slot):
        dve.wait_ge(self.split, j + 1)
        self.nc.vector.tensor_tensor(self.lo[:, slot], self.raw[:], self.hi[:, slot].bitcast(F32),
                                     ALU.subtract).then_inc(self.ready, 1)

    def tensor_start(self, pe):
        credit(pe, self.products, 3 * self.slots)
        credit(pe, self.activated, 3)

    def multiply(self, pe, j, slot, n):
        if n == 0:
            pe.wait_ge(self.ready, j + 2)
        pe.wait_ge(self.activated, 3 * j + n + 1)
        project(self.nc, self.acc[:, n, :NB], self.hi[:, slot], self.lo[:, slot], self.x_hi, self.x_lo, n).then_inc(self.products, 1)


def routing_phase(nc, consts, t, x_hi, x_lo, top_v, top_i, routes):
    HK = PEER_HEADS * TOPK
    with phase(nc, "route") as (sb, ps, sem, blk):
        cand, rest = sb("cand", [P, PEER_HEADS, TOPK, TOPK]), sb("rest", [P, PEER_HEADS, TOPK * TOPK])
        best_v, best_i = sb("best_v", [P, PEER_HEADS, TOPK]), sb("best_i", [P, PEER_HEADS, TOPK], U32)
        half_i, half = sb("half_i", [P, 2, PEER_HEADS, TOPK], U32), sb("half", [P, 2, HK])
        found = sb("found", [P, 2, PEER_HEADS * TOPK, TOPK])
        rows = sb("rows", [P, 3, HK])
        shifted = sb("shifted", [P, PEER_HEADS, TOPK])
        total = sb("total", [P, PEER_HEADS])
        turned = ps("turned", [P, 2, 4, P])
        early = EarlyHidden(nc, t, sb, ps, sem, x_hi, x_lo, 0, ROUTE_U)
        passed, gates_split = sem("passed"), sem("gates_split")
        iota = consts["iota"]
        step, maxed, exp_done, rows_ready, transposed, copied = (
            sem("step"), sem("maxed"), sem("exp_done"), sem("rows_ready"), sem("transposed"), sem("copied"))
        with blk as block:
            @block.sync
            def _(sp):
                early.sync_start(sp)
                for j in range(ROUTE_U):
                    early.load(sp, j)
                with sp.Fori(0, TILES - 1) as i:
                    for a in range(ROUTE_U):
                        early.load(sp, ROUTE_U * i + a + ROUTE_U)
                        early.store(sp, ROUTE_U * i + a)
                early.load(sp, EARLY_ROUTE - 1)
                for a in range(ROUTE_U + 1):
                    early.store(sp, ROUTE_U * (TILES - 1) + a)
                early.sync_end(sp, EARLY_ROUTE)

            @block.scalar
            def _(act):
                def tile(i, n, at, extra=0):
                    for a in range(ROUTE_U + extra):
                        for b in range(NBN):
                            early.activate(act, ROUTE_U * i + a, b)
                        if extra == 0 or a == 0:
                            early.split_high(act, ROUTE_U * i + a + ROUTE_U, a)
                        if a == 1:
                            act.wait_ge(maxed, i + 1)
                            nc.scalar.activation(shifted[:n], shifted[:n], ACT.Exp).then_inc(exp_done, 1)
                    act.wait_ge(transposed, i + 2)
                    nc.scalar.activation(routes[:, :2, bass.ds(at, n)], turned[:, 0, :2, :n], ACT.Copy).then_inc(copied, 1)
                    nc.scalar.activation(routes[:, 2:3, bass.ds(at, n)].bitcast(F32R), turned[:, 0, 2:3, :n], ACT.Copy).then_inc(copied, 1)

                for a in range(ROUTE_U):
                    early.split_high(act, a, a)
                with act.Fori(0, TILES - 1) as i:
                    tile(i, P, i * P)
                tile(TILES - 1, SAMPLE, PROMPT, 1)

            @block.tensor
            def _(pe):
                credit(pe, gates_split, 1)
                credit(pe, transposed, 1)
                early.tensor_start(pe)

                def tile(i, n, extra=0):
                    for a in range(ROUTE_U + extra):
                        for b in range(NBN):
                            early.multiply(pe, ROUTE_U * i + a, a % ROUTE_U, b)
                    pe.wait_ge(rows_ready, i + 1)
                    pe.wait_ge(gates_split, i + 1)
                    for a in range(3):
                        last = nc.tensor.transpose(turned[:, 0, a, :n], rows[:n, a], consts["ident"][:n, :n])
                    last.then_inc(transposed, 1)

                with pe.Fori(0, TILES - 1) as i:
                    tile(i, P)
                tile(TILES - 1, SAMPLE, 1)

            @block.vector
            def _(dve):
                STEPS = 12

                def split_gates(i, n, at):
                    dve.wait_ge(copied, 2 * i + 2)
                    nc.vector.tensor_tensor(routes[:, 3:4, bass.ds(at, n)], turned[:, 0, 2:3, :n], routes[:, 2:3, bass.ds(at, n)],
                                            ALU.subtract).then_inc(gates_split, 1)

                def tile(i, n, at, extra=0):
                    done = [0]

                    def link(instruction):
                        instruction.then_inc(step, 1)
                        done[0] += 1
                        held(dve, step, i * STEPS + done[0], passed)

                    halves = top_v[:n, bass.ds(i, 1)].rearrange("p a (h s) k -> p (a h) s k", s=2)
                    places = top_i[:n, bass.ds(i, 1)].rearrange("p a (h s) k -> p (a h) s k", s=2)
                    shape = [n, PEER_HEADS, TOPK, TOPK]
                    link(nc.vector.tensor_tensor(cand[:n], halves[:, :, 0].unsqueeze(3).to_broadcast(shape),
                                                 halves[:, :, 1].unsqueeze(2).to_broadcast(shape), ALU.add))
                    sums = cand[:n].rearrange("p h i j -> p h (i j)")
                    for h in range(PEER_HEADS):
                        last = nc.vector.max(best_v[:n, h, :8], sums[:, h])
                    link(last)
                    for h in range(PEER_HEADS):
                        nc.vector.max_index(best_i[:n, h, :8], best_v[:n, h, :8], sums[:, h])
                    for h in range(PEER_HEADS):
                        last = nc.vector.match_replace(rest[:n, h], best_v[:n, h, :8], sums[:, h], LOWEST)
                    link(last)
                    for h in range(PEER_HEADS):
                        last = nc.vector.max(best_v[:n, h, 8:], rest[:n, h])
                    link(last)
                    nc.vector.tensor_tensor(shifted[:n], best_v[:n], best_v[:n, :, :1].to_broadcast([n, PEER_HEADS, TOPK]),
                                            ALU.subtract).then_inc(maxed, 1)
                    for h in range(PEER_HEADS):
                        last = nc.vector.max_index(best_i[:n, h, 8:], best_v[:n, h, 8:], rest[:n, h])
                    link(last)
                    nc.vector.tensor_scalar(half_i[:n, 0], best_i[:n], 4, None, ALU.logical_shift_right)
                    link(nc.vector.tensor_scalar(half_i[:n, 1], best_i[:n], TOPK - 1, None, ALU.bitwise_and))
                    early.split_low(dve, ROUTE_U * i + ROUTE_U, 0)
                    link(nc.vector.tensor_copy(half[:n], half_i[:n].rearrange("p a h k -> p a (h k)")))
                    wide = [n, HK, TOPK]
                    for s in range(2):
                        last = nc.vector.tensor_tensor(found[:n, s], half[:n, s].unsqueeze(2).to_broadcast(wide),
                                                       iota[:n, :TOPK].unsqueeze(1).to_broadcast(wide), ALU.is_equal)
                    link(last)
                    for s in range(2):
                        by_head = found[:n, s].rearrange("p (h k) i -> p h k i", h=PEER_HEADS)
                        last = nc.vector.tensor_tensor(by_head, by_head, places[:, :, s].unsqueeze(2).to_broadcast(shape), ALU.mult)
                    link(last)
                    if not extra:
                        early.split_low(dve, ROUTE_U * i + ROUTE_U + 1, 1)
                    dve.wait_ge(transposed, i + 1)
                    nc.vector.tensor_reduce(rows[:n, 0:2], found[:n], AX.X, ALU.add)
                    dve.wait_ge(exp_done, i + 1)
                    link(nc.vector.tensor_reduce(total[:n], shifted[:n], AX.X, ALU.add))
                    link(nc.vector.reciprocal(total[:n], total[:n]))
                    gate = rows[:n, 2].rearrange("p (h k) -> p h k", h=PEER_HEADS)
                    link(nc.vector.tensor_tensor(gate, shifted[:n], total[:n].unsqueeze(2).to_broadcast([n, PEER_HEADS, TOPK]), ALU.mult))
                    dve.sem_inc(rows_ready, 1)
                    assert done[0] == STEPS
                    if not extra:
                        early.split_low(dve, ROUTE_U * i + ROUTE_U + 2, 2)

                for a in range(ROUTE_U):
                    early.split_low(dve, a, a)
                tile(0, P, 0)
                with dve.Fori(1, TILES - 1) as i:
                    tile(i, P, i * P)
                    split_gates(i - 1, P, i * P - P)
                tile(TILES - 1, SAMPLE, PROMPT, 1)
                split_gates(TILES - 2, P, PROMPT - P)
                split_gates(TILES - 1, SAMPLE, PROMPT)


def gate_phase(nc, consts, t, x_hi, x_lo, routes):
    with phase(nc, "gates") as (sb, ps, sem, blk):
        early = EarlyHidden(nc, t, sb, ps, sem, x_hi, x_lo, EARLY_ROUTE, 2)
        row_hot, col_hot = sb("row_hot", [P, RING, GG, P], F32R), sb("col_hot", [P, RING, GG, P])
        gate_hi, gate_lo = sb("gate_hi", [P, RING, GG, P], F32R), sb("gate_lo", [P, RING, GG, P], F32R)
        tile_buf = sb("tile_buf", [P, 2, KEYS, GT])
        product = ps("product", [P, RING, 4, P])
        stored = [sem("stored0"), sem("stored1")]
        cols_ready, hi_ready, lo_ready = sem("cols_ready"), sem("hi_ready"), sem("lo_ready")
        multiplied, copied = sem("multiplied"), sem("copied")
        iota = consts["iota"]
        groups = GT // GG
        slots = NBN * GATE_U
        PARTS = NBN * (GATE_U - 1)
        after = [range(groups * c // slots, groups * (c + 1) // slots) for c in range(slots)]
        wide = [P, GG, P]

        def of_group(a, g):
            return routes[:, a, bass.ds(g * GG, GG)].unsqueeze(2).to_broadcast(wide)

        def over_tiles(engine, tile):
            with engine.Fori(0, GTILES // 2) as i:
                for u in range(2):
                    tile(2 * i + u, u, i, 2 * groups * i + u * groups, 2 * GATE_U * i + u * GATE_U)

        with blk as block:
            @block.sync
            def _(sp):
                credit(sp, stored[0], 16 * PARTS)
                credit(sp, stored[1], 16 * PARTS)
                early.sync_start(sp)

                def store_part(at, u, c):
                    cols = slice(KEYS * c // PARTS, KEYS * (c + 1) // PARTS)
                    sp.dma_start(t["gates"][:, bass.ds(at, 1), cols].rearrange("p a c l -> p (a c l)"),
                                 tile_buf[:, u, cols].rearrange("p c l -> p (c l)")).then_inc(stored[u], 16)

                def tile(at, u, first=False, last=False):
                    j = at * GATE_U
                    for a in range(GATE_U):
                        if not (last and a >= GATE_U - 2):
                            early.load(sp, j + a + 2)
                        if a == 0 and not first:
                            sp.wait_ge(copied, at * groups + RING)
                        for n in range(NBN):
                            early.store_bank(sp, j + a, n)
                            if not first and a < GATE_U - 1:
                                store_part(at - 1, 1 - u, NBN * a + n)

                for j in range(2):
                    early.load(sp, j)
                tile(0, 0, first=True)
                with sp.Fori(0, GTILES // 2 - 1) as i:
                    tile(2 * i + 1, 1)
                    tile(2 * i + 2, 0)
                tile(GTILES - 1, 1, last=True)
                sp.wait_ge(copied, GTILES * groups + RING)
                for c in range(PARTS):
                    store_part(GTILES - 1, 1, c)
                for u in range(2):
                    sp.wait_ge(stored[u], 16 * PARTS * (GTILES // 2 + 1))
                early.sync_end(sp, GATE_U * GTILES)

            @block.vector
            def _(dve):
                credit(dve, multiplied, RING)
                credit(dve, cols_ready, RING)
                credit(dve, lo_ready, RING)

                def group(g, s):
                    dve.wait_ge(lo_ready, g + 1)
                    dve.wait_ge(hi_ready, g + 1)
                    dve.wait_ge(multiplied, g + 1)
                    every = iota[:].unsqueeze(1).to_broadcast(wide)
                    nc.vector.tensor_tensor(col_hot[:, s], every, of_group(1, g),
                                            ALU.is_equal).then_inc(cols_ready, 1)
                    nc.vector.tensor_tensor(row_hot[:, s], every, of_group(0, g), ALU.is_equal)
                    dve.wait_ge(cols_ready, g + RING + 1)
                    nc.vector.tensor_tensor(gate_lo[:, s], col_hot[:, s], of_group(3, g),
                                            ALU.mult).then_inc(lo_ready, 1)

                def tile(at, u, i, first, j, last=False):
                    for c in range(slots):
                        for g in after[c]:
                            group(first + g, (u * groups + g) % RING)
                        if c % NBN == NBN - 1 and not (last and c // NBN >= GATE_U - 2):
                            early.split_low(dve, j + c // NBN + 2, (u * GATE_U + c // NBN) % 2)

                early.split_low(dve, 0, 0)
                early.split_low(dve, 1, 1)
                pairs = GTILES // 2
                with dve.Fori(0, pairs - 1) as i:
                    for u in range(2):
                        tile(2 * i + u, u, i, 2 * groups * i + u * groups, 2 * GATE_U * i + u * GATE_U)
                tile(GTILES - 2, 0, pairs - 1, groups * (GTILES - 2), GATE_U * (GTILES - 2))
                tile(GTILES - 1, 1, pairs - 1, groups * (GTILES - 1), GATE_U * (GTILES - 1), last=True)

            @block.gpsimd
            def _(pool):
                credit(pool, hi_ready, RING)
                with pool.Fori(0, TOK // GG // RING) as g:
                    for s in range(RING):
                        pool.wait_ge(cols_ready, RING * g + s + RING + 1)
                        pool.wait_ge(multiplied, RING * g + s + 1)
                        nc.gpsimd.tensor_tensor(gate_hi[:, s], col_hot[:, s], of_group(2, RING * g + s),
                                                ALU.mult).then_inc(hi_ready, 1)

            @block.tensor
            def _(pe):
                credit(pe, copied, RING)
                early.tensor_start(pe)

                def tile(at, u, i, first, j):
                    for c in range(slots):
                        early.multiply(pe, j + c // NBN, (u * GATE_U + c // NBN) % 2, c % NBN)
                        for k in after[c]:
                            g, s = first + k, (u * groups + k) % RING
                            pe.wait_ge(lo_ready, g + RING + 1)
                            pe.wait_ge(hi_ready, g + RING + 1)
                            pe.wait_ge(copied, g + 1)
                            for a in range(GG):
                                nc.tensor.matmul(product[:, s, a], row_hot[:, s, a], gate_hi[:, s, a], start=True, stop=False)
                                last = nc.tensor.matmul(product[:, s, a], row_hot[:, s, a], gate_lo[:, s, a], start=False, stop=True)
                            last.then_inc(multiplied, 1)

                over_tiles(pe, tile)

            @block.scalar
            def _(act):
                act.preload_act_table_set("gelu_and_others")

                def tile(at, u, i, first, j, last=False):
                    act.wait_ge(stored[u], 16 * PARTS * (i + 1))
                    for c in range(slots):
                        early.activate(act, j + c // NBN, c % NBN)
                        if c % NBN == NBN - 1 and not (last and c // NBN >= GATE_U - 2):
                            early.split_high(act, j + c // NBN + 2, (u * GATE_U + c // NBN) % 2)
                        for k in after[c]:
                            act.wait_ge(multiplied, first + k + RING + 1)
                            to = tile_buf[:, u, :, k * GG:k * GG + GG].rearrange("p c l -> p l c")
                            nc.scalar.activation(to, product[:, (u * groups + k) % RING, :GG], ACT.Copy).then_inc(copied, 1)

                early.split_high(act, 0, 0)
                early.split_high(act, 1, 1)
                pairs = GTILES // 2
                with act.Fori(0, pairs - 1) as i:
                    for u in range(2):
                        tile(2 * i + u, u, i, 2 * groups * i + u * groups, 2 * GATE_U * i + u * GATE_U)
                tile(GTILES - 2, 0, pairs - 1, groups * (GTILES - 2), GATE_U * (GTILES - 2))
                tile(GTILES - 1, 1, pairs - 1, groups * (GTILES - 1), GATE_U * (GTILES - 1), last=True)


def experts_phase(nc, t, x_hi, x_lo, acc):
    DT, CH = D // P, 4
    with phase(nc, "experts") as (sb, ps, sem, blk):
        u_raw, v_raw = sb("u_raw", [P, DC, P]), sb("v_raw", [P, D])
        u_hi, u_lo = sb("u_hi", [P, KE, DC, P], F32R), sb("u_lo", [P, KE, DC, P], F32R)
        v_hi, v_lo = sb("v_hi", [P, 2, KE, D], F32R), sb("v_lo", [P, 2, KE, D], F32R)
        gate = sb("gate", [P, KE, TOK])
        coef = sb("coef", [P, KE, TOK])
        c_hi, c_lo = sb("c_hi", [P, 2, KE, TOK], F32R), sb("c_lo", [P, 2, KE, TOK], F32R)
        hidden = ps("hidden", [P, 3, 512])
        mixed = ps("mixed", [P, CH, 512])
        h_landed = sem("h_landed")
        u_landed, v_landed, g_landed = sem("u_landed"), sem("v_landed"), [sem("g_landed0"), sem("g_landed1")]
        u_split, u_ready, v_split, v_ready = sem("u_split"), sem("u_ready"), sem("v_split"), sem("v_ready")
        hidden_ready, activated, gated, c_split, c_ready = (
            sem("hidden_ready"), sem("activated"), sem("gated"), sem("c_split"), sem("c_ready"))
        mixed_ready, added = sem("mixed_ready"), sem("added")

        early_landed = [sem("early_landed0"), sem("early_landed1")]
        made_blocks = BLOCKS - EARLY // KE
        assert EARLY % KE == 0 and EARLY // KE >= made_blocks and (BLOCKS - 2 * made_blocks) % 2 == 0
        LOAD, MAKE = "load", "make"

        def over_blocks(engine, step):
            step(0, 0, LOAD, 0, 0, False)
            step(1, 1, MAKE, EARLY, 0, True)
            with engine.Fori(1, made_blocks) as i:
                step(2 * i, 0, LOAD, KE * i, KE * i, True)
                step(2 * i + 1, 1, MAKE, KE * i + EARLY, KE * i, True)
            with engine.Fori(made_blocks, BLOCKS // 2) as i:
                for par in range(2):
                    step(2 * i + par, par, LOAD, KE * (2 * i + par - made_blocks), None, True)
            step(BLOCKS, 0, None, None, None, True)

        with blk as block:
            @block.sync
            def _(sp):
                credit(sp, u_ready, 1)
                credit(sp, v_ready, 1)
                credit(sp, gated, 2)

                def load_u(made):
                    sp.wait_ge(u_ready, made + 1)
                    sp.dma_start(u_raw[:], t["peer_u"][bass.ds(made + EARLY, 1)].rearrange("a p k m -> p (a k) m")).then_inc(u_landed, 16)

                def step(b, par, how, tile, made, has_v):
                    if not how:
                        return
                    for a in range(KE):
                        at = KE * b + a
                        sp.wait_ge(gated, at + 1)
                        sp.dma_start(gate[:, a].rearrange("p (n l) -> p n l", n=GTILES),
                                     t["gates"][:, :, bass.ds(tile + a, 1), :].rearrange("p n a l -> p n (a l)")).then_inc(g_landed[a], 16)
                        if how == LOAD:
                            sp.wait_ge(c_ready, at + 1)
                            sp.dma_start(coef[:, a], t["hidden"][bass.ds(tile + a, 1)].rearrange("a p t -> (a p) t")).then_inc(early_landed[a], 16)
                            if made is not None:
                                load_u(made + a)
                        sp.wait_ge(v_ready, at + 1)
                        sp.dma_start(v_raw[:], t["peer_v"][bass.ds(tile + a, 1)].rearrange("a p d -> (a p) d")).then_inc(v_landed, 16)
                    if not has_v:
                        sp.dma_start(acc[:], t["h"]).then_inc(h_landed, 16)

                over_blocks(sp, step)

            @block.scalar
            def _(act):
                def split_u(made, a):
                    act.wait_ge(u_landed, 16 * made + 16)
                    act.wait_ge(hidden_ready, 3 * made + 3)
                    nc.scalar.activation(u_hi[:, a], u_raw[:], ACT.Copy).then_inc(u_split, 1)

                def step(b, par, how, tile, made, has_v):
                    if not how:
                        return
                    for a in range(KE):
                        at = KE * b + a
                        if how == MAKE:
                            act.wait_ge(c_ready, at + 1)
                            for n in range(NBN):
                                act.wait_ge(hidden_ready, 3 * (made + a) + n + 7)
                                nc.scalar.activation(coef[:, a, n * NB:n * NB + NB], hidden[:, n, :NB], ACT.Gelu).then_inc(activated, 1)
                        elif made is not None:
                            split_u(made + a, a)
                        act.wait_ge(v_landed, 16 * at + 16)
                        act.wait_ge(mixed_ready, 24 * b + 24)
                        nc.scalar.activation(v_hi[:, par, a], v_raw[:], ACT.Copy).then_inc(v_split, 1)
                        act.wait_ge(gated, at + 3)
                        nc.scalar.activation(c_hi[:, par, a], coef[:, a], ACT.Copy).then_inc(c_split, 1)

                act.preload_act_table_set("gelu_and_others")
                credit(act, mixed_ready, 48)
                over_blocks(act, step)

            @block.tensor
            def _(pe):
                def step(b, par, how, tile, made, has_v):
                    for a in range(KE if how == MAKE else 0):
                        pe.wait_ge(u_ready, made + a + 2)
                        for n in range(NBN):
                            pe.wait_ge(activated, 3 * (made + a) + n + 1)
                            project(nc, hidden[:, n, :NB], u_hi[:, a], u_lo[:, a], x_hi, x_lo, n).then_inc(hidden_ready, 1)
                    if not has_v:
                        return
                    old = 1 - par
                    pe.wait_ge(v_ready, KE * b + 1)
                    pe.wait_ge(c_ready, KE * b + 2)
                    for d in range(DT):
                        cols = slice(d * P, d * P + P)
                        for n in range(NBN):
                            at = NBN * d + n
                            tok = slice(n * NB, n * NB + NB)
                            pe.wait_ge(added, 24 * b + at - 23)
                            out = mixed[:, at % CH, :NB]
                            for a in range(KE):
                                nc.tensor.matmul(out, v_hi[:, old, a, cols], c_hi[:, old, a, tok], start=(a == 0), stop=False)
                                nc.tensor.matmul(out, v_lo[:, old, a, cols], c_hi[:, old, a, tok], start=False, stop=False)
                                last = nc.tensor.matmul(out, v_hi[:, old, a, cols], c_lo[:, old, a, tok], start=False, stop=(a == KE - 1))
                            last.then_inc(mixed_ready, 1)

                credit(pe, hidden_ready, 6)
                credit(pe, activated, 3)
                credit(pe, added, CH)
                over_blocks(pe, step)

            @block.gpsimd
            def _(pool):
                def split_v(tile, par, a):
                    pool.wait_ge(v_split, tile + 1)
                    nc.gpsimd.tensor_tensor(v_lo[:, par, a], v_raw[:], v_hi[:, par, a].bitcast(F32), ALU.subtract).then_inc(v_ready, 1)

                def coefficients(b, a, how, tile, made):
                    pool.wait_ge(g_landed[a], 16 * b + 16)
                    if how == LOAD:
                        pool.wait_ge(early_landed[a], tile * (16 // KE) + 16)
                    else:
                        pool.wait_ge(activated, 3 * (made + a) + 6)
                    nc.gpsimd.tensor_tensor(coef[:, a], coef[:, a], gate[:, a], ALU.mult).then_inc(gated, 1)

                def step(b, par, how, tile, made, has_v):
                    for a in range(KE if how else 0):
                        coefficients(b, a, how, tile, made)
                        split_v(KE * b + a, par, a)

                over_blocks(pool, step)

            @block.vector
            def _(dve):
                def split_u(made, a):
                    dve.wait_ge(u_split, made + 1)
                    nc.vector.tensor_tensor(u_lo[:, a], u_raw[:], u_hi[:, a].bitcast(F32), ALU.subtract).then_inc(u_ready, 1)

                def split_c(tile, par, a):
                    dve.wait_ge(c_split, tile + 1)
                    nc.vector.tensor_tensor(c_lo[:, par, a], coef[:, a], c_hi[:, par, a].bitcast(F32), ALU.subtract).then_inc(c_ready, 1)

                def add(b, lo, hi):
                    for at in range(lo, hi):
                        d, tok = at // NBN, slice(at % NBN * NB, at % NBN * NB + NB)
                        dve.wait_ge(mixed_ready, 24 * b + at + 25)
                        nc.vector.tensor_tensor(acc[:, d, tok], acc[:, d, tok], mixed[:, at % CH, :NB], ALU.add).then_inc(added, 1)

                def step(b, par, how, tile, made, has_v):
                    splits_u = how == LOAD and made is not None
                    for a in range(KE):
                        if splits_u:
                            split_u(made + a, a)
                            if has_v:
                                add(b, 8 * a, 8 * a + 4)
                        if how:
                            split_c(KE * b + a, par, a)
                        if has_v:
                            add(b, 8 * a + (4 if splits_u else 0), 8 * a + 8)
                    if has_v:
                        add(b, 8 * KE, 24)
                    else:
                        dve.wait_ge(h_landed, 16)

                credit(dve, c_ready, 2)
                over_blocks(dve, step)


def build(nc, t, upto=99):
    with ExitStack() as ctx:
        def sb(n, shape, dt=F32):
            return ctx.enter_context(nc.sbuf_tensor(n, shape, dt))

        ones, ident, iota = sb("ones", [P, P]), sb("ident", [P, P]), sb("iota", [P, P])
        vectors = sb("vectors", [P, 4 * DC + CONV_TILES * (TAPS + 1)])
        norm1_w, norm2_w, final_w = (vectors[:, DC * a:DC * (a + 1)] for a in range(3))
        ssm_norm_w, d_skip = vectors[:, 3 * DC:3 * DC + 4], vectors[:, 3 * DC + 4:4 * DC]
        conv_wb = vectors[:, 4 * DC:].rearrange("p (c a) -> p c a", a=TAPS + 1)
        mixers = ctx.enter_context(ExitStack())
        causal, masked, suffix = (mixers.enter_context(nc.sbuf_tensor(n, [P, P], F32)) for n in ("causal", "masked", "suffix"))
        head_vec = mixers.enter_context(nc.sbuf_tensor("head_vec", [P, 2, SSM_HEADS], F32))
        dt_raw = mixers.enter_context(nc.sbuf_tensor("dt_raw", [P, TILES, SSM_HEADS], F32))
        consts = {"ones": ones, "ident": ident, "causal": causal, "masked": masked, "suffix": suffix, "iota": iota}
        const_landed = ctx.enter_context(nc.semaphore("const_landed"))
        with nc.Block() as block:
            @block.sync
            def _(sp):
                for tile, src in ((ones, "ones"), (ident, "ident"), (causal, "causal"), (masked, "masked"),
                                  (suffix, "suffix"), (iota, "iota"), (vectors, "vectors"), (head_vec, "head_vec")):
                    sp.dma_start(tile[:], t[src]).then_inc(const_landed, 16)
                sp.wait_ge(const_landed, 16 * 8)

        with ExitStack() as early:
            x_hi = early.enter_context(nc.sbuf_tensor("x1_hi", [P, DC, TOK], F32R))
            x_lo = early.enter_context(nc.sbuf_tensor("x1_lo", [P, DC, TOK], F32R))
            with nc.sbuf_tensor("x", [P, DC, TOK], F32) as x:
                norm_phase(nc, "norm1", x, norm1_w, consts, hi=x_hi, lo=x_lo, src_dram=t["x"])
            input_projection(nc, consts, x_hi, x_lo, dt_raw, t["w_in"], t["w_dt"], t["proj"])
        if upto <= 1:
            return
        with ExitStack() as middle:
            mixed = middle.enter_context(nc.sbuf_tensor("mixed", [P, DC, TOK], F32))
            ssd_phase(nc, consts, (ssm_norm_w, d_skip, conv_wb), head_vec, dt_raw, t, mixed)
            if upto == 2:
                return dump(nc, mixed[:, :4], t["mixed"][:, :4])
            attention_phase(nc, consts, t, mixed)
            if upto == 3:
                return dump(nc, mixed[:], t["mixed"])
            h = middle.enter_context(nc.sbuf_tensor("h_tile", [P, DC, TOK], F32))
            output_projection(nc, mixed, h, t["w_out"], t["x"], t["h"])
        if upto == 4:
            return
        mixers.close()
        with ExitStack() as late:
            n_hi = late.enter_context(nc.sbuf_tensor("n_hi", [P, DC, TOK], F32R))
            n_lo = late.enter_context(nc.sbuf_tensor("n_lo", [P, DC, TOK], F32R))
            with nc.sbuf_tensor("h_again", [P, DC, TOK], F32) as h:
                norm_phase(nc, "norm2", h, norm2_w, consts, hi=n_hi, lo=n_lo, src_dram=t["h"])
            with ExitStack() as routing:
                routes = routing.enter_context(nc.sbuf_tensor("routes", [P, 4, TOK], F32))
                with ExitStack() as tops:
                    top_v = tops.enter_context(nc.sbuf_tensor("top_v", [P, TILES, HALVES, TOPK], F32))
                    top_i = tops.enter_context(nc.sbuf_tensor("top_i", [P, TILES, HALVES, TOPK], F32))
                    retrieval_phase(nc, n_hi, n_lo, t["w_q"], t["keys"], top_v, top_i)
                    routing_phase(nc, consts, t, n_hi, n_lo, top_v, top_i, routes)
                gate_phase(nc, consts, t, n_hi, n_lo, routes)
            if upto == 5:
                return
            acc = late.enter_context(nc.sbuf_tensor("acc", [P, DC, TOK], F32))
            experts_phase(nc, t, n_hi, n_lo, acc)
            with nc.sbuf_tensor("y", [P, DC, TOK], F32) as y:
                norm_phase(nc, "norm3", acc, final_w, consts, out=y, out_dram=t["y"])


_OUT = {
    "proj": [IN_TILES, P, TOK], "y": [P, DC, TOK], "state_prompt": [P, SSM_HEADS * HD],
    "state_sample": [P, SSM_HEADS * HD],
}
_SCRATCH = {"mixed": [P, DC, TOK], "h": [P, DC, TOK], "gates": [P, GTILES, KEYS, GT],
            "hidden": [EARLY, P, TOK]}


def dump(nc, tile, dram):
    with nc.semaphore("dumped") as sem, nc.Block() as block:
        @block.sync
        def _(sp):
            sp.dma_start(dram, tile[:]).then_inc(sem, 16)
            sp.wait_ge(sem, 16)


def chunked(w, cols):
    n = w.shape[1] // cols
    return np.ascontiguousarray(w.reshape(DC, P, n, cols).transpose(2, 1, 0, 3))


def per_partition(v):
    return v.reshape(-1, P).T


def lay_out(x_prompt, x_sample, cache_sb_k, cache_sb_v, state_ssm, state_conv,
            norm1_w, w_in, conv_w, conv_b, dt_bias, a_log, d_skip, ssm_norm_w, w_out,
            norm2_w, peer_wq, peer_k1, peer_k2, peer_u, peer_v, final_norm_w):
    x = np.concatenate([x_prompt[0], x_sample[0]], 0)
    w = w_in[0]
    conv = np.concatenate([conv_w[0], conv_b[0][None]], 0)
    k_idx, q_idx = np.arange(P)[:, None], np.arange(P)[None]
    vectors = np.concatenate([
        per_partition(norm1_w[0]), per_partition(norm2_w[0]), per_partition(final_norm_w),
        per_partition(ssm_norm_w[0]), per_partition(np.repeat(d_skip[0], HD)),
        conv.reshape(TAPS + 1, CONV_TILES, P).transpose(2, 1, 0).reshape(P, -1)], 1)
    a = {
        "x": x.T.reshape(DC, P, TOK).transpose(1, 0, 2),
        "w_in": chunked(np.concatenate([w[:, 512:1536], w[:, :512], w[:, 1544:]], 1), P),
        "w_dt": w[:, 1536:1544].reshape(DC, P, SSM_HEADS).transpose(1, 0, 2),
        "vectors": vectors,
        "head_vec": np.broadcast_to(np.stack([dt_bias[0], a_log[0]])[None], (P, 2, SSM_HEADS)),
        "conv_in": state_conv[0, 0].T.reshape(CONV_TILES, P, TAPS - 1).transpose(1, 0, 2),
        "state_in": state_ssm[0, 0].transpose(2, 0, 1).reshape(P, SSM_HEADS * HD),
        "past_k": cache_sb_k[0, 0].reshape(PAST, PAIRS, 2 * HD).transpose(1, 2, 0),
        "past_v": cache_sb_v[0, 0].reshape(PB, P, PAIRS, 2 * HD).transpose(2, 1, 0, 3),
        "w_out": chunked(w_out[0], P),
        "w_q": chunked(peer_wq[0], P),
        "keys": np.stack([peer_k1[0], peer_k2[0]], 1).reshape(HALVES, KEYS, P).transpose(0, 2, 1),
        "peer_u": peer_u[0].reshape(KEYS, KEYS, DC, P).transpose(1, 3, 2, 0),
        "peer_v": peer_v[0].reshape(KEYS, KEYS, D).transpose(1, 0, 2),
        "ones": np.ones((P, P), np.float32),
        "ident": np.eye(P, dtype=np.float32),
        "causal": (k_idx <= q_idx).astype(np.float32),
        "masked": np.where(k_idx <= q_idx, 0.0, MASKED).astype(np.float32),
        "strict": (k_idx < q_idx).astype(np.float32),
        "strict_masked": np.where(k_idx < q_idx, 0.0, MASKED).astype(np.float32),
        "neg_ones": -np.ones((P, P), np.float32),
        "suffix": -(k_idx >= q_idx).astype(np.float32),
        "iota": np.broadcast_to(np.arange(P, dtype=np.float32)[None], (P, P)),
    }
    return {n: np.ascontiguousarray(v) for n, v in a.items()}


def give_back(r):
    proj = r["proj"]

    def rows(tile, lo, hi):
        return proj[tile:tile + 4, :, lo:hi].transpose(2, 0, 1).reshape(1, 1, hi - lo, 8, HD)

    def conv_state(end):
        return proj[:CONV_TILES, :, end - (TAPS - 1):end].transpose(2, 0, 1).reshape(1, 1, TAPS - 1, D)

    def state(s):
        return s.reshape(P, SSM_HEADS, HD).transpose(1, 2, 0)[None, None]

    y = r["y"].transpose(2, 1, 0).reshape(TOK, D)
    out = (y[None, :PROMPT], y[None, PROMPT:], rows(K_TILE, 0, PROMPT), rows(V_TILE, 0, PROMPT),
           state(r["state_prompt"]), conv_state(PROMPT), rows(K_TILE, PROMPT, TOK), rows(V_TILE, PROMPT, TOK),
           state(r["state_sample"]), conv_state(TOK))
    return tuple(np.ascontiguousarray(o) for o in out)


def kernel(**inputs):
    import concourse.bacc as bacc
    from concourse.bass_utils import run_bass_kernel_spmd

    nc = bacc.Bacc("TRN2", target_bir_lowering=False, num_devices=1)
    arrays = lay_out(**{n: np.asarray(v) for n, v in inputs.items()})
    t = {n: nc.dram_tensor(f"in_{n}", a.shape, F32, kind="ExternalInput").ap() for n, a in arrays.items()}
    for n, shape in _OUT.items():
        t[n] = nc.dram_tensor(f"out_{n}", shape, F32, kind="ExternalOutput").ap()
    for n, shape in _SCRATCH.items():
        t[n] = nc.dram_tensor(f"scratch_{n}", shape, F32, kind="Internal").ap()
    build(nc, t)
    r = run_bass_kernel_spmd(nc, [{f"in_{n}": a for n, a in arrays.items()}], core_ids=[0])
    return give_back({n: r.results[0][f"out_{n}"] for n in _OUT})
```

```python
from contextlib import ExitStack, contextmanager
from functools import partial

import numpy as np

import concourse.bass as bass
from concourse import mybir

F32 = mybir.dt.float32
F32R = mybir.dt.float32r
U32 = mybir.dt.uint32
ACT = mybir.ActivationFunctionType
ALU = mybir.AluOpType
AX = mybir.AxisListType

P = 128
D = 1024
DC = D // P
PROMPT = 1024
SAMPLE = 32
TOK = PROMPT + SAMPLE
NB = 352
NBN = TOK // NB
EPS = 1e-6

SSM_HEADS = 8
HD = 64
STATE = 128
TAPS = 4
CONV_TILES = 8
Z_TILES, QKV_TILES = 4, 12
IN_TILES = CONV_TILES + Z_TILES + QKV_TILES
Q_TILE, K_TILE, V_TILE = 0, 4, 8
CHUNKS = PROMPT // P
S_OFF = PROMPT + TAPS - 1
CONV_W = TOK + 2 * (TAPS - 1)
CONV_OUT = CONV_W - (TAPS - 1)

PAIRS = 4
PAST = 2048
PB = PAST // P
QW = 512

PEER_HEADS = 8
HALVES = 2 * PEER_HEADS
KEYS = 128
TOPK = 16
TILES = 9
LOWEST = -3.0e38
MASKED = -1.0e30
GT = 66
GTILES = TOK // GT
GG = 3
RING = 4

KE = 2
BLOCKS = KEYS // KE
ROUTE_U = 3
GATE_U = 3
EARLY_RETRIEVE, EARLY_ROUTE = 2, ROUTE_U * TILES + 1
EARLY_GATES = GATE_U * GTILES + 2
EARLY = EARLY_RETRIEVE + EARLY_ROUTE + EARLY_GATES


def credit(engine, sem, n):
    engine.sem_inc(sem, n)


def tokens_of(tile):
    return P if tile < TILES - 1 else SAMPLE


class Sems:

    def __init__(self, nc, phase):
        self.nc, self.phase = nc, phase

    def __call__(self, name):
        return self.nc.alloc_semaphore(f"{self.phase}_{name}")


@contextmanager
def phase(nc, name):
    with nc.cleanup_on_exit(), ExitStack() as ctx:
        def sb(n, shape, dt=F32):
            return ctx.enter_context(nc.sbuf_tensor(f"{name}_{n}", shape, dt))

        def ps(n, shape, dt=F32):
            return ctx.enter_context(nc.psum_tensor(f"{name}_{n}", shape, dt))

        yield sb, ps, Sems(nc, name), nc.Block()


def project(nc, out, w_hi, w_lo, x_hi, x_lo, n, between=()):
    tok = slice(n * NB, (n + 1) * NB)
    at = [(2 * a + 1) * DC // (2 * len(between)) for a in range(len(between))]
    for k in range(DC):
        if k in at:
            between[at.index(k)]()
        nc.tensor.matmul(out, w_hi[:, k, :], x_hi[:, k, tok], start=(k == 0), stop=False)
        nc.tensor.matmul(out, w_hi[:, k, :], x_lo[:, k, tok], start=False, stop=False)
        last = nc.tensor.matmul(out, w_lo[:, k, :], x_hi[:, k, tok], start=False, stop=(k == DC - 1))
    return last


def norm_phase(nc, name, src, weight, consts, hi=None, lo=None, src_dram=None, out=None, out_dram=None):
    PARTS, CP = 4, DC // 4
    with phase(nc, name) as (sb, ps, sem, blk):
        squares = sb("squares", [P, 2, TOK])
        sum_sq = sb("sum_sq", [P, TOK])
        rstd = sb("rstd", [P, 1, TILES])
        scaled = sb("scaled", [P, 4, TOK])
        total = ps("total", [P, 1, TILES])
        spread_out = ps("spread", [P, NBN, 512])
        split = hi is not None
        squared, summed, totalled, scaled_ready = sem("squared"), sem("summed"), sem("totalled"), sem("scaled")
        rstd_step, spread_ready = sem("rstd_step"), sem("spread_ready")
        if src_dram is not None:
            landed = [sem(f"landed{a}") for a in range(PARTS)]
        if split:
            hi_ready, lo_ready = sem("hi"), [sem("lo_pool"), sem("lo_dve")]
        else:
            stored = sem("stored")
        with blk as block:
            @block.sync
            def _(sp):
                for a in range(PARTS if src_dram is not None else 0):
                    chunks = slice(a * CP, a * CP + CP)
                    sp.dma_start(src[:, chunks], src_dram[:, chunks]).then_inc(landed[a], 16)
                if not split:
                    for a in range(PARTS):
                        chunks = slice(a * CP, a * CP + CP)
                        sp.wait_ge(scaled_ready, a * CP + CP)
                        sp.dma_start(out_dram[:, chunks], out[:, chunks]).then_inc(stored, 16)
                    sp.wait_ge(stored, 16 * PARTS)

            @block.scalar
            def _(act):
                for k in range(DC):
                    if src_dram is not None and k % CP == 0:
                        act.wait_ge(landed[k // CP], 16)
                    if k >= 2:
                        act.wait_ge(summed, k - 1)
                    nc.scalar.activation(squares[:, k % 2, :], src[:, k, :], ACT.Square).then_inc(squared, 1)
                act.wait_ge(rstd_step, 1)
                nc.scalar.activation(rstd[:], rstd[:], ACT.Sqrt).then_inc(rstd_step, 1)
                if split:
                    for k in range(DC):
                        act.wait_ge(scaled_ready, k + 1)
                        nc.scalar.activation(hi[:, k, :], scaled[:, k % 4, :], ACT.Copy).then_inc(hi_ready, 1)

            @block.tensor
            def _(pe):
                pe.wait_ge(summed, DC)
                for t in range(TILES):
                    n = tokens_of(t)
                    last = nc.tensor.matmul(total[:n, 0, t:t + 1], sum_sq[:, t * P:t * P + n], consts["ones"][:, :1],
                                            start=True, stop=True)
                last.then_inc(totalled, 1)
                pe.wait_ge(rstd_step, 3)
                spread(nc, consts, rstd[:, 0], lambda bank: spread_out[:, bank]).then_inc(spread_ready, 1)

            def split_low(engine, k):
                engine.wait_ge(hi_ready, k + 1)
                (nc.gpsimd, nc.vector)[k % 2].tensor_tensor(lo[:, k, :], scaled[:, k % 4, :], hi[:, k, :].bitcast(F32),
                                                            ALU.subtract).then_inc(lo_ready[k % 2], 1)

            @block.gpsimd
            def _(pool):
                for k in range(0, DC if split else 0, 2):
                    split_low(pool, k)

            @block.vector
            def _(dve):
                dve.wait_ge(squared, 1)
                nc.vector.tensor_copy(sum_sq[:], squares[:, 0, :]).then_inc(summed, 1)
                for k in range(1, DC):
                    dve.wait_ge(squared, k + 1)
                    dve.wait_ge(summed, k)
                    nc.vector.tensor_tensor(sum_sq[:], sum_sq[:], squares[:, k % 2, :], ALU.add).then_inc(summed, 1)
                dve.wait_ge(totalled, 1)
                mean_square(nc, rstd, total, 1.0 / D).then_inc(rstd_step, 1)
                dve.wait_ge(rstd_step, 2)
                nc.vector.reciprocal(rstd[:], rstd[:]).then_inc(rstd_step, 1)
                dve.wait_ge(spread_ready, 1)
                for k in range(DC):
                    if split and k >= 2 and k % 2:
                        split_low(dve, k - 2)
                    if split and k >= 4:
                        dve.wait_ge(lo_ready[k % 2], k // 2 - 1)
                    to = scaled[:, k % 4, :] if split else out[:, k, :]
                    nc.vector.scalar_tensor_tensor(to.rearrange("p (n t) -> p n t", n=NBN),
                                                   src[:, k, :].rearrange("p (n t) -> p n t", n=NBN), weight[:, k:k + 1],
                                                   spread_out[:, :, :NB], ALU.mult, ALU.mult).then_inc(scaled_ready, 1)
                if split:
                    split_low(dve, DC - 1)


def mean_square(nc, rstd, total, scale):
    full, part = slice(0, TILES - 1), slice(TILES - 1, TILES)
    nc.vector.tensor_scalar(rstd[:, :, full], total[:, :, full], scale, EPS, ALU.mult, ALU.add)
    for q in range(P // SAMPLE):
        rows = slice(q * SAMPLE, q * SAMPLE + SAMPLE)
        last = nc.vector.tensor_scalar(rstd[rows, :, part], total[:SAMPLE, :, part], scale, EPS, ALU.mult, ALU.add)
    return last


def spread(nc, consts, values, bank_of):
    for t in range(TILES):
        lo, hi, n = t * P, t * P + tokens_of(t), tokens_of(t)
        cuts = [lo] + [c for c in range(NB, TOK, NB) if lo < c < hi] + [hi]
        for a, b in zip(cuts[:-1], cuts[1:]):
            last = nc.tensor.matmul(bank_of(a // NB)[:, a % NB:a % NB + b - a], values[:n, t:t + 1].to_broadcast([n, P]),
                                    consts["ident"][:n, a - lo:b - lo], start=True, stop=True)
    return last


def input_projection(nc, consts, x_hi, x_lo, dt_raw, conv_wb, conv, gate, t):
    STEPS = TAPS + 1
    with phase(nc, "inproj") as (sb, ps, sem, blk):
        w_raw = sb("w_raw", [P, 2, DC, P])
        w_hi = sb("w_hi", [P, 2, DC, P], F32R)
        w_lo = sb("w_lo", [P, 2, DC, P], F32R)
        wdt_raw = sb("wdt_raw", [P, DC, SSM_HEADS])
        wdt_hi = sb("wdt_hi", [P, DC, SSM_HEADS], F32R)
        wdt_lo = sb("wdt_lo", [P, DC, SSM_HEADS], F32R)
        dt_rows = sb("dt_rows", [SSM_HEADS, TOK])
        conv_in = sb("conv_in", [P, CONV_TILES, TAPS - 1])
        tails = sb("tails", [P, CONV_TILES, 2, TAPS - 1])
        result = sb("result", [P, 2, CONV_W])
        acc = ps("acc", [P, 2, 3, 512])
        dt_acc = ps("dt_acc", [P, TILES, SSM_HEADS])
        w_landed = [sem("w_landed0"), sem("w_landed1")]
        hi_ready, lo_ready = sem("hi_ready"), sem("lo_ready")
        projected, acc_free = sem("projected"), sem("acc_free")
        stored = [sem("stored0"), sem("stored1")]
        dt_landed, dt_split, dt_done, dt_copied, dt_turned = (
            sem("dt_landed"), sem("dt_split"), sem("dt_done"), sem("dt_copied"), sem("dt_turned"))
        past_landed, cleared, convolved, silu_done, tails_stored = (
            sem("past_landed"), sem("cleared"), sem("convolved"), sem("silu_done"), sem("tails_stored"))
        pairs, conv_pairs, own_pairs = IN_TILES // 2, CONV_TILES // 2, (CONV_TILES + Z_TILES) // 2
        with blk as block:
            @block.sync
            def _(sp):
                sp.dma_start(wdt_raw[:], t["w_dt"]).then_inc(dt_landed, 16)
                credit(sp, lo_ready, 2)

                def load(i):
                    for u in range(2):
                        sp.wait_ge(lo_ready, 2 * i + u + 1)
                        sp.dma_start(w_raw[:, u], t["w_in"][bass.ds(2 * i + u, 1)]
                                     .rearrange("a p k m -> p (a k) m")).then_inc(w_landed[u], 16)

                load(0)
                sp.dma_start(conv_in[:], t["conv_in"]).then_inc(past_landed, 16)
                with sp.Fori(1, pairs) as i:
                    load(i)
                sp.wait_ge(convolved, STEPS * (CONV_TILES + 2))
                sp.dma_start(t["conv_tails"], tails[:]).then_inc(tails_stored, 16)
                sp.wait_ge(tails_stored, 16)

            @block.gpsimd
            def _(pool):
                nc.gpsimd.memset(result[:, :, :TAPS - 1], 0.0).then_inc(cleared, 1)

            @block.scalar
            def _(act):
                act.wait_ge(dt_landed, 16)
                nc.scalar.activation(wdt_hi[:], wdt_raw[:], ACT.Copy).then_inc(dt_split, 1)
                credit(act, convolved, 2 * STEPS)
                credit(act, stored[0], 16)
                credit(act, stored[1], 16)

                def split_high(i, u):
                    act.wait_ge(w_landed[u], 16 * i + 16)
                    act.wait_ge(projected, 6 * i + 3 * u + 3)
                    nc.scalar.activation(w_hi[:, u], w_raw[:, u], ACT.Copy).then_inc(hi_ready, 1)

                def silu(i, u):
                    act.wait_ge(convolved, STEPS * (2 * i + u + 3))
                    tile = conv[:, bass.ds(2 * i + u, 1)]
                    nc.scalar.activation(tile, tile, ACT.Silu).then_inc(silu_done, 1)

                def to_window(i, u):
                    act.wait_ge(convolved, STEPS * (2 * i + u + 1))
                    for n in range(NBN):
                        act.wait_ge(projected, 6 * i + 3 * u + n + 7)
                        lo, hi = n * NB, min((n + 1) * NB, PROMPT)
                        if n == NBN - 1:
                            nc.scalar.activation(result[:, u, S_OFF + TAPS - 1:], acc[:, u, n, hi - lo:NB], ACT.Copy)
                        nc.scalar.activation(result[:, u, TAPS - 1 + lo:TAPS - 1 + hi], acc[:, u, n, :hi - lo],
                                             ACT.Copy).then_inc(acc_free, 1)

                def to_gate(i, u):
                    for n in range(NBN):
                        act.wait_ge(projected, 6 * i + 3 * u + n + 7)
                        nc.scalar.activation(gate[:, 2 * i + u - CONV_TILES, n * NB:(n + 1) * NB], acc[:, u, n, :NB],
                                             ACT.Silu).then_inc(acc_free, 1)

                def to_dram(i, u):
                    act.wait_ge(stored[u], 16 * (i - own_pairs) + 16)
                    for n in range(NBN):
                        act.wait_ge(projected, 6 * i + 3 * u + n + 7)
                        nc.scalar.activation(result[:, u, n * NB:(n + 1) * NB], acc[:, u, n, :NB],
                                             ACT.Copy).then_inc(acc_free, 1)
                    act.wait_ge(acc_free, 6 * i + 3 * u + 9)
                    act.dma_start(t["proj"][bass.ds(2 * (i - own_pairs) + u, 1)].rearrange("a p t -> (a p) t"),
                                  result[:, u, :TOK]).then_inc(stored[u], 16)

                def pair(i, take, convolve_before=False):
                    for u in range(2):
                        split_high(i + u, 1 - u)
                        if convolve_before:
                            silu(i - 1, u)
                        take(i, u)

                for n in range(NBN):
                    act.wait_ge(dt_done, n + 1)
                    nc.scalar.activation(dt_rows[:, n * NB:(n + 1) * NB], acc[:SSM_HEADS, 1, n, :NB], ACT.Copy).then_inc(dt_copied, 1)
                split_high(0, 0)
                pair(0, to_window)
                with act.Fori(1, conv_pairs) as i:
                    pair(i, to_window, convolve_before=True)
                pair(conv_pairs, to_gate, convolve_before=True)
                for i in range(conv_pairs + 1, own_pairs):
                    pair(i, to_gate)
                with act.Fori(own_pairs, pairs - 1) as i:
                    pair(i, to_dram)
                split_high(pairs - 1, 1)
                to_dram(pairs - 1, 0)
                to_dram(pairs - 1, 1)
                for u in range(2):
                    act.wait_ge(stored[u], 16 * (pairs - own_pairs) + 16)

            @block.vector
            def _(dve):
                dve.wait_ge(dt_split, 1)
                nc.vector.tensor_tensor(wdt_lo[:], wdt_raw[:], wdt_hi[:].bitcast(F32), ALU.subtract).then_inc(dt_split, 1)
                nc.vector.memset(dt_raw[:], 0.0).then_inc(dt_split, 1)

                def split_low(i, u):
                    dve.wait_ge(hi_ready, 2 * i + u + 1)
                    nc.vector.tensor_tensor(w_lo[:, u], w_raw[:, u], w_hi[:, u].bitcast(F32),
                                            ALU.subtract).then_inc(lo_ready, 1)

                def convolve(i, u):
                    tile = bass.ds(2 * i + u, 1)
                    done = STEPS * (2 * i + u + 2)
                    window, out = result[:, u], conv[:, tile].rearrange("p a t -> p (a t)")
                    wb = conv_wb[:, tile].rearrange("p a j -> p (a j)")
                    dve.wait_ge(acc_free, 6 * i + 3 * u + 9)
                    nc.vector.tensor_copy(window[:, S_OFF:S_OFF + TAPS - 1], conv_in[:, tile].rearrange("p a j -> p (a j)"))
                    for s, end in enumerate((S_OFF, CONV_W)):
                        last = nc.vector.tensor_copy(tails[:, tile, s].rearrange("p a j -> p (a j)"), window[:, end - (TAPS - 1):end])
                    last.then_inc(convolved, 1)
                    dve.wait_ge(convolved, done + 1)
                    nc.vector.tensor_scalar(out, window[:, :CONV_OUT], wb[:, 0:1], wb[:, TAPS:], ALU.mult, ALU.add).then_inc(convolved, 1)
                    for j in range(1, TAPS):
                        dve.wait_ge(convolved, done + j + 1)
                        nc.vector.scalar_tensor_tensor(out, window[:, j:j + CONV_OUT], wb[:, j:j + 1], out,
                                                       ALU.mult, ALU.add).then_inc(convolved, 1)

                split_low(0, 0)
                dve.wait_ge(dt_turned, 1)
                dve.wait_ge(dt_split, 3)
                nc.vector.tensor_copy(dt_raw[:, :TILES - 1], dt_acc[:, :TILES - 1])
                nc.vector.tensor_copy(dt_raw[:SAMPLE, TILES - 1], dt_acc[:SAMPLE, TILES - 1])
                split_low(0, 1)
                dve.wait_ge(past_landed, 16)
                dve.wait_ge(cleared, 1)
                with dve.Fori(1, conv_pairs + 1) as i:
                    for u in range(2):
                        split_low(i, u)
                        convolve(i - 1, u)
                with dve.Fori(conv_pairs + 1, pairs) as i:
                    for u in range(2):
                        split_low(i, u)

            @block.tensor
            def _(pe):
                credit(pe, acc_free, 6)
                credit(pe, projected, 6)
                pe.wait_ge(dt_split, 2)
                for n in range(NBN):
                    project(nc, acc[:SSM_HEADS, 1, n, :NB], wdt_hi, wdt_lo, x_hi, x_lo, n).then_inc(dt_done, 1)
                pe.wait_ge(dt_copied, NBN)
                for a in range(TILES):
                    n = tokens_of(a)
                    last = nc.tensor.transpose(dt_acc[:n, a, :], dt_rows[:, a * P:a * P + n], consts["ident"][:SSM_HEADS, :SSM_HEADS])
                last.then_inc(dt_turned, 1)
                with pe.Fori(0, pairs) as i:
                    for u in range(2):
                        pe.wait_ge(lo_ready, 2 * i + u + 3)
                        for n in range(NBN):
                            pe.wait_ge(acc_free, 6 * i + 3 * u + n + 1)
                            last = project(nc, acc[:, u, n, :NB], w_hi[:, u], w_lo[:, u], x_hi, x_lo, n)
                            last.then_inc(projected, 1)


def ssd_phase(nc, consts, vecs, head_vec, dt_raw, conv, gate, t, mixed, prefetch):
    ssm_norm_w, d_skip = vecs
    XT, BT, CT = 4, 2, 2
    CW = SSM_HEADS * TILES
    with phase(nc, "ssd") as (sb, ps, sem, blk):
        rstd = sb("rstd", [P, 2, TILES])
        state = sb("state", [P, 2, SSM_HEADS, HD])
        stage = sb("stage", [P, XT + BT, P])
        dta_stage = sb("dta_stage", [P, SSM_HEADS])
        dt, dta, tmp, acum, to_end, decay, dt_end = (sb(n, [P, CW]) for n in (
            "dt", "dta", "tmp", "acum", "to_end", "decay", "dt_end"))
        exp_row = sb("exp_row", [P, SSM_HEADS, P])
        segs, c_scaled_s = sb("segs", [P, 2, SSM_HEADS, P]), sb("c_scaled", [P, 2, SSM_HEADS, P])
        xdt_s = sb("xdt", [P, 2, SSM_HEADS, HD])
        x_end = sb("x_end", [P, SSM_HEADS, HD])
        b_rows = sb("b_rows", [P, BT, P])
        rows_ps = ps("rows_ps", [P, XT + BT, P])
        acum_ps = ps("acum_ps", [P, SSM_HEADS, P])
        score_ps = ps("score_ps", [P, BT, 256])
        y_ps = ps("y_ps", [P, XT, P])
        state_ps = ps("state_ps", [P, SSM_HEADS, HD])
        small_ps = ps("small_ps", [P, 2, 256])
        landed, cleared = sem("landed"), sem("cleared")
        dt_step, dt_act, dt_pe = sem("dt_step"), sem("dt_act"), sem("dt_pe")
        staged, transposed, acum_ready, scored = sem("staged"), sem("transposed"), sem("acum_ready"), sem("scored")
        exp_row_done, seg_ready, seg_exp, weighted = sem("exp_row_done"), sem("seg_ready"), sem("seg_exp"), sem("weighted")
        x_ready, c_ready, b_ready = sem("x_ready"), sem("c_ready"), sem("b_ready")
        y_done, state_done, y_out, decayed, state_new = (
            sem("y_done"), sem("state_done"), sem("y_out"), sem("decayed"), sem("state_new"))
        gated, squared, totalled, spread_ready = sem("gated"), sem("squared"), sem("totalled"), sem("spread_ready")
        rstd_step = sem("rstd_step")
        stored = sem("stored")

        def group_out(g, n):
            flat = [acum_ps[:, 0:4], acum_ps[:, 4:8], rows_ps[:, 0:4], y_ps[:], state_ps[:], score_ps[:]][3 * g + n]
            return flat.rearrange("p a b -> p (a b)")[:, :NB]

        def columns(c):
            return (bass.ds(c * P, P), P) if c is not None else (slice(S_OFF, S_OFF + SAMPLE), SAMPLE)

        with blk as block:
            @block.sync
            def _(sp):
                sp.dma_start(state[:, 1].rearrange("p h d -> p (h d)"), t["state_in"]).then_inc(landed, 16)
                prefetch(sp)
                sp.wait_ge(state_new, CHUNKS + 1)
                sp.dma_start(t["state_prompt"], state[:, 0].rearrange("p h d -> p (h d)")).then_inc(stored, 16)
                sp.wait_ge(state_new, CHUNKS + 2)
                sp.dma_start(t["state_sample"], state[:, 1].rearrange("p h d -> p (h d)")).then_inc(stored, 16)
                sp.wait_ge(stored, 32)

            @block.gpsimd
            def _(pool):
                nc.gpsimd.memset(state[:, 0], 0.0).then_inc(cleared, 1)
                pool.wait_ge(dt_step, 5)
                credit(pool, acum_ready, 1)
                credit(pool, transposed, 1)
                credit(pool, scored, 1)

                def stage_chunk(c, i):
                    cols, n = columns(c)
                    pool.wait_ge(transposed, i + 1)
                    pool.wait_ge(scored, i + 1)
                    pool.wait_ge(acum_ready, i + 1)
                    nc.gpsimd.tensor_copy(stage[:, :, :n], conv[:, :XT + BT, cols]).then_inc(staged, 1)
                    h = bass.ds(i * SSM_HEADS, SSM_HEADS)
                    nc.gpsimd.tensor_copy(dta_stage[:], dta[:, h]).then_inc(staged, 1)

                with pool.Fori(0, CHUNKS) as c:
                    stage_chunk(c, c)
                stage_chunk(None, CHUNKS)

            @block.scalar
            def _(act):
                act.preload_act_table_set("natural_log_exp_and_others")
                act.wait_ge(dt_step, 2)
                nc.scalar.activation(tmp[:], tmp[:], ACT.Exp).then_inc(dt_act, 1)
                act.wait_ge(dt_act, 1)
                nc.scalar.activation(tmp[:], tmp[:], ACT.Ln, bias=1.0).then_inc(dt_act, 1)
                nc.scalar.activation(head_vec[:, 1], head_vec[:, 1], ACT.Exp).then_inc(dt_act, 1)
                act.wait_ge(dt_step, 7)
                nc.scalar.activation(to_end[:], to_end[:], ACT.Exp).then_inc(dt_act, 1)
                nc.scalar.activation(decay[:], small_ps[:, 1, :CW], ACT.Exp).then_inc(dt_act, 1)
                credit(act, c_ready, 1)
                credit(act, y_done, 2)
                credit(act, state_done, 1)

                def chunk(c, i, par):
                    _, n = columns(c)
                    seg = segs[:, par]
                    act.wait_ge(c_ready, i + 1)
                    act.wait_ge(acum_ready, i + 2)
                    nc.scalar.activation(exp_row[:, :, :n], acum_ps[:, :, :n], ACT.Exp).then_inc(exp_row_done, 1)
                    act.wait_ge(seg_ready, i * SSM_HEADS + SSM_HEADS)
                    nc.scalar.activation(seg[:n, :, :n], seg[:n, :, :n], ACT.Exp).then_inc(seg_exp, 1)
                    act.wait_ge(transposed, i + 2)
                    act.wait_ge(state_done, i + 1)
                    nc.scalar.activation(b_rows[:n], rows_ps[:n, XT:], ACT.Copy).then_inc(b_ready, 1)

                with act.Fori(0, CHUNKS // 2) as i:
                    for par in range(2):
                        chunk(2 * i + par, 2 * i + par, par)
                chunk(None, CHUNKS, 0)
                for j in range(XT):
                    act.wait_ge(gated, j + 1)
                    nc.scalar.activation(conv[:, j, :TOK], mixed[:, j, :], ACT.Square).then_inc(squared, 1)
                act.wait_ge(rstd_step, 1)
                nc.scalar.activation(rstd[:], rstd[:], ACT.Sqrt).then_inc(rstd_step, 1)

            @block.tensor
            def _(pe):
                pe.wait_ge(dt_step, 5)
                for a, lhs in enumerate(("causal", "ones")):
                    last = nc.tensor.matmul(small_ps[:, a, :CW], consts[lhs][:], dta[:], start=True, stop=True)
                last.then_inc(dt_pe, 1)
                pe.wait_ge(cleared, 1)
                pe.wait_ge(landed, 16)
                credit(pe, exp_row_done, 1)
                credit(pe, seg_exp, 1)
                credit(pe, b_ready, 1)
                credit(pe, x_ready, 2)
                credit(pe, weighted, 2)
                credit(pe, y_out, XT)
                credit(pe, state_new, 1)

                def front(c, i):
                    _, n = columns(c)
                    pe.wait_ge(staged, 2 * i + 2)
                    pe.wait_ge(exp_row_done, i + 1)
                    pe.wait_ge(seg_exp, i + 1)
                    for h in range(SSM_HEADS):
                        last = nc.tensor.matmul(acum_ps[:, h, :n], dta_stage[:n, h:h + 1].to_broadcast([n, P]),
                                                consts["causal"][:n, :n], start=True, stop=True)
                    last.then_inc(acum_ready, 1)
                    pe.wait_ge(b_ready, i + 1)
                    pe.wait_ge(x_ready, 2 * i + 2)
                    for j in range(XT + BT):
                        last = nc.tensor.transpose(rows_ps[:n, j, :], stage[:, j, :n], consts["ident"][:])
                    last.then_inc(transposed, 1)

                def score(c, i):
                    cols, n = columns(c)
                    pe.wait_ge(weighted, 2 * i + 2)
                    for g in range(BT):
                        last = nc.tensor.matmul(score_ps[:n, g, :n], stage[:, XT + g, :n], conv[:, XT + BT + g, cols],
                                                start=True, stop=True)
                    last.then_inc(scored, 1)

                def back(c, i, par):
                    _, n = columns(c)
                    s = 0 if c is not None else 1
                    pe.wait_ge(x_ready, 2 * i + 4)
                    pe.wait_ge(b_ready, i + 2)
                    pe.wait_ge(state_new, i + 1)
                    for g in range(BT):
                        last = nc.tensor.matmul(state_ps[:, 4 * g:4 * g + 4], b_rows[:n, g], x_end[:n, 4 * g:4 * g + 4],
                                                start=True, stop=True)
                    last.then_inc(state_done, 1)
                    pe.wait_ge(weighted, 2 * i + 4)
                    pe.wait_ge(c_ready, i + 2)
                    pe.wait_ge(y_out, XT * i + XT)
                    for h in range(SSM_HEADS):
                        out = y_ps[HD * (h % 2):HD * (h % 2) + HD, h // 2, :n]
                        nc.tensor.matmul(out, xdt_s[:n, par, h], segs[:n, par, h, :n], start=True, stop=False)
                        last = nc.tensor.matmul(out, state[:, s, h], c_scaled_s[:, par, h, :n], start=False, stop=True)
                    last.then_inc(y_done, 1)

                front(0, 0)
                score(0, 0)
                with pe.Fori(0, CHUNKS // 2 - 1) as i:
                    for par in range(2):
                        c = 2 * i + par
                        front(c + 1, c + 1)
                        back(c, c, par)
                        score(c + 1, c + 1)
                front(CHUNKS - 1, CHUNKS - 1)
                back(CHUNKS - 2, CHUNKS - 2, 0)
                score(CHUNKS - 1, CHUNKS - 1)
                front(None, CHUNKS)
                back(CHUNKS - 1, CHUNKS - 1, 1)
                score(None, CHUNKS)
                back(None, CHUNKS, 0)
                pe.wait_ge(squared, XT)
                for g in range(2):
                    for c in range(TILES):
                        n = tokens_of(c)
                        for j in (2 * g, 2 * g + 1):
                            last = nc.tensor.matmul(small_ps[:n, g, c:c + 1], conv[:, j, c * P:c * P + n], consts["ones"][:, :1],
                                                    start=(j == 2 * g), stop=(j == 2 * g + 1))
                last.then_inc(totalled, 1)
                pe.wait_ge(rstd_step, 3)
                for g in range(2):
                    last = spread(nc, consts, rstd[:, g], lambda bank: group_out(g, bank))
                    last.then_inc(spread_ready, 1)

            @block.vector
            def _(dve):
                dt_bias = head_vec[:, 0:1].to_broadcast([P, TILES, SSM_HEADS])
                neg_a = head_vec[:, 1:2].to_broadcast([P, TILES, SSM_HEADS])
                flat = dt[:].rearrange("p (c h) -> p c h", h=SSM_HEADS)
                nc.vector.tensor_tensor(flat, dt_raw[:], dt_bias, ALU.add).then_inc(dt_step, 1)
                dve.wait_ge(dt_step, 1)
                nc.vector.scalar_tensor_tensor(tmp[:], dt[:], -1.0, dt[:], ALU.mult, ALU.min).then_inc(dt_step, 1)
                dve.wait_ge(dt_act, 3)
                nc.vector.scalar_tensor_tensor(dt[:], dt[:], 0.0, tmp[:], ALU.max, ALU.add).then_inc(dt_step, 1)
                dve.wait_ge(dt_step, 3)
                nc.vector.scalar_tensor_tensor(dta[:].rearrange("p (c h) -> p c h", h=SSM_HEADS), flat, -1.0, neg_a,
                                               ALU.mult, ALU.mult).then_inc(dt_step, 1)
                dve.wait_ge(dt_step, 4)
                nc.vector.memset(dta[SAMPLE:SAMPLE * 2, CW - SSM_HEADS:], 0.0)
                nc.vector.memset(dta[HD:, CW - SSM_HEADS:], 0.0).then_inc(dt_step, 1)
                dve.wait_ge(dt_pe, 1)
                nc.vector.tensor_copy(acum[:], small_ps[:, 0, :CW]).then_inc(dt_step, 1)
                dve.wait_ge(dt_step, 6)
                nc.vector.scalar_tensor_tensor(to_end[:], small_ps[:, 1, :CW], 1.0, acum[:],
                                               ALU.mult, ALU.subtract).then_inc(dt_step, 1)
                dve.wait_ge(dt_act, 5)
                nc.vector.tensor_tensor(dt_end[:], dt[:], to_end[:], ALU.mult).then_inc(dt_step, 1)
                dve.wait_ge(cleared, 1)
                dve.wait_ge(landed, 16)
                dve.wait_ge(dt_step, 8)

                def front(c, i, par):
                    cols, n = columns(c)
                    seg, c_scaled, xdt = segs[:, par], c_scaled_s[:, par], xdt_s[:, par]
                    per_head = bass.ds(i * SSM_HEADS, SSM_HEADS)
                    dve.wait_ge(exp_row_done, i + 2)
                    dve.wait_ge(y_done, i + 1)
                    for h in range(SSM_HEADS):
                        nc.vector.scalar_tensor_tensor(seg[:n, h, :n], acum_ps[:n, h, :n],
                                                       acum[:n, bass.ds(i * SSM_HEADS + h, 1)],
                                                       consts["masked"][:n, :n], ALU.subtract, ALU.add).then_inc(seg_ready, 1)
                    for g in range(BT):
                        heads = slice(4 * g, 4 * g + 4)
                        c_rows = conv[:, XT + BT + g:XT + BT + g + 1, cols].to_broadcast([P, 4, n])
                        last = nc.vector.tensor_tensor(c_scaled[:, heads, :n], exp_row[:, heads, :n], c_rows, ALU.mult)
                    last.then_inc(c_ready, 1)
                    dve.wait_ge(transposed, i + 2)
                    dve.wait_ge(state_done, i + 1)
                    x_rows = rows_ps[:n, :XT].rearrange("p j (a d) -> p (j a) d", a=2)
                    for to, by in ((xdt, dt), (x_end, dt_end)):
                        scale = by[:n, per_head].unsqueeze(2).to_broadcast([n, SSM_HEADS, HD])
                        nc.vector.tensor_tensor(to[:n], x_rows, scale, ALU.mult).then_inc(x_ready, 1)

                def weigh(c, i, par):
                    _, n = columns(c)
                    seg = segs[:, par]
                    dve.wait_ge(seg_exp, i + 2)
                    dve.wait_ge(scored, i + 2)
                    for g in range(BT):
                        heads = slice(4 * g, 4 * g + 4)
                        nc.vector.tensor_tensor(seg[:n, heads, :n], seg[:n, heads, :n],
                                                score_ps[:n, g:g + 1, :n].to_broadcast([n, 4, n]),
                                                ALU.mult).then_inc(weighted, 1)

                def back(c, i):
                    cols, n = columns(c)
                    s = 0 if c is not None else 1
                    per_head = bass.ds(i * SSM_HEADS, SSM_HEADS)
                    dve.wait_ge(y_done, i + 3)
                    scale = decay[:, per_head].unsqueeze(2).to_broadcast([P, SSM_HEADS, HD])
                    nc.vector.tensor_tensor(state[:, s], state[:, s], scale, ALU.mult).then_inc(decayed, 1)
                    for j in range(XT):
                        nc.vector.scalar_tensor_tensor(mixed[:, j, bass.ds(i * P, n)], conv[:, j, cols], d_skip[:, j:j + 1],
                                                       y_ps[:, j, :n], ALU.mult, ALU.add).then_inc(y_out, 1)
                    dve.wait_ge(decayed, i + 1)
                    nc.vector.tensor_tensor(state[:, s], state[:, s], state_ps[:], ALU.add).then_inc(state_new, 1)
                    dve.wait_ge(state_new, i + 2)

                front(0, 0, 0)
                weigh(0, 0, 0)
                with dve.Fori(0, CHUNKS // 2 - 1) as i:
                    for par in range(2):
                        c = 2 * i + par
                        front(c + 1, c + 1, 1 - par)
                        back(c, c)
                        weigh(c + 1, c + 1, 1 - par)
                front(CHUNKS - 1, CHUNKS - 1, 1)
                back(CHUNKS - 2, CHUNKS - 2)
                weigh(CHUNKS - 1, CHUNKS - 1, 1)
                front(None, CHUNKS, 0)
                back(CHUNKS - 1, CHUNKS - 1)
                weigh(None, CHUNKS, 0)
                back(None, CHUNKS)
                dve.wait_ge(y_out, XT * (TILES + 1))
                for j in range(XT):
                    nc.vector.tensor_tensor(mixed[:, j, :], mixed[:, j, :], gate[:, j, :], ALU.mult).then_inc(gated, 1)
                dve.wait_ge(gated, XT)
                dve.wait_ge(totalled, 1)
                mean_square(nc, rstd, small_ps[:, :, :TILES], 2.0 / (SSM_HEADS * HD)).then_inc(rstd_step, 1)
                dve.wait_ge(rstd_step, 2)
                nc.vector.reciprocal(rstd[:], rstd[:]).then_inc(rstd_step, 1)
                for g in range(2):
                    dve.wait_ge(spread_ready, g + 1)
                    for n in range(NBN):
                        tok = slice(n * NB, (n + 1) * NB)
                        for j in (2 * g, 2 * g + 1):
                            nc.vector.scalar_tensor_tensor(mixed[:, j, tok], mixed[:, j, tok], ssm_norm_w[:, j:j + 1], group_out(g, n),
                                                           ALU.mult, ALU.mult)


class Job:

    def __init__(self, kind, n, h=0, qb=0, j=0, b0=0):
        self.kind, self.n, self.h, self.qb, self.j, self.b0 = kind, n, h, qb, j, b0
        self.slot = n % 4
        if kind == "prompt":
            self.step = 4 * qb + 3 - j
            self.diag = self.step < 4
            self.lo = max(0, j - 4 * qb) * P
            self.hi, self.keys = QW, P
            self.t_lo = self.lo + P if self.diag else self.lo
        else:
            self.lo, self.hi = 0, 2 * SAMPLE if kind == "new" else QW
            self.keys = SAMPLE if kind == "new" else P

    @property
    def cols(self):
        return slice(self.lo, self.hi)


def attention_jobs():
    jobs = []
    for qb in range(PROMPT // QW):
        for j in range(4 * qb + 3, -1, -1):
            for h in range(2):
                jobs.append(Job("prompt", len(jobs), h, qb, j))
    jobs.append(Job("new", len(jobs)))
    jobs.append(Job("past", len(jobs), b0=8))
    jobs.append(Job("past", len(jobs), b0=0))
    return jobs


class AttentionInputs:

    def __init__(self, nc, t, ctx):
        def sb(name, shape):
            return ctx.enter_context(nc.sbuf_tensor(f"att_{name}", shape, F32))

        self.t = t
        self.q, self.k, self.v = (sb(n, [P, 2, TOK]) for n in "qkv")
        self.past_k, self.past_v = sb("past_k", [P, 2, PAST]), sb("past_v", [P, 2, PB, P])
        self.landed = [ctx.enter_context(nc.semaphore(f"att_landed{u}")) for u in range(2)]

    def load(self, sp, p, u):
        t, landed = self.t, self.landed[u]
        for to, base in ((self.q, Q_TILE), (self.k, K_TILE), (self.v, V_TILE)):
            sp.dma_start(to[:, u], t["proj"][bass.ds(p + base, 1)].rearrange("a p t -> (a p) t")).then_inc(landed, 16)
        sp.dma_start(self.past_k[:, u], t["past_k"][bass.ds(p, 1)].rearrange("a p t -> (a p) t")).then_inc(landed, 16)
        sp.dma_start(self.past_v[:, u].rearrange("p b d -> p (b d)"),
                     t["past_v"][bass.ds(p, 1)].rearrange("a p b d -> (a p) (b d)")).then_inc(landed, 16)


def attention_phase(nc, consts, t, inputs, mixed):
    jobs = attention_jobs()
    JN = len(jobs)
    SL = slice(PROMPT, TOK)
    with phase(nc, "sb") as (sb, ps, sem, blk):
        q, k, v, past_k, past_v, landed = inputs.q, inputs.k, inputs.v, inputs.past_k, inputs.past_v, inputs.landed
        q_diag = sb("q_diag", [P, 2, 2 * SAMPLE])
        v_rows = sb("v_rows", [P, TILES, P])
        e, softplus, weight = sb("e", [P, 4, QW]), sb("softplus", [P, 4, QW]), sb("weight", [P, 4, QW])
        later = sb("later", [P, 2, 2, QW])
        s_later = sb("s_later", [P, PB, 2 * SAMPLE])
        strict, strict_masked, neg_ones = sb("strict", [P, P]), sb("strict_masked", [P, P]), sb("neg_ones", [P, P])
        z = ps("z", [P, 4, QW])
        o = ps("o", [P, 2, QW])
        spare = ps("spare", [P, 2, 4, P])
        const_landed = sem("const_landed")
        cleared = sem("cleared")
        scaled, v_turned, v_copied = sem("scaled"), sem("v_turned"), sem("v_copied")
        z_ready, clipped, exp_done, log_done, sp_ready = (
            sem("z_ready"), sem("clipped"), sem("exp_done"), sem("log_done"), sem("sp_ready"))
        sums_ready, w_ready, pv_done, o_copied, dve_step, passed = (
            sem("sums_ready"), sem("w_ready"), sem("pv_done"), sem("o_copied"), sem("dve_step"), sem("passed"))

        def keys_of(job):
            return slice(0, job.keys)

        with blk as block:
            @block.sync
            def _(sp):
                for tile, src in ((strict, "strict"), (strict_masked, "strict_masked"), (neg_ones, "neg_ones")):
                    sp.dma_start(tile[:], t[src]).then_inc(const_landed, 16)

                for p in range(2, PAIRS):
                    sp.wait_ge(pv_done, 4 + JN * (p - 1))
                    inputs.load(sp, p, p % 2)

            @block.gpsimd
            def _(pool):
                nc.gpsimd.memset(q_diag[:], 0.0).then_inc(cleared, 1)

            @block.scalar
            def _(act):
                credit(act, pv_done, 4)
                act.wait_ge(cleared, 1)
                act.preload_act_table_set("natural_log_exp_and_others")

                def weights(p, job):
                    act.wait_ge(sums_ready, JN * p + job.n + 5)
                    act.wait_ge(pv_done, JN * p + job.n + 1)
                    nc.scalar.activation(weight[keys_of(job), job.slot, job.cols], z[keys_of(job), job.slot, job.cols],
                                         ACT.Exp).then_inc(w_ready, 1)

                def copy_out(p, job):
                    act.wait_ge(pv_done, JN * p + job.n + 5)
                    if job.kind == "prompt":
                        to, src = slice(job.qb * QW, job.qb * QW + QW), o[:, job.qb, :]
                    else:
                        to, src = SL, spare[:, 1, 0, :SAMPLE]
                    nc.scalar.activation(mixed[:, bass.ds(p + 4, 1), to], src.unsqueeze(1), ACT.Copy).then_inc(o_copied, 1)

                def pair(p, u):
                    act.wait_ge(landed[u], (p - u) * 40 + 80)
                    for h in range(2):
                        hp = slice(HD * h, HD * h + HD)
                        nc.scalar.activation(q_diag[hp, u, h * SAMPLE:h * SAMPLE + SAMPLE], q[hp, u, SL], ACT.Copy,
                                             scale=HD ** -0.5).then_inc(scaled, 1)
                    nc.scalar.activation(q[:, u, :PROMPT], q[:, u, :PROMPT], ACT.Copy, scale=HD ** -0.5).then_inc(scaled, 1)
                    for part, (lo, hi) in enumerate(((0, 4), (4, 8), (8, 9))):
                        act.wait_ge(v_turned, 3 * p + part + 1)
                        n = P if part < 2 else SAMPLE
                        nc.scalar.activation(v_rows[:n, lo:hi, :], spare[:n, part % 2, :hi - lo, :], ACT.Copy).then_inc(v_copied, 1)
                    for step in range(JN + 3):
                        if step < JN:
                            job = jobs[step]
                            tile = e[keys_of(job), job.slot, job.cols]
                            act.wait_ge(clipped, JN * p + job.n + 1)
                            nc.scalar.activation(tile, tile, ACT.Exp).then_inc(exp_done, 1)
                            act.wait_ge(exp_done, JN * p + job.n + 1)
                            nc.scalar.activation(tile, tile, ACT.Ln, bias=1.0).then_inc(log_done, 1)
                        if 2 <= step < JN + 2:
                            weights(p, jobs[step - 2])
                        done = jobs[step - 3] if step >= 3 else None
                        if done and (done.kind == "past" and done.b0 == 0 or done.kind == "prompt" and done.j == 0 and done.h):
                            copy_out(p, done)

                with act.Fori(0, PAIRS // 2) as i:
                    for u in range(2):
                        pair(2 * i + u, u)

            @block.tensor
            def _(pe):
                pe.wait_ge(const_landed, 48)
                credit(pe, w_ready, 4)
                credit(pe, o_copied, 3)
                credit(pe, v_copied, 3)

                def turn_v(p, u):
                    pe.wait_ge(landed[u], (p - u) * 40 + 80)
                    pe.wait_ge(pv_done, JN * p + 4)
                    pe.wait_ge(o_copied, 3 * p + 3)
                    for part, (lo, hi) in enumerate(((0, 4), (4, 8), (8, 9))):
                        if part == 2:
                            pe.wait_ge(v_copied, 3 * p + 4)
                        for b in range(lo, hi):
                            n = tokens_of(b)
                            last = nc.tensor.transpose(spare[:n, part % 2, b - lo, :], v[:, u, b * P:b * P + n], consts["ident"][:])
                        last.then_inc(v_turned, 1)

                def scores(p, u, job):
                    pe.wait_ge(w_ready, JN * p + job.n + 1)
                    if job.kind == "prompt":
                        hp = slice(HD * job.h, HD * job.h + HD)
                        last = nc.tensor.matmul(z[:, job.slot, job.cols], k[hp, u, job.j * P:job.j * P + P],
                                                q[hp, u, job.qb * QW + job.lo:job.qb * QW + QW],
                                                start=True, stop=True, skip_group_check=True)
                    else:
                        for b in range(1 if job.kind == "new" else 8):
                            rows = k[:, u, SL] if job.kind == "new" else past_k[:, u, (job.b0 + b) * P:(job.b0 + b + 1) * P]
                            last = nc.tensor.matmul(z[keys_of(job), job.slot, b * 64:b * 64 + 64], rows, q_diag[:, u],
                                                    start=True, stop=True, skip_group_check=True)
                    last.then_inc(z_ready, 1)

                def suffix_sums(p, job):
                    pe.wait_ge(sp_ready, JN * p + job.n + 1)
                    if job.kind == "new":
                        pe.sem_inc(passed, 1)
                    bank, sp_tile, kk = z[keys_of(job), job.slot, :], softplus[keys_of(job), job.slot, :], job.keys

                    def add(cols, lhs, rhs):
                        return nc.tensor.matmul(bank[:, cols], lhs, rhs, start=False, stop=True, skip_group_check=True)

                    if job.kind == "prompt" and job.diag:
                        add(slice(job.lo, job.lo + P), consts["ident"][:], strict_masked[:])
                    if job.kind == "new":
                        for h in range(2):
                            add(slice(h * SAMPLE, h * SAMPLE + SAMPLE), consts["ident"][:kk, :kk], strict_masked[:kk, :SAMPLE])
                    last = add(job.cols, consts["suffix"][:kk, :kk], sp_tile[:, job.cols])
                    if job.kind == "prompt" and job.step:
                        cols = slice(job.t_lo, QW)
                        last = add(cols, neg_ones[:], later[:, job.h, job.step % 2, cols])
                    if job.kind == "past":
                        new = softplus[:SAMPLE, jobs[JN - 3].slot, :2 * SAMPLE]
                        for b in range(8):
                            last = add(slice(b * 64, b * 64 + 64), neg_ones[:SAMPLE], new)
                        nb = min(job.b0 + 8, PB - 1) - job.b0
                        last = add(slice(0, nb * 64), neg_ones[:], s_later[:, job.b0:job.b0 + nb].rearrange("p b c -> p (b c)"))
                    last.then_inc(sums_ready, 1)

                def outputs(p, u, job):
                    pe.wait_ge(w_ready, JN * p + job.n + 5)
                    if job.kind == "prompt":
                        if job.step == 0:
                            pe.wait_ge(o_copied, 3 * p + job.qb + 1)
                        hp = slice(HD * job.h, HD * job.h + HD)
                        last = nc.tensor.matmul(o[hp, job.qb, job.cols], v_rows[:, job.j, hp], weight[:, job.slot, job.cols],
                                                start=(job.step == 0), stop=(job.j == 0), skip_group_check=True)
                    else:
                        for b in range(1 if job.kind == "new" else 8):
                            for h in range(2):
                                hp = slice(HD * h, HD * h + HD)
                                rows = v_rows[:SAMPLE, TILES - 1, hp] if job.kind == "new" else past_v[:, u, job.b0 + b, hp]
                                at = (2 * b + h) * SAMPLE
                                last = nc.tensor.matmul(spare[hp, 1, 0, :SAMPLE], rows, weight[keys_of(job), job.slot, at:at + SAMPLE],
                                                        start=(job.kind == "new"), stop=(job.kind == "past" and job.b0 == 0 and b == 7),
                                                        skip_group_check=True)
                    last.then_inc(pv_done, 1)

                def pair(p, u):
                    turn_v(p, u)
                    pe.wait_ge(scaled, 3 * p + 3)
                    for step in range(JN + 3):
                        if step < JN:
                            scores(p, u, jobs[step])
                        if 2 <= step < JN + 2:
                            suffix_sums(p, jobs[step - 2])
                        if step == 3:
                            pe.wait_ge(v_copied, 3 * p + 6)
                        if step >= 3:
                            outputs(p, u, jobs[step - 3])

                with pe.Fori(0, PAIRS // 2) as i:
                    for u in range(2):
                        pair(2 * i + u, u)

            @block.vector
            def _(dve):
                dve.wait_ge(const_landed, 48)
                credit(dve, sums_ready, 4)
                LINKS = 52

                def link(p, links, instruction):
                    links.append(instruction)
                    instruction.then_inc(dve_step, 1)
                    dve.wait_ge(dve_step, LINKS * p + len(links))

                def clip(p, job):
                    dve.wait_ge(z_ready, JN * p + job.n + 1)
                    nc.vector.tensor_scalar(e[keys_of(job), job.slot, job.cols], z[keys_of(job), job.slot, job.cols],
                                            40.0, None, ALU.min).then_inc(clipped, 1)

                def soft(p, job, links):
                    tile = softplus[keys_of(job), job.slot, :]
                    dve.wait_ge(log_done, JN * p + job.n + 1)
                    dve.wait_ge(sums_ready, JN * p + job.n + 1)
                    soft_max = nc.vector.tensor_tensor(tile[:, job.cols], z[keys_of(job), job.slot, job.cols],
                                                       e[keys_of(job), job.slot, job.cols], ALU.max)
                    if job.kind == "prompt":
                        first = slice(job.lo, job.lo + P)
                        if job.diag:
                            link(p, links, soft_max)
                            masking = nc.vector.tensor_tensor(tile[:, first], tile[:, first], strict[:], ALU.mult)
                        last = masking if job.diag else soft_max
                        if job.j:
                            link(p, links, last)
                            dve.wait_ge(sums_ready, JN * p + job.n + 3)
                            to = later[:, job.h, (job.step + 1) % 2, :]
                            if job.diag:
                                last = nc.vector.tensor_copy(to[:, first], tile[:, first])
                            if job.step:
                                cols = slice(job.t_lo, QW)
                                last = nc.vector.tensor_tensor(to[:, cols], later[:, job.h, job.step % 2, cols], tile[:, cols], ALU.add)
                    elif job.kind == "new":
                        link(p, links, soft_max)
                        halves = tile[:, :64].rearrange("p (h q) -> p h q", h=2)
                        last = nc.vector.tensor_tensor(halves, halves, strict[:SAMPLE, :SAMPLE].unsqueeze(1).to_broadcast([SAMPLE, 2, SAMPLE]), ALU.mult)
                    else:
                        link(p, links, soft_max)
                        if job.b0:
                            dve.wait_ge(sums_ready, JN * p + 4)
                            link(p, links, nc.vector.tensor_copy(s_later[:, PB - 2], tile[:, 7 * 64:8 * 64]))
                        for b in range(PB - 3 if job.b0 else 7, job.b0 - 1 if job.b0 else -1, -1):
                            nxt = jobs[JN - 2 if b + 1 >= 8 else JN - 1]
                            last = nc.vector.tensor_tensor(s_later[:, b], s_later[:, b + 1],
                                                           softplus[:, nxt.slot, (b + 1) % 8 * 64:(b + 1) % 8 * 64 + 64], ALU.add)
                            if b > job.b0:
                                link(p, links, last)
                    last.then_inc(sp_ready, 1)
                    dve.wait_ge(sp_ready, JN * p + job.n + 1)

                def pair(p):
                    links = []
                    clip(p, jobs[0])
                    for n in range(JN):
                        if n + 1 < JN:
                            clip(p, jobs[n + 1])
                        soft(p, jobs[n], links)
                    assert len(links) == LINKS, len(links)

                with dve.Fori(0, PAIRS // 2) as i:
                    for u in range(2):
                        pair(2 * i + u)


def output_projection(nc, mixed, m_hi, m_lo, w_out, x, h_dram):
    h = mixed
    with phase(nc, "outproj") as (sb, ps, sem, blk):
        w_raw = sb("w_raw", [P, DC, P])
        w_hi, w_lo = sb("w_hi", [P, 2, DC, P], F32R), sb("w_lo", [P, 2, DC, P], F32R)
        residual = sb("residual", [P, 2, TOK])
        acc = ps("acc", [P, 2, 3, 512])
        w_landed, x_landed = sem("w_landed"), [sem("x_landed0"), sem("x_landed1")]
        m_hi_ready, m_lo_ready = sem("m_hi_ready"), sem("m_lo_ready")
        hi_ready, lo_ready, projected, added, stored = (
            sem("hi_ready"), sem("lo_ready"), sem("projected"), sem("added"), sem("stored"))
        pairs = DC // 2
        with blk as block:
            @block.sync
            def _(sp):
                credit(sp, lo_ready, 1)

                def store(tile):
                    sp.dma_start(h_dram[:, tile, :].rearrange("p a t -> p (a t)"), h[:, tile, :].rearrange("p a t -> p (a t)")).then_inc(stored, 16)

                def pair(i, first=False):
                    for u in range(2):
                        sp.wait_ge(lo_ready, 2 * i + u + 1)
                        sp.dma_start(w_raw[:], w_out[bass.ds(2 * i + u, 1)].rearrange("a p k m -> p (a k) m")).then_inc(w_landed, 16)
                        sp.wait_ge(added, 6 * i + 3 * u + 3)
                        sp.dma_start(residual[:, u], x[:, bass.ds(2 * i + u, 1), :].rearrange("p a t -> p (a t)")).then_inc(x_landed[u], 16)
                        if not first:
                            store(bass.ds(2 * i + u - 2, 1))

                pair(0, first=True)
                with sp.Fori(1, pairs) as i:
                    pair(i)
                for u in range(2):
                    sp.wait_ge(added, 3 * DC + 3 * u + 3)
                    store(slice(DC - 2 + u, DC - 1 + u))
                sp.wait_ge(stored, 16 * DC)

            @block.scalar
            def _(act):
                for k in range(DC):
                    nc.scalar.activation(m_hi[:, k], mixed[:, k], ACT.Copy).then_inc(m_hi_ready, 1)
                with act.Fori(0, pairs) as i:
                    for u in range(2):
                        act.wait_ge(w_landed, 32 * i + 16 * u + 16)
                        act.wait_ge(projected, 6 * i + 3 * u + 3)
                        nc.scalar.activation(w_hi[:, u], w_raw[:], ACT.Copy).then_inc(hi_ready, 1)

            @block.vector
            def _(dve):
                credit(dve, added, 6)
                for k in range(DC):
                    dve.wait_ge(m_hi_ready, k + 1)
                    nc.vector.tensor_tensor(m_lo[:, k], mixed[:, k], m_hi[:, k].bitcast(F32), ALU.subtract).then_inc(m_lo_ready, 1)

                def split_low(i, u):
                    dve.wait_ge(hi_ready, 2 * i + u + 1)
                    nc.vector.tensor_tensor(w_lo[:, u], w_raw[:], w_hi[:, u].bitcast(F32), ALU.subtract).then_inc(lo_ready, 1)

                def add_residual(i, u):
                    dve.wait_ge(x_landed[u], 16 * i + 16)
                    for n in range(NBN):
                        tok = slice(n * NB, n * NB + NB)
                        dve.wait_ge(projected, 6 * i + 3 * u + n + 7)
                        nc.vector.tensor_tensor(h[:, bass.ds(2 * i + u, 1), tok], acc[:, u:u + 1, n, :NB], residual[:, u:u + 1, tok],
                                                ALU.add).then_inc(added, 1)

                split_low(0, 0)
                with dve.Fori(0, pairs - 1) as i:
                    split_low(i, 1)
                    add_residual(i, 0)
                    split_low(i + 1, 0)
                    add_residual(i, 1)
                split_low(pairs - 1, 1)
                add_residual(pairs - 1, 0)
                add_residual(pairs - 1, 1)

            @block.tensor
            def _(pe):
                credit(pe, projected, 6)
                pe.wait_ge(m_lo_ready, DC)
                with pe.Fori(0, pairs) as i:
                    for u in range(2):
                        pe.wait_ge(lo_ready, 2 * i + u + 2)
                        for n in range(NBN):
                            pe.wait_ge(added, 6 * i + 3 * u + n + 1)
                            project(nc, acc[:, u, n, :NB], w_hi[:, u], w_lo[:, u], m_hi, m_lo, n).then_inc(projected, 1)


def held(dve, sem, value, passed):
    dve.wait_ge(sem, value)
    dve.sem_inc(passed, 1)


def retrieval_phase(nc, t, x_hi, x_lo, w_q, keys, top_v, top_i):
    with phase(nc, "retrieve") as (sb, ps, sem, blk):
        w_raw = sb("w_raw", [P, DC, P])
        w_hi, w_lo = sb("w_hi", [P, 2, DC, P], F32R), sb("w_lo", [P, 2, DC, P], F32R)
        key_tile = sb("key_tile", [P, 2, KEYS])
        query = sb("query", [P, 2, TOK])
        scores = sb("scores", [P, 2, TILES, KEYS])
        rest = sb("rest", [P, TILES, KEYS])
        best_v, best_i = sb("best_v", [P, TILES, TOPK]), sb("best_i", [P, TILES, TOPK], U32)
        acc = ps("acc", [P, 3, 512])
        score_ps = ps("score_ps", [P, 3, 4, KEYS])
        early = EarlyHidden(nc, t, sb, ps, sem, x_hi, x_lo, 0, EARLY_RETRIEVE, acc)
        w_landed, k_landed = sem("w_landed"), [sem("k_landed0"), sem("k_landed1")]
        hi_ready, lo_ready, projected, query_ready = sem("hi_ready"), sem("lo_ready"), sem("projected"), sem("query_ready")
        scored, copied = sem("scored"), sem("copied")
        max1, place1, replaced, max2, place2, kept = (sem(n) for n in ("max1", "place1", "replaced", "max2", "place2", "kept"))
        passed, cleared = sem("passed"), sem("cleared")
        pairs = HALVES // 2
        with blk as block:
            @block.sync
            def _(sp):
                credit(sp, lo_ready, 1)
                early.sync_start(sp)

                def pair(i):
                    for u in range(2):
                        sp.wait_ge(lo_ready, 2 * i + u + 1)
                        sp.dma_start(w_raw[:], w_q[bass.ds(2 * i + u, 1)].rearrange("a p k m -> p (a k) m")).then_inc(w_landed, 16)
                        sp.wait_ge(scored, 6 * i + 3 * u + 3)
                        sp.dma_start(key_tile[:, u], keys[bass.ds(2 * i + u, 1)].rearrange("a p n -> (a p) n")).then_inc(k_landed[u], 16)

                pair(0)
                for j in range(EARLY_RETRIEVE):
                    early.load(sp, j)
                with sp.Fori(1, pairs) as i:
                    pair(i)
                for j in range(EARLY_RETRIEVE):
                    early.store(sp, j)
                early.sync_end(sp, EARLY_RETRIEVE)

            @block.gpsimd
            def _(pool):
                nc.gpsimd.memset(best_v[:, TILES - 1], 0.0).then_inc(cleared, 1)
                nc.gpsimd.memset(best_i[:, TILES - 1], 0).then_inc(cleared, 1)
                for j in range(EARLY_RETRIEVE):
                    early.split_low(pool, j, j)

            @block.scalar
            def _(act):
                credit(act, scored, 6)
                credit(act, kept, 2)

                def split_high(i, u):
                    act.wait_ge(w_landed, 32 * i + 16 * u + 16)
                    act.wait_ge(projected, 6 * i + 3 * u + 3)
                    nc.scalar.activation(w_hi[:, u], w_raw[:], ACT.Copy).then_inc(hi_ready, 1)

                def copy_query(i, u):
                    act.wait_ge(scored, 6 * i + 3 * u + 3)
                    for n in range(NBN):
                        act.wait_ge(projected, 6 * i + 3 * u + n + 7)
                        nc.scalar.activation(query[:, u, n * NB:n * NB + NB], acc[:, n, :NB], ACT.Copy).then_inc(query_ready, 1)

                def copy_scores(i, u):
                    act.wait_ge(kept, 2 * i + u + 1)
                    for b in range(3):
                        act.wait_ge(scored, 6 * i + 3 * u + b + 7)
                        rows, last = (P, 4) if b < 2 else (SAMPLE, 1)
                        nc.scalar.activation(scores[:rows, u, 4 * b:4 * b + last], score_ps[:rows, b, :last], ACT.Copy).then_inc(copied, 1)

                split_high(0, 0)
                split_high(0, 1)
                copy_query(0, 0)
                for j in range(EARLY_RETRIEVE):
                    early.split_high(act, j, j)
                with act.Fori(0, pairs - 1) as i:
                    split_high(i + 1, 0)
                    copy_query(i, 1)
                    copy_scores(i, 0)
                    split_high(i + 1, 1)
                    copy_query(i + 1, 0)
                    copy_scores(i, 1)
                copy_query(pairs - 1, 1)
                copy_scores(pairs - 1, 0)
                copy_scores(pairs - 1, 1)
                for j in range(EARLY_RETRIEVE):
                    for n in range(NBN):
                        early.activate(act, j, n)

            @block.tensor
            def _(pe):
                credit(pe, projected, 6)
                credit(pe, query_ready, 3)
                credit(pe, copied, 3)
                early.tensor_start(pe)

                def queries(i, u):
                    pe.wait_ge(lo_ready, 2 * i + u + 2)
                    for n in range(NBN):
                        pe.wait_ge(query_ready, 6 * i + 3 * u + n + 1)
                        project(nc, acc[:, n, :NB], w_hi[:, u], w_lo[:, u], x_hi, x_lo, n).then_inc(projected, 1)

                def score(i, u):
                    pe.wait_ge(query_ready, 6 * i + 3 * u + 6)
                    pe.wait_ge(k_landed[u], 16 * i + 16)
                    for b in range(3):
                        pe.wait_ge(copied, 6 * i + 3 * u + b + 1)
                        for tile in range(4 * b, min(4 * b + 4, TILES)):
                            n = tokens_of(tile)
                            last = nc.tensor.matmul(score_ps[:n, b, tile - 4 * b], query[:, u, tile * P:tile * P + n],
                                                    key_tile[:, u], start=True, stop=True)
                        last.then_inc(scored, 1)

                queries(0, 0)
                with pe.Fori(0, pairs - 1) as i:
                    queries(i, 1)
                    score(i, 0)
                    queries(i + 1, 0)
                    score(i, 1)
                queries(pairs - 1, 1)
                score(pairs - 1, 0)
                score(pairs - 1, 1)
                for j in range(EARLY_RETRIEVE):
                    for n in range(NBN):
                        early.multiply(pe, j, j, n)

            @block.vector
            def _(dve):
                dve.wait_ge(cleared, 2)

                def split_low(i, u):
                    dve.wait_ge(hi_ready, 2 * i + u + 1)
                    nc.vector.tensor_tensor(w_lo[:, u], w_raw[:], w_hi[:, u].bitcast(F32), ALU.subtract).then_inc(lo_ready, 1)

                def best(i, u):
                    at = 2 * i + u
                    rows = [(tile, tokens_of(tile)) for tile in range(TILES)]
                    first, second = slice(0, 8), slice(8, 16)
                    held(dve, copied, 6 * i + 3 * u + 6, passed)
                    held(dve, kept, at + 2, passed)
                    for tile, n in rows:
                        nc.vector.max(best_v[:n, tile, first], scores[:n, u, tile]).then_inc(max1, 1)
                    held(dve, max1, TILES * at + TILES, passed)
                    for tile, n in rows:
                        nc.vector.max_index(best_i[:n, tile, first], best_v[:n, tile, first], scores[:n, u, tile]).then_inc(place1, 1)
                    for tile, n in rows:
                        nc.vector.match_replace(rest[:n, tile], best_v[:n, tile, first], scores[:n, u, tile], LOWEST).then_inc(replaced, 1)
                    held(dve, replaced, TILES * at + TILES, passed)
                    for tile, n in rows:
                        nc.vector.max(best_v[:n, tile, second], rest[:n, tile]).then_inc(max2, 1)
                    held(dve, max2, TILES * at + TILES, passed)
                    for tile, n in rows:
                        nc.vector.max_index(best_i[:n, tile, second], best_v[:n, tile, second], rest[:n, tile]).then_inc(place2, 1)
                    dve.wait_ge(place2, TILES * at + TILES)
                    nc.vector.tensor_copy(top_v[:, :, bass.ds(at, 1), :], best_v[:].unsqueeze(2))
                    nc.vector.tensor_copy(top_i[:, :, bass.ds(at, 1), :], best_i[:].unsqueeze(2)).then_inc(kept, 1)

                split_low(0, 0)
                split_low(0, 1)
                with dve.Fori(0, pairs - 1) as i:
                    split_low(i + 1, 0)
                    best(i, 0)
                    split_low(i + 1, 1)
                    best(i, 1)
                best(pairs - 1, 0)
                best(pairs - 1, 1)


class EarlyHidden:

    def __init__(self, nc, t, sb, ps, sem, x_hi, x_lo, base, slots, acc=None):
        self.nc, self.t, self.x_hi, self.x_lo, self.base, self.slots = nc, t, x_hi, x_lo, base, slots
        self.raw = sb("u_raw", [P, DC, P])
        self.hi, self.lo = sb("u_hi", [P, slots, DC, P], F32R), sb("u_lo", [P, slots, DC, P], F32R)
        self.out = sb("hidden_out", [P, NBN, NB])
        self.acc = ps("hidden", [P, NBN, 512]) if acc is None else acc
        self.landed, self.split, self.ready = sem("u_landed"), sem("u_split"), sem("u_ready")
        self.products, self.activated = sem("u_products"), sem("u_activated")
        self.stored = [sem(f"u_stored{n}") for n in range(NBN)]

    def sync_start(self, sp):
        credit(sp, self.ready, 1)
        for n in range(NBN):
            credit(sp, self.stored[n], 16)

    def load(self, sp, j):
        sp.wait_ge(self.ready, j + 1)
        sp.dma_start(self.raw[:], self.t["peer_u"][bass.ds(j + self.base, 1)]
                     .rearrange("a p k m -> p (a k) m")).then_inc(self.landed, 16)

    def store_bank(self, sp, j, n):
        sp.wait_ge(self.activated, 3 * j + n + 4)
        sp.dma_start(self.t["hidden"][bass.ds(j + self.base, 1), :, n * NB:n * NB + NB].rearrange("a p t -> (a p) t"),
                     self.out[:, n]).then_inc(self.stored[n], 16)

    def store(self, sp, j):
        for n in range(NBN):
            self.store_bank(sp, j, n)

    def sync_end(self, sp, tiles):
        for n in range(NBN):
            sp.wait_ge(self.stored[n], 16 * tiles + 16)

    def split_high(self, act, j, slot):
        act.wait_ge(self.landed, 16 * j + 16)
        act.wait_ge(self.products, 3 * j + 3)
        self.nc.scalar.activation(self.hi[:, slot], self.raw[:], ACT.Copy).then_inc(self.split, 1)

    def activate(self, act, j, n):
        act.wait_ge(self.stored[n], 16 * j + 16)
        act.wait_ge(self.products, 3 * j + n + 3 * self.slots + 1)
        self.nc.scalar.activation(self.out[:, n], self.acc[:, n, :NB], ACT.Gelu).then_inc(self.activated, 1)

    def split_low(self, pool, j, slot):
        pool.wait_ge(self.split, j + 1)
        self.nc.gpsimd.tensor_tensor(self.lo[:, slot], self.raw[:], self.hi[:, slot].bitcast(F32),
                                     ALU.subtract).then_inc(self.ready, 1)

    def tensor_start(self, pe):
        credit(pe, self.products, 3 * self.slots)
        credit(pe, self.activated, 3)

    def multiply(self, pe, j, slot, n, between=()):
        if n == 0:
            pe.wait_ge(self.ready, j + 2)
        pe.wait_ge(self.activated, 3 * j + n + 1)
        project(self.nc, self.acc[:, n, :NB], self.hi[:, slot], self.lo[:, slot], self.x_hi, self.x_lo, n, between).then_inc(self.products, 1)


def routing_phase(nc, consts, t, x_hi, x_lo, top_v, top_i, routes):
    HK = PEER_HEADS * TOPK
    with phase(nc, "route") as (sb, ps, sem, blk):
        cand, rest = sb("cand", [P, PEER_HEADS, TOPK, TOPK]), sb("rest", [P, PEER_HEADS, TOPK * TOPK])
        best_v, best_i = sb("best_v", [P, PEER_HEADS, TOPK]), sb("best_i", [P, PEER_HEADS, TOPK], U32)
        half_i, half = sb("half_i", [P, 2, PEER_HEADS, TOPK], U32), sb("half", [P, 2, HK])
        found = sb("found", [P, 2, PEER_HEADS * TOPK, TOPK])
        rows = sb("rows", [P, 3, HK])
        shifted = sb("shifted", [P, PEER_HEADS, TOPK])
        total = sb("total", [P, PEER_HEADS])
        turned = ps("turned", [P, 2, 4, P])
        early = EarlyHidden(nc, t, sb, ps, sem, x_hi, x_lo, EARLY_RETRIEVE, ROUTE_U)
        passed, gates_split = sem("passed"), sem("gates_split")
        iota = consts["iota"]
        step, maxed, exp_done, rows_ready, transposed, copied = (
            sem("step"), sem("maxed"), sem("exp_done"), sem("rows_ready"), sem("transposed"), sem("copied"))
        with blk as block:
            @block.sync
            def _(sp):
                early.sync_start(sp)
                for j in range(ROUTE_U):
                    early.load(sp, j)
                with sp.Fori(0, TILES - 1) as i:
                    for a in range(ROUTE_U):
                        early.load(sp, ROUTE_U * i + a + ROUTE_U)
                        early.store(sp, ROUTE_U * i + a)
                early.load(sp, EARLY_ROUTE - 1)
                for a in range(ROUTE_U + 1):
                    early.store(sp, ROUTE_U * (TILES - 1) + a)
                early.sync_end(sp, EARLY_ROUTE)

            @block.scalar
            def _(act):
                def tile(i, n, at, extra=0):
                    for a in range(ROUTE_U + extra):
                        for b in range(NBN):
                            early.activate(act, ROUTE_U * i + a, b)
                        if extra == 0 or a == 0:
                            early.split_high(act, ROUTE_U * i + a + ROUTE_U, a)
                        if a == 1:
                            act.wait_ge(maxed, i + 1)
                            nc.scalar.activation(shifted[:n], shifted[:n], ACT.Exp).then_inc(exp_done, 1)
                    act.wait_ge(transposed, i + 2)
                    nc.scalar.activation(routes[:, :2, bass.ds(at, n)], turned[:, 0, :2, :n], ACT.Copy).then_inc(copied, 1)
                    nc.scalar.activation(routes[:, 2:3, bass.ds(at, n)].bitcast(F32R), turned[:, 0, 2:3, :n], ACT.Copy).then_inc(copied, 1)

                for a in range(ROUTE_U):
                    early.split_high(act, a, a)
                with act.Fori(0, TILES - 1) as i:
                    tile(i, P, i * P)
                tile(TILES - 1, SAMPLE, PROMPT, 1)

            @block.tensor
            def _(pe):
                credit(pe, gates_split, 1)
                credit(pe, transposed, 1)
                early.tensor_start(pe)

                def tile(i, n, extra=0):
                    for a in range(ROUTE_U + extra):
                        for b in range(NBN):
                            early.multiply(pe, ROUTE_U * i + a, a % ROUTE_U, b)
                    pe.wait_ge(rows_ready, i + 1)
                    pe.wait_ge(gates_split, i + 1)
                    for a in range(3):
                        last = nc.tensor.transpose(turned[:, 0, a, :n], rows[:n, a], consts["ident"][:n, :n])
                    last.then_inc(transposed, 1)

                with pe.Fori(0, TILES - 1) as i:
                    tile(i, P)
                tile(TILES - 1, SAMPLE, 1)

            @block.gpsimd
            def _(pool):
                with pool.Fori(0, TILES) as i:
                    for a in range(ROUTE_U):
                        early.split_low(pool, ROUTE_U * i + a, a)
                early.split_low(pool, EARLY_ROUTE - 1, 0)

            @block.vector
            def _(dve):
                STEPS = 12

                def split_gates(i, n, at):
                    dve.wait_ge(copied, 2 * i + 2)
                    nc.vector.tensor_tensor(routes[:, 3:4, bass.ds(at, n)], turned[:, 0, 2:3, :n], routes[:, 2:3, bass.ds(at, n)],
                                            ALU.subtract).then_inc(gates_split, 1)

                def tile(i, n, at):
                    done = [0]

                    def link(instruction):
                        instruction.then_inc(step, 1)
                        done[0] += 1
                        held(dve, step, i * STEPS + done[0], passed)

                    halves = top_v[:n, bass.ds(i, 1)].rearrange("p a (h s) k -> p (a h) s k", s=2)
                    places = top_i[:n, bass.ds(i, 1)].rearrange("p a (h s) k -> p (a h) s k", s=2)
                    shape = [n, PEER_HEADS, TOPK, TOPK]
                    link(nc.vector.tensor_tensor(cand[:n], halves[:, :, 0].unsqueeze(3).to_broadcast(shape),
                                                 halves[:, :, 1].unsqueeze(2).to_broadcast(shape), ALU.add))
                    sums = cand[:n].rearrange("p h i j -> p h (i j)")
                    for h in range(PEER_HEADS):
                        last = nc.vector.max(best_v[:n, h, :8], sums[:, h])
                    link(last)
                    for h in range(PEER_HEADS):
                        nc.vector.max_index(best_i[:n, h, :8], best_v[:n, h, :8], sums[:, h])
                    for h in range(PEER_HEADS):
                        last = nc.vector.match_replace(rest[:n, h], best_v[:n, h, :8], sums[:, h], LOWEST)
                    link(last)
                    for h in range(PEER_HEADS):
                        last = nc.vector.max(best_v[:n, h, 8:], rest[:n, h])
                    link(last)
                    nc.vector.tensor_tensor(shifted[:n], best_v[:n], best_v[:n, :, :1].to_broadcast([n, PEER_HEADS, TOPK]),
                                            ALU.subtract).then_inc(maxed, 1)
                    for h in range(PEER_HEADS):
                        last = nc.vector.max_index(best_i[:n, h, 8:], best_v[:n, h, 8:], rest[:n, h])
                    link(last)
                    nc.vector.tensor_scalar(half_i[:n, 0], best_i[:n], 4, None, ALU.logical_shift_right)
                    link(nc.vector.tensor_scalar(half_i[:n, 1], best_i[:n], TOPK - 1, None, ALU.bitwise_and))
                    link(nc.vector.tensor_copy(half[:n], half_i[:n].rearrange("p a h k -> p a (h k)")))
                    wide = [n, HK, TOPK]
                    for s in range(2):
                        last = nc.vector.tensor_tensor(found[:n, s], half[:n, s].unsqueeze(2).to_broadcast(wide),
                                                       iota[:n, :TOPK].unsqueeze(1).to_broadcast(wide), ALU.is_equal)
                    link(last)
                    for s in range(2):
                        by_head = found[:n, s].rearrange("p (h k) i -> p h k i", h=PEER_HEADS)
                        last = nc.vector.tensor_tensor(by_head, by_head, places[:, :, s].unsqueeze(2).to_broadcast(shape), ALU.mult)
                    link(last)
                    dve.wait_ge(transposed, i + 1)
                    nc.vector.tensor_reduce(rows[:n, 0:2], found[:n], AX.X, ALU.add)
                    dve.wait_ge(exp_done, i + 1)
                    link(nc.vector.tensor_reduce(total[:n], shifted[:n], AX.X, ALU.add))
                    link(nc.vector.reciprocal(total[:n], total[:n]))
                    gate = rows[:n, 2].rearrange("p (h k) -> p h k", h=PEER_HEADS)
                    link(nc.vector.tensor_tensor(gate, shifted[:n], total[:n].unsqueeze(2).to_broadcast([n, PEER_HEADS, TOPK]), ALU.mult))
                    dve.sem_inc(rows_ready, 1)
                    assert done[0] == STEPS

                tile(0, P, 0)
                with dve.Fori(1, TILES - 1) as i:
                    tile(i, P, i * P)
                    split_gates(i - 1, P, i * P - P)
                tile(TILES - 1, SAMPLE, PROMPT)
                split_gates(TILES - 2, P, PROMPT - P)
                split_gates(TILES - 1, SAMPLE, PROMPT)


def gate_phase(nc, consts, t, x_hi, x_lo, routes, spare):
    with phase(nc, "gates") as (sb, ps, sem, blk):
        early = EarlyHidden(nc, t, sb, ps, sem, x_hi, x_lo, EARLY_RETRIEVE + EARLY_ROUTE, 2)
        row_hot, col_hot = sb("row_hot", [P, RING, GG, P], F32R), sb("col_hot", [P, RING, GG, P])
        gated = sb("gated", [P, RING, GG, 2, P], F32R)
        tile_bufs = [spare[:].rearrange("p k t -> p (k t)").rearrange("p (c l) -> p c l", l=GT), sb("tile_buf", [P, KEYS, GT])[:]]
        product = ps("product", [P, 2, 4, 2 * P])
        lower, lower_ready = sb("lower", [P, 2, GG, P]), sem("lower_ready")
        stored = [sem("stored0"), sem("stored1")]
        cols_ready, hi_ready, lo_ready = sem("cols_ready"), sem("hi_ready"), sem("lo_ready")
        multiplied, copied = sem("multiplied"), sem("copied")
        iota = consts["iota"]
        groups = GT // GG
        slots = NBN * GATE_U
        PARTS = NBN * (GATE_U - 1)
        beside = [range(groups * c // slots, groups * (c + 1) // slots) for c in range(slots)]
        wide = [P, GG, P]

        def of_group(a, g):
            return routes[:, a, bass.ds(g * GG, GG)].unsqueeze(2).to_broadcast(wide)

        def over_tiles(engine, tile):
            with engine.Fori(0, GTILES // 2) as i:
                for u in range(2):
                    tile(2 * i + u, u, i, 2 * groups * i + u * groups, 2 * GATE_U * i + u * GATE_U)

        with blk as block:
            @block.sync
            def _(sp):
                credit(sp, stored[0], 16 * PARTS)
                credit(sp, stored[1], 16 * PARTS)
                early.sync_start(sp)

                def store_part(at, u, c):
                    cols = slice(KEYS * c // PARTS, KEYS * (c + 1) // PARTS)
                    sp.dma_start(t["gates"][:, bass.ds(at, 1), cols].rearrange("p a c l -> p (a c l)"),
                                 tile_bufs[u][:, cols].rearrange("p c l -> p (c l)")).then_inc(stored[u], 16)

                def tile(at, u, first=False):
                    j = at * GATE_U
                    for a in range(GATE_U):
                        early.load(sp, j + a + 2)
                        if a == 0 and not first:
                            sp.wait_ge(copied, at * groups + 2)
                        for n in range(NBN):
                            early.store_bank(sp, j + a, n)
                            if not first and a < GATE_U - 1:
                                store_part(at - 1, 1 - u, NBN * a + n)

                for j in range(2):
                    early.load(sp, j)
                tile(0, 0, first=True)
                with sp.Fori(0, GTILES // 2 - 1) as i:
                    tile(2 * i + 1, 1)
                    tile(2 * i + 2, 0)
                tile(GTILES - 1, 1)
                sp.wait_ge(copied, GTILES * groups + 2)
                for c in range(PARTS):
                    store_part(GTILES - 1, 1, c)
                early.store(sp, EARLY_GATES - 2)
                early.store(sp, EARLY_GATES - 1)
                for u in range(2):
                    sp.wait_ge(stored[u], 16 * PARTS * (GTILES // 2 + 1))
                early.sync_end(sp, EARLY_GATES)

            @block.vector
            def _(dve):
                credit(dve, multiplied, RING)
                credit(dve, cols_ready, RING)
                credit(dve, lo_ready, RING)

                def group(g, s):
                    dve.wait_ge(lo_ready, g + 1)
                    dve.wait_ge(hi_ready, g + 1)
                    dve.wait_ge(multiplied, g + 1)
                    every = iota[:].unsqueeze(1).to_broadcast(wide)
                    nc.vector.tensor_tensor(col_hot[:, s], every, of_group(1, g),
                                            ALU.is_equal).then_inc(cols_ready, 1)
                    last = nc.vector.tensor_tensor(row_hot[:, s], every, of_group(0, g), ALU.is_equal)
                    if s % 2:
                        dve.wait_ge(cols_ready, g + RING + 1)
                        last = nc.vector.tensor_tensor(gated[:, s, :, 1], col_hot[:, s], of_group(3, g), ALU.mult)
                    last.then_inc(lo_ready, 1)

                def pair(i, last=False):
                    for m in range(2 * groups):
                        u, k = m // groups, m % groups
                        if k == 0:
                            dve.wait_ge(stored[u], 16 * PARTS * (i + 1))
                        g = 2 * groups * i + m
                        dve.wait_ge(lower_ready, g + 1)
                        to = tile_bufs[u][:, :, k * GG:k * GG + GG].rearrange("p c l -> p l c")
                        nc.vector.tensor_tensor(to, product[:, m % 2, :GG, :P], lower[:, m % 2], ALU.add).then_inc(copied, 1)
                        if not (last and m >= 2 * groups - RING):
                            group(g + RING, m % RING)

                for s in range(RING):
                    group(s, s)
                with dve.Fori(0, GTILES // 2 - 1) as i:
                    pair(i)
                pair(GTILES // 2 - 1, last=True)

            @block.gpsimd
            def _(pool):
                credit(pool, hi_ready, RING)

                def group(g, s):
                    pool.wait_ge(cols_ready, g + RING + 1)
                    pool.wait_ge(multiplied, g + 1)
                    if s % 2:
                        last = nc.gpsimd.tensor_tensor(gated[:, s, :, 0], col_hot[:, s], of_group(2, g), ALU.mult)
                    else:
                        both = [P, GG, 2, P]
                        last = nc.gpsimd.tensor_tensor(gated[:, s], col_hot[:, s].unsqueeze(2).to_broadcast(both),
                                                       routes[:, 2:4, bass.ds(g * GG, GG)].rearrange("p a l -> p l a")
                                                       .unsqueeze(3).to_broadcast(both), ALU.mult)
                    last.then_inc(hi_ready, 1)

                def tile(u, first, j):
                    for c in range(slots):
                        for g in beside[c]:
                            group(first + g, (u * groups + g) % RING)
                        if c % NBN == 0:
                            early.split_low(pool, j + c // NBN + 1, (u * GATE_U + c // NBN + 1) % 2)

                early.split_low(pool, 0, 0)
                with pool.Fori(0, GTILES // 2) as i:
                    for u in range(2):
                        tile(u, 2 * groups * i + u * groups, 2 * GATE_U * i + u * GATE_U)
                early.split_low(pool, EARLY_GATES - 1, 1)

            @block.tensor
            def _(pe):
                credit(pe, copied, 2)
                early.tensor_start(pe)

                def group(g, s, half):
                    pe.wait_ge(lo_ready, g + RING + 1)
                    pe.wait_ge(hi_ready, g + RING + 1)
                    pe.wait_ge(copied, g + 1)
                    for a in range(GG):
                        last = nc.tensor.matmul(product[:, half, a], row_hot[:, s, a],
                                                gated[:, s, a].rearrange("p a c -> p (a c)"), start=True, stop=True)
                    last.then_inc(multiplied, 1)

                def tile(at, u, i, first, j):
                    for c in range(slots):
                        early.multiply(pe, j + c // NBN, (u * GATE_U + c // NBN) % 2, c % NBN,
                                       [partial(group, first + k, (u * groups + k) % RING, k % 2) for k in beside[c]])

                over_tiles(pe, tile)
                for j in (EARLY_GATES - 2, EARLY_GATES - 1):
                    for n in range(NBN):
                        early.multiply(pe, j, j % 2, n)

            @block.scalar
            def _(act):
                act.preload_act_table_set("gelu_and_others")

                def tile(at, u, i, first, j):
                    for c in range(slots):
                        for k in beside[c]:
                            act.wait_ge(multiplied, first + k + RING + 1)
                            act.wait_ge(copied, first + k + 1)
                            nc.scalar.activation(lower[:, k % 2], product[:, k % 2, :GG, P:], ACT.Copy).then_inc(lower_ready, 1)
                        early.activate(act, j + c // NBN, c % NBN)
                        if c % NBN == NBN - 1:
                            early.split_high(act, j + c // NBN + 2, (u * GATE_U + c // NBN) % 2)

                early.split_high(act, 0, 0)
                early.split_high(act, 1, 1)
                over_tiles(act, tile)
                for j in (EARLY_GATES - 2, EARLY_GATES - 1):
                    for n in range(NBN):
                        early.activate(act, j, n)


def experts_phase(nc, t, x_hi, x_lo, acc):
    DT, CH = D // P, 4
    with phase(nc, "experts") as (sb, ps, sem, blk):
        u_raw, v_raw = sb("u_raw", [P, DC, P]), sb("v_raw", [P, D])
        u_hi, u_lo = sb("u_hi", [P, KE, DC, P], F32R), sb("u_lo", [P, KE, DC, P], F32R)
        v_hi, v_lo = sb("v_hi", [P, 2, KE, D], F32R), sb("v_lo", [P, 2, KE, D], F32R)
        gate = sb("gate", [P, KE, TOK])
        coef = sb("coef", [P, KE, TOK])
        c_hi, c_lo = sb("c_hi", [P, 2, KE, TOK], F32R), sb("c_lo", [P, 2, KE, TOK], F32R)
        hidden = ps("hidden", [P, 3, 512])
        mixed = ps("mixed", [P, CH, 512])
        h_landed = sem("h_landed")
        u_landed, v_landed, g_landed = sem("u_landed"), sem("v_landed"), [sem("g_landed0"), sem("g_landed1")]
        u_split, u_ready, v_split, v_ready = sem("u_split"), sem("u_ready"), sem("v_split"), sem("v_ready")
        hidden_ready, activated, gated, c_split, c_ready = (
            sem("hidden_ready"), sem("activated"), sem("gated"), sem("c_split"), sem("c_ready"))
        mixed_ready, added = sem("mixed_ready"), sem("added")

        early_landed = [sem("early_landed0"), sem("early_landed1")]
        made_blocks = BLOCKS - EARLY // KE
        assert EARLY % KE == 0 and EARLY // KE >= made_blocks and (BLOCKS - 2 * made_blocks) % 2 == 0
        LOAD, MAKE = "load", "make"

        def over_blocks(engine, step):
            step(0, 0, LOAD, 0, 0, False)
            step(1, 1, MAKE, EARLY, 0, True)
            with engine.Fori(1, made_blocks) as i:
                step(2 * i, 0, LOAD, KE * i, KE * i, True)
                step(2 * i + 1, 1, MAKE, KE * i + EARLY, KE * i, True)
            with engine.Fori(made_blocks, BLOCKS // 2) as i:
                for par in range(2):
                    step(2 * i + par, par, LOAD, KE * (2 * i + par - made_blocks), None, True)
            step(BLOCKS, 0, None, None, None, True)

        with blk as block:
            @block.sync
            def _(sp):
                credit(sp, u_ready, 1)
                credit(sp, v_ready, 1)
                credit(sp, gated, 2)

                def load_u(made):
                    sp.wait_ge(u_ready, made + 1)
                    sp.dma_start(u_raw[:], t["peer_u"][bass.ds(made + EARLY, 1)].rearrange("a p k m -> p (a k) m")).then_inc(u_landed, 16)

                def step(b, par, how, tile, made, has_v):
                    if not how:
                        return
                    for a in range(KE):
                        at = KE * b + a
                        sp.wait_ge(gated, at + 1)
                        sp.dma_start(gate[:, a].rearrange("p (n l) -> p n l", n=GTILES),
                                     t["gates"][:, :, bass.ds(tile + a, 1), :].rearrange("p n a l -> p n (a l)")).then_inc(g_landed[a], 16)
                        if how == LOAD:
                            sp.wait_ge(c_ready, at + 1)
                            sp.dma_start(coef[:, a], t["hidden"][bass.ds(tile + a, 1)].rearrange("a p t -> (a p) t")).then_inc(early_landed[a], 16)
                            if made is not None:
                                load_u(made + a)
                        sp.wait_ge(v_ready, at + 1)
                        sp.dma_start(v_raw[:], t["peer_v"][bass.ds(tile + a, 1)].rearrange("a p d -> (a p) d")).then_inc(v_landed, 16)
                    if not has_v:
                        sp.dma_start(acc[:], t["h"]).then_inc(h_landed, 16)

                over_blocks(sp, step)

            @block.scalar
            def _(act):
                def split_u(made, a):
                    act.wait_ge(u_landed, 16 * made + 16)
                    act.wait_ge(hidden_ready, 3 * made + 3)
                    nc.scalar.activation(u_hi[:, a], u_raw[:], ACT.Copy).then_inc(u_split, 1)

                def step(b, par, how, tile, made, has_v):
                    if not how:
                        return
                    for a in range(KE):
                        at = KE * b + a
                        if how == MAKE:
                            act.wait_ge(c_ready, at + 1)
                            for n in range(NBN):
                                act.wait_ge(hidden_ready, 3 * (made + a) + n + 7)
                                nc.scalar.activation(coef[:, a, n * NB:n * NB + NB], hidden[:, n, :NB], ACT.Gelu).then_inc(activated, 1)
                        elif made is not None:
                            split_u(made + a, a)
                        act.wait_ge(v_landed, 16 * at + 16)
                        act.wait_ge(mixed_ready, 24 * b + 24)
                        nc.scalar.activation(v_hi[:, par, a], v_raw[:], ACT.Copy).then_inc(v_split, 1)
                        act.wait_ge(gated, at + 3)
                        nc.scalar.activation(c_hi[:, par, a], coef[:, a], ACT.Copy).then_inc(c_split, 1)

                act.preload_act_table_set("gelu_and_others")
                credit(act, mixed_ready, 48)
                over_blocks(act, step)

            @block.tensor
            def _(pe):
                def step(b, par, how, tile, made, has_v):
                    for a in range(KE if how == MAKE else 0):
                        pe.wait_ge(u_ready, made + a + 2)
                        for n in range(NBN):
                            pe.wait_ge(activated, 3 * (made + a) + n + 1)
                            project(nc, hidden[:, n, :NB], u_hi[:, a], u_lo[:, a], x_hi, x_lo, n).then_inc(hidden_ready, 1)
                    if not has_v:
                        return
                    old = 1 - par
                    pe.wait_ge(v_ready, KE * b + 1)
                    pe.wait_ge(c_ready, KE * b + 2)
                    for d in range(DT):
                        cols = slice(d * P, d * P + P)
                        for n in range(NBN):
                            at = NBN * d + n
                            tok = slice(n * NB, n * NB + NB)
                            pe.wait_ge(added, 24 * b + at - 23)
                            out = mixed[:, at % CH, :NB]
                            for a in range(KE):
                                nc.tensor.matmul(out, v_hi[:, old, a, cols], c_hi[:, old, a, tok], start=(a == 0), stop=False)
                                nc.tensor.matmul(out, v_lo[:, old, a, cols], c_hi[:, old, a, tok], start=False, stop=False)
                                last = nc.tensor.matmul(out, v_hi[:, old, a, cols], c_lo[:, old, a, tok], start=False, stop=(a == KE - 1))
                            last.then_inc(mixed_ready, 1)

                credit(pe, hidden_ready, 6)
                credit(pe, activated, 3)
                credit(pe, added, CH)
                over_blocks(pe, step)

            @block.gpsimd
            def _(pool):
                def split_v(tile, par, a):
                    pool.wait_ge(v_split, tile + 1)
                    nc.gpsimd.tensor_tensor(v_lo[:, par, a], v_raw[:], v_hi[:, par, a].bitcast(F32), ALU.subtract).then_inc(v_ready, 1)

                def coefficients(b, a, how, tile, made):
                    pool.wait_ge(g_landed[a], 16 * b + 16)
                    if how == LOAD:
                        pool.wait_ge(early_landed[a], tile * (16 // KE) + 16)
                    else:
                        pool.wait_ge(activated, 3 * (made + a) + 6)
                    nc.gpsimd.tensor_tensor(coef[:, a], coef[:, a], gate[:, a], ALU.mult).then_inc(gated, 1)

                def step(b, par, how, tile, made, has_v):
                    for a in range(KE if how else 0):
                        coefficients(b, a, how, tile, made)
                        split_v(KE * b + a, par, a)

                over_blocks(pool, step)

            @block.vector
            def _(dve):
                def split_u(made, a):
                    dve.wait_ge(u_split, made + 1)
                    nc.vector.tensor_tensor(u_lo[:, a], u_raw[:], u_hi[:, a].bitcast(F32), ALU.subtract).then_inc(u_ready, 1)

                def split_c(tile, par, a):
                    dve.wait_ge(c_split, tile + 1)
                    nc.vector.tensor_tensor(c_lo[:, par, a], coef[:, a], c_hi[:, par, a].bitcast(F32), ALU.subtract).then_inc(c_ready, 1)

                def add(b, lo, hi):
                    for at in range(lo, hi):
                        d, tok = at // NBN, slice(at % NBN * NB, at % NBN * NB + NB)
                        dve.wait_ge(mixed_ready, 24 * b + at + 25)
                        nc.vector.tensor_tensor(acc[:, d, tok], acc[:, d, tok], mixed[:, at % CH, :NB], ALU.add).then_inc(added, 1)

                def step(b, par, how, tile, made, has_v):
                    splits_u = how == LOAD and made is not None
                    for a in range(KE):
                        if splits_u:
                            split_u(made + a, a)
                            if has_v:
                                add(b, 8 * a, 8 * a + 4)
                        if how:
                            split_c(KE * b + a, par, a)
                        if has_v:
                            add(b, 8 * a + (4 if splits_u else 0), 8 * a + 8)
                    if has_v:
                        add(b, 8 * KE, 24)
                    else:
                        dve.wait_ge(h_landed, 16)

                credit(dve, c_ready, 2)
                over_blocks(dve, step)


def build(nc, t):
    with ExitStack() as ctx:
        def sb(n, shape, dt=F32):
            return ctx.enter_context(nc.sbuf_tensor(n, shape, dt))

        ones, ident, iota = sb("ones", [P, P]), sb("ident", [P, P]), sb("iota", [P, P])
        vectors = sb("vectors", [P, 4 * DC + CONV_TILES * (TAPS + 1)])
        norm1_w, norm2_w, final_w = (vectors[:, DC * a:DC * (a + 1)] for a in range(3))
        ssm_norm_w, d_skip = vectors[:, 3 * DC:3 * DC + 4], vectors[:, 3 * DC + 4:4 * DC]
        conv_wb = vectors[:, 4 * DC:].rearrange("p (c a) -> p c a", a=TAPS + 1)
        mixed = sb("mixed", [P, DC, TOK])
        mixers = ctx.enter_context(ExitStack())
        causal, masked, suffix = (mixers.enter_context(nc.sbuf_tensor(n, [P, P], F32)) for n in ("causal", "masked", "suffix"))
        head_vec = mixers.enter_context(nc.sbuf_tensor("head_vec", [P, 2, SSM_HEADS], F32))
        dt_raw = mixers.enter_context(nc.sbuf_tensor("dt_raw", [P, TILES, SSM_HEADS], F32))
        consts = {"ones": ones, "ident": ident, "causal": causal, "masked": masked, "suffix": suffix, "iota": iota}
        const_landed = ctx.enter_context(nc.semaphore("const_landed"))
        with nc.Block() as block:
            @block.sync
            def _(sp):
                for tile, src in ((ones, "ones"), (ident, "ident"), (causal, "causal"), (masked, "masked"),
                                  (suffix, "suffix"), (iota, "iota"), (vectors, "vectors"), (head_vec, "head_vec")):
                    sp.dma_start(tile[:], t[src]).then_inc(const_landed, 16)
                sp.wait_ge(const_landed, 16 * 8)

        with ExitStack() as inner:
            conv = inner.enter_context(nc.sbuf_tensor("conv", [P, CONV_TILES, CONV_OUT], F32))
            gate = inner.enter_context(nc.sbuf_tensor("gate", [P, Z_TILES, TOK], F32))
            with ExitStack() as early:
                x_hi = early.enter_context(nc.sbuf_tensor("x1_hi", [P, DC, TOK], F32R))
                x_lo = early.enter_context(nc.sbuf_tensor("x1_lo", [P, DC, TOK], F32R))
                norm_phase(nc, "norm1", mixed, norm1_w, consts, hi=x_hi, lo=x_lo, src_dram=t["x"])
                input_projection(nc, consts, x_hi, x_lo, dt_raw, conv_wb, conv, gate, t)
            inputs = AttentionInputs(nc, t, inner)

            def prefetch(sp):
                for u in range(2):
                    inputs.load(sp, u, u)

            ssd_phase(nc, consts, (ssm_norm_w, d_skip), head_vec, dt_raw, conv, gate, t, mixed, prefetch)
            attention_phase(nc, consts, t, inputs, mixed)
        mixers.close()
        with ExitStack() as late:
            n_hi = late.enter_context(nc.sbuf_tensor("n_hi", [P, DC, TOK], F32R))
            n_lo = late.enter_context(nc.sbuf_tensor("n_lo", [P, DC, TOK], F32R))
            output_projection(nc, mixed, n_hi, n_lo, t["w_out"], t["x"], t["h"])
            norm_phase(nc, "norm2", mixed, norm2_w, consts, hi=n_hi, lo=n_lo)
            with ExitStack() as routing:
                routes = routing.enter_context(nc.sbuf_tensor("routes", [P, 4, TOK], F32))
                with ExitStack() as tops:
                    top_v = tops.enter_context(nc.sbuf_tensor("top_v", [P, TILES, HALVES, TOPK], F32))
                    top_i = tops.enter_context(nc.sbuf_tensor("top_i", [P, TILES, HALVES, TOPK], F32))
                    retrieval_phase(nc, t, n_hi, n_lo, t["w_q"], t["keys"], top_v, top_i)
                    routing_phase(nc, consts, t, n_hi, n_lo, top_v, top_i, routes)
                gate_phase(nc, consts, t, n_hi, n_lo, routes, mixed)
            experts_phase(nc, t, n_hi, n_lo, mixed)
            with nc.sbuf_tensor("y", [P, DC, TOK], F32) as y:
                norm_phase(nc, "norm3", mixed, final_w, consts, out=y, out_dram=t["y"])


_OUT = {
    "proj": [QKV_TILES, P, TOK], "conv_tails": [P, CONV_TILES, 2, TAPS - 1], "y": [P, DC, TOK], "state_prompt": [P, SSM_HEADS * HD],
    "state_sample": [P, SSM_HEADS * HD],
}
_SCRATCH = {"h": [P, DC, TOK], "gates": [P, GTILES, KEYS, GT],
            "hidden": [EARLY, P, TOK]}


def chunked(w, cols):
    n = w.shape[1] // cols
    return np.ascontiguousarray(w.reshape(DC, P, n, cols).transpose(2, 1, 0, 3))


def per_partition(v):
    return v.reshape(-1, P).T


def lay_out(x_prompt, x_sample, cache_sb_k, cache_sb_v, state_ssm, state_conv,
            norm1_w, w_in, conv_w, conv_b, dt_bias, a_log, d_skip, ssm_norm_w, w_out,
            norm2_w, peer_wq, peer_k1, peer_k2, peer_u, peer_v, final_norm_w):
    x = np.concatenate([x_prompt[0], x_sample[0]], 0)
    w = w_in[0]
    conv = np.concatenate([conv_w[0], conv_b[0][None]], 0)
    k_idx, q_idx = np.arange(P)[:, None], np.arange(P)[None]
    vectors = np.concatenate([
        per_partition(norm1_w[0]), per_partition(norm2_w[0]), per_partition(final_norm_w),
        per_partition(ssm_norm_w[0]), per_partition(np.repeat(d_skip[0], HD)),
        conv.reshape(TAPS + 1, CONV_TILES, P).transpose(2, 1, 0).reshape(P, -1)], 1)
    a = {
        "x": x.T.reshape(DC, P, TOK).transpose(1, 0, 2),
        "w_in": chunked(np.concatenate([w[:, 512:1536], w[:, :512], w[:, 1544:]], 1), P),
        "w_dt": w[:, 1536:1544].reshape(DC, P, SSM_HEADS).transpose(1, 0, 2),
        "vectors": vectors,
        "head_vec": np.broadcast_to(np.stack([dt_bias[0], a_log[0]])[None], (P, 2, SSM_HEADS)),
        "conv_in": state_conv[0, 0].T.reshape(CONV_TILES, P, TAPS - 1).transpose(1, 0, 2),
        "state_in": state_ssm[0, 0].transpose(2, 0, 1).reshape(P, SSM_HEADS * HD),
        "past_k": cache_sb_k[0, 0].reshape(PAST, PAIRS, 2 * HD).transpose(1, 2, 0),
        "past_v": cache_sb_v[0, 0].reshape(PB, P, PAIRS, 2 * HD).transpose(2, 1, 0, 3),
        "w_out": chunked(w_out[0], P),
        "w_q": chunked(peer_wq[0], P),
        "keys": np.stack([peer_k1[0], peer_k2[0]], 1).reshape(HALVES, KEYS, P).transpose(0, 2, 1),
        "peer_u": peer_u[0].reshape(KEYS, KEYS, DC, P).transpose(1, 3, 2, 0),
        "peer_v": peer_v[0].reshape(KEYS, KEYS, D).transpose(1, 0, 2),
        "ones": np.ones((P, P), np.float32),
        "ident": np.eye(P, dtype=np.float32),
        "causal": (k_idx <= q_idx).astype(np.float32),
        "masked": np.where(k_idx <= q_idx, 0.0, MASKED).astype(np.float32),
        "strict": (k_idx < q_idx).astype(np.float32),
        "strict_masked": np.where(k_idx < q_idx, 0.0, MASKED).astype(np.float32),
        "neg_ones": -np.ones((P, P), np.float32),
        "suffix": -(k_idx >= q_idx).astype(np.float32),
        "iota": np.broadcast_to(np.arange(P, dtype=np.float32)[None], (P, P)),
    }
    return {n: np.ascontiguousarray(v) for n, v in a.items()}


def give_back(r):
    proj = r["proj"]

    def rows(tile, lo, hi):
        return proj[tile:tile + 4, :, lo:hi].transpose(2, 0, 1).reshape(1, 1, hi - lo, 8, HD)

    def conv_state(s):
        return r["conv_tails"][:, :, s].transpose(2, 1, 0).reshape(1, 1, TAPS - 1, D)

    def state(s):
        return s.reshape(P, SSM_HEADS, HD).transpose(1, 2, 0)[None, None]

    y = r["y"].transpose(2, 1, 0).reshape(TOK, D)
    out = (y[None, :PROMPT], y[None, PROMPT:], rows(K_TILE, 0, PROMPT), rows(V_TILE, 0, PROMPT),
           state(r["state_prompt"]), conv_state(0), rows(K_TILE, PROMPT, TOK), rows(V_TILE, PROMPT, TOK),
           state(r["state_sample"]), conv_state(1))
    return tuple(np.ascontiguousarray(o) for o in out)


def kernel(**inputs):
    import concourse.bacc as bacc
    from concourse.bass_utils import run_bass_kernel_spmd

    nc = bacc.Bacc("TRN2", target_bir_lowering=False, num_devices=1)
    arrays = lay_out(**{n: np.asarray(v) for n, v in inputs.items()})
    t = {n: nc.dram_tensor(f"in_{n}", a.shape, F32, kind="ExternalInput").ap() for n, a in arrays.items()}
    for n, shape in _OUT.items():
        t[n] = nc.dram_tensor(f"out_{n}", shape, F32, kind="ExternalOutput").ap()
    for n, shape in _SCRATCH.items():
        t[n] = nc.dram_tensor(f"scratch_{n}", shape, F32, kind="Internal").ap()
    build(nc, t)
    r = run_bass_kernel_spmd(nc, [{f"in_{n}": a for n, a in arrays.items()}], core_ids=[0])
    return give_back({n: r.results[0][f"out_{n}"] for n in _OUT})
```
